# Optimizing a Trainium2 kernel written in Bass

```python
import math
import jax, jax.numpy as jnp
from jax import lax
import numpy as np

D_MODEL = 1024
BATCH = 1
SEQ = 512
DEPTH = 2
DEC_BATCH = 8
DEC_SEQ = 8
PAST_LEN = 1024
PAGE_SIZE = 128

HEAD_DIM = 64
POOL_WINDOWS = (2, 4, 8, 16)
POOL_GROUP = D_MODEL // 16
POOL_WIDTH = POOL_GROUP * len(POOL_WINDOWS)
POOL_BUF = max(POOL_WINDOWS) - 1
ATT_WIDTH = 3 * D_MODEL // 8
ATT_HEADS = ATT_WIDTH // HEAD_DIM
DILATED_GROUPS = ((128, 1), (512, 4), (2048, 16))
ATT_BUF = max(w for w, _ in DILATED_GROUPS)
ROPE_DIM = HEAD_DIM // 4
ROPE_THETA = 500000.0
NEG_INF = -1e30
RWKV_WIDTH = 3 * D_MODEL // 8
RWKV_HEADS = RWKV_WIDTH // HEAD_DIM
DECAY_LORA = 64
ICLR_LORA = 64
GATE_LORA = 128
RWKV_PROJ = 3 * RWKV_WIDTH + DECAY_LORA + ICLR_LORA + GATE_LORA
GN_EPS = HEAD_DIM * 1e-5
MIX_WIDTH = POOL_WIDTH + ATT_WIDTH + RWKV_WIDTH
IN_WIDTH = POOL_WIDTH + 3 * ATT_WIDTH + RWKV_PROJ
N_KEYS = 128
N_EXPERTS = N_KEYS * N_KEYS
PEER_HEADS = 8
PEER_TOPK = 16
PEER_QDIM = 256
PEER_BLOCK = 128
RMS_EPS = 1e-6

kernel_name = "hybrid_pool_dilattn_rwkv7_peer_step"

def rms_norm(x, g):
    xf = x.astype(jnp.float32)
    y = xf * lax.rsqrt(jnp.mean(xf * xf, axis=-1, keepdims=True) + RMS_EPS)
    return (y * g.astype(jnp.float32)).astype(x.dtype)

def rope(x, pos):
    half = ROPE_DIM // 2
    inv = ROPE_THETA ** (-jnp.arange(half, dtype=jnp.float32) * 2.0 / ROPE_DIM)
    ang = pos.astype(jnp.float32)[:, None] * inv[None, :]
    cos = jnp.cos(ang)[None, :, None, :]
    sin = jnp.sin(ang)[None, :, None, :]
    xr = x[..., :ROPE_DIM].astype(jnp.float32)
    x1, x2 = xr[..., :half], xr[..., half:]
    rot = jnp.concatenate([x1 * cos - x2 * sin, x2 * cos + x1 * sin], axis=-1).astype(x.dtype)
    return jnp.concatenate([rot, x[..., ROPE_DIM:]], axis=-1)

def pool_mixer(x_new, buf, pos0, w, scale):
    B, L, _ = x_new.shape
    G = len(POOL_WINDOWS)
    xfull = jnp.concatenate([buf.astype(x_new.dtype), x_new], axis=1)
    xg = xfull.astype(jnp.float32).reshape(B, POOL_BUF + L, G, POOL_GROUP)
    csum = jnp.concatenate([jnp.zeros((B, 1, G, POOL_GROUP), jnp.float32), jnp.cumsum(xg, axis=1)], axis=1)
    win = jnp.array(POOL_WINDOWS, jnp.int32)
    t = jnp.arange(L, dtype=jnp.int32)
    hi = t + POOL_BUF + 1
    lo = hi[:, None] - win[None, :]
    gi = jnp.arange(G)[None, :]
    sums = csum[:, hi] - csum[:, lo, gi]
    cnt = jnp.minimum(win[None, :], pos0 + t[:, None] + 1).astype(jnp.float32)
    diff = sums / cnt[None, :, :, None] - xg[:, POOL_BUF:]
    y = jnp.einsum('blgc,gcd->blgd', diff, w.astype(jnp.float32)).reshape(B, L, POOL_WIDTH)
    y = y * scale.astype(jnp.float32)
    return y.astype(x_new.dtype), xfull[:, -POOL_BUF:].astype(buf.dtype)

def _combine_branches(outs, lses):
    wts = jax.nn.softmax(jnp.stack(lses, 0), axis=0)
    return jnp.sum(wts[..., None] * jnp.stack(outs, 0), axis=0)

def dilated_attn_prompt(q, k, v):
    B, S, H, Dh = q.shape
    scale = HEAD_DIM ** -0.5
    outs, lses = [], []
    for window, dil in DILATED_GROUPS:
        nb = window // dil
        blk = nb
        span = dil * blk
        s_pad = -(-S // span) * span
        M = s_pad // dil
        nblk = M // blk

        def to_res(a):
            a = jnp.pad(a, ((0, 0), (0, s_pad - S), (0, 0), (0, 0)))
            a = a.reshape(B, M, dil, H, Dh).transpose(0, 2, 1, 3, 4)
            return a.reshape(B, dil, nblk, blk, H, Dh)

        def with_prev(a):
            prev = jnp.pad(a, ((0, 0), (0, 0), (1, 0), (0, 0), (0, 0), (0, 0)))[:, :, :-1]
            return jnp.concatenate([prev, a], axis=3)

        qr = to_res(q)
        kb = with_prev(to_res(k))
        vb = with_prev(to_res(v))
        s = jnp.einsum('brnqhd,brnkhd->brnhqk', qr, kb, preferred_element_type=jnp.float32) * scale
        iq = jnp.arange(blk)[:, None]
        ik = jnp.arange(2 * blk)[None, :]
        rel = blk + iq - ik
        mk = jnp.arange(nblk)[:, None, None] * blk + ik[None] - blk
        valid = (rel >= 0)[None] & (rel <= nb)[None] & (mk >= 0)
        s = jnp.where(valid[None, None, :, None], s, NEG_INF)
        m = jnp.max(s, axis=-1, keepdims=True)
        p = jnp.exp(s - m)
        den = jnp.sum(p, axis=-1, keepdims=True)
        o = jnp.einsum('brnhqk,brnkhd->brnqhd', p / den, vb.astype(jnp.float32))
        lse = (m + jnp.log(den))[..., 0]
        o = o.reshape(B, dil, M, H, Dh).transpose(0, 2, 1, 3, 4).reshape(B, s_pad, H, Dh)[:, :S]
        lse = lse.transpose(0, 1, 2, 4, 3).reshape(B, dil, M, H).transpose(0, 2, 1, 3).reshape(B, s_pad, H)[:, :S]
        outs.append(o)
        lses.append(lse)
    return _combine_branches(outs, lses).astype(q.dtype)

def dilated_attn_sample(q, k_all, v_all, n_past):
    B, T, H, Dh = q.shape
    scale = HEAD_DIM ** -0.5
    outs, lses = [], []
    for window, dil in DILATED_GROUPS:
        nb = window // dil
        idx = n_past + jnp.arange(T)[:, None] - dil * jnp.arange(nb + 1)[None, :]
        valid = idx >= 0
        idc = jnp.maximum(idx, 0)
        kg = k_all[:, idc]
        vg = v_all[:, idc]
        s = jnp.einsum('bthd,btkhd->bthk', q, kg, preferred_element_type=jnp.float32) * scale
        s = jnp.where(valid[None, :, None, :], s, NEG_INF)
        m = jnp.max(s, axis=-1, keepdims=True)
        p = jnp.exp(s - m)
        den = jnp.sum(p, axis=-1, keepdims=True)
        o = jnp.einsum('bthk,btkhd->bthd', p / den, vg.astype(jnp.float32))
        outs.append(o)
        lses.append((m + jnp.log(den))[..., 0])
    return _combine_branches(outs, lses).astype(q.dtype)

def rwkv_mixer(p, prev, wkv0, mu, w0, w_up, a0, a_up, g_up, k_k, k_a, r_k, ln_w, ln_b):
    B, L, _ = p.shape
    f32 = jnp.float32
    pf = p.astype(f32)
    p_prev = jnp.concatenate([prev.astype(f32)[:, None, :], pf[:, :-1]], axis=1)
    ps = pf + (p_prev - pf) * mu.astype(f32)
    c1, c2, c3 = RWKV_WIDTH, 2 * RWKV_WIDTH, 3 * RWKV_WIDTH
    c4 = c3 + DECAY_LORA
    c5 = c4 + ICLR_LORA
    r, k, v = ps[..., :c1], ps[..., c1:c2], ps[..., c2:c3]
    wd, ad, gd = ps[..., c3:c4], ps[..., c4:c5], ps[..., c5:]
    w_log = -jax.nn.softplus(-(w0.astype(f32) + jnp.tanh(wd) @ w_up.astype(f32))) - 0.5
    decay = jnp.exp(-jnp.exp(w_log))
    a = jax.nn.sigmoid(a0.astype(f32) + ad @ a_up.astype(f32))
    g = jax.nn.sigmoid(gd) @ g_up.astype(f32)
    hd = lambda t: t.reshape(B, L, RWKV_HEADS, HEAD_DIM)
    kk = hd(k * k_k.astype(f32))
    kk = kk / jnp.maximum(jnp.sqrt(jnp.sum(kk * kk, axis=-1, keepdims=True)), 1e-12)
    k = k * (1.0 + (a - 1.0) * k_a.astype(f32))
    r_h, k_h, v_h, w_h, a_h = hd(r), hd(k), hd(v), hd(decay), hd(a)

    def step(S, inp):
        r_t, w_t, k_t, v_t, kk_t, a_t = inp
        sa = jnp.einsum('bhij,bhj->bhi', S, -kk_t)
        S = (S * w_t[:, :, None, :] + sa[..., None] * (kk_t * a_t)[:, :, None, :]
             + v_t[..., None] * k_t[:, :, None, :])
        return S, jnp.einsum('bhij,bhj->bhi', S, r_t)

    xs = tuple(jnp.moveaxis(t, 1, 0) for t in (r_h, w_h, k_h, v_h, kk, a_h))
    S_T, o = lax.scan(step, wkv0.astype(f32), xs)
    o = jnp.moveaxis(o, 0, 1)
    mean = jnp.mean(o, axis=-1, keepdims=True)
    var = jnp.mean(jnp.square(o - mean), axis=-1, keepdims=True)
    o = ((o - mean) * lax.rsqrt(var + GN_EPS)).reshape(B, L, RWKV_WIDTH)
    o = o * ln_w.astype(f32) + ln_b.astype(f32)
    bonus = jnp.sum(r_h * k_h * r_k.astype(f32), axis=-1, keepdims=True) * v_h
    o = (o + bonus.reshape(B, L, RWKV_WIDTH)) * g
    return o.astype(p.dtype), p[:, -1].astype(prev.dtype), S_T.astype(wkv0.dtype)

def peer_ffn(x, wq, subkeys, u, v):
    B, L, D = x.shape
    T = B * L
    xt = x.reshape(T, D)
    q = (xt @ wq).reshape(T, PEER_HEADS, 2, PEER_QDIM // 2)
    sc = jnp.einsum('thcd,hcnd->thcn', q, subkeys, preferred_element_type=jnp.float32)
    s_half, i_half = lax.top_k(sc, PEER_TOPK)
    cand = (s_half[:, :, 0, :, None] + s_half[:, :, 1, None, :]).reshape(T, PEER_HEADS, PEER_TOPK * PEER_TOPK)
    cidx = (i_half[:, :, 0, :, None] * N_KEYS + i_half[:, :, 1, None, :]).reshape(T, PEER_HEADS, PEER_TOPK * PEER_TOPK)
    s_top, j = lax.top_k(cand, PEER_TOPK)
    eidx = jnp.take_along_axis(cidx, j, axis=-1)
    gate = jax.nn.softmax(s_top, axis=-1)
    pad = (-T) % PEER_BLOCK
    nblk = (T + pad) // PEER_BLOCK
    xb = jnp.pad(xt, ((0, pad), (0, 0))).reshape(nblk, PEER_BLOCK, D)
    eb = jnp.pad(eidx, ((0, pad), (0, 0), (0, 0))).reshape(nblk, PEER_BLOCK, PEER_HEADS, PEER_TOPK)
    gb = jnp.pad(gate, ((0, pad), (0, 0), (0, 0))).reshape(nblk, PEER_BLOCK, PEER_HEADS, PEER_TOPK)

    def expert_block(args):
        xs, es, gs = args
        h = jax.nn.gelu(jnp.einsum('td,thkd->thk', xs, u[es], preferred_element_type=jnp.float32), approximate=False)
        return jnp.einsum('thk,thkd->td', gs * h, v[es].astype(jnp.float32)).astype(x.dtype)

    out = lax.map(expert_block, (xb, eb, gb))
    return out.reshape(nblk * PEER_BLOCK, D)[:T].reshape(B, L, D)

def trunk_layer(h, lp, pos0, pool_buf, k_buf, v_buf, shift_prev, wkv0):
    B, L, _ = h.shape
    xn = rms_norm(h, lp['norm1_g'])
    proj = xn @ lp['w_in']
    o1 = POOL_WIDTH
    o2 = o1 + ATT_WIDTH
    o3 = o2 + ATT_WIDTH
    o4 = o3 + ATT_WIDTH
    heads = lambda t: t.reshape(B, L, ATT_HEADS, HEAD_DIM)
    pos = pos0 + jnp.arange(L, dtype=jnp.int32)
    q = rope(heads(proj[..., o1:o2]), pos)
    k = rope(heads(proj[..., o2:o3]), pos)
    v = heads(proj[..., o3:o4])
    pool_out, pool_new = pool_mixer(proj[..., :o1], pool_buf, pos0, lp['pool_w'], lp['pool_scale'])
    if k_buf is None:
        att = dilated_attn_prompt(q, k, v)
        keep = min(ATT_BUF, L)
        k_new, v_new = k[:, -keep:], v[:, -keep:]
    else:
        n_past = k_buf.shape[1]
        k_all = jnp.concatenate([k_buf.astype(k.dtype), k], axis=1)
        v_all = jnp.concatenate([v_buf.astype(v.dtype), v], axis=1)
        att = dilated_attn_sample(q, k_all, v_all, n_past)
        k_new, v_new = k_all[:, -n_past:], v_all[:, -n_past:]
    rw_out, shift_new, wkv_new = rwkv_mixer(
        proj[..., o4:], shift_prev, wkv0, lp['rwkv_mu'], lp['rwkv_w0'], lp['rwkv_w_up'], lp['rwkv_a0'],
        lp['rwkv_a_up'], lp['rwkv_g_up'], lp['rwkv_k_k'], lp['rwkv_k_a'], lp['rwkv_r_k'],
        lp['rwkv_ln_w'], lp['rwkv_ln_b'])
    mixed = jnp.concatenate([pool_out, att.reshape(B, L, ATT_WIDTH), rw_out], axis=-1)
    h = h + mixed @ lp['w_out']
    h = h + peer_ffn(rms_norm(h, lp['norm2_g']), lp['peer_wq'], lp['peer_subkeys'], lp['peer_u'], lp['peer_v'])
    return h, pool_new, k_new, v_new, shift_new, wkv_new

def setup_inputs(seed: int = 0) -> dict:
    key = jax.random.key(seed)
    ks = iter(jax.random.split(key, 40))
    nrm = lambda shape, s: jax.random.normal(next(ks), shape, jnp.float32) * s
    uni = lambda shape, lo, hi: jax.random.uniform(next(ks), shape, jnp.float32, lo, hi)
    n_att = min(ATT_BUF, PAST_LEN)
    return {
        'x_prompt': nrm((BATCH, SEQ, D_MODEL), 1.0),
        'x_sample': nrm((DEC_BATCH, DEC_SEQ, D_MODEL), 1.0),
        'state_pool': nrm((DEPTH, DEC_BATCH, POOL_BUF, POOL_WIDTH), 1.0),
        'cache_k': nrm((DEPTH, DEC_BATCH, n_att, ATT_HEADS, HEAD_DIM), 1.0),
        'cache_v': nrm((DEPTH, DEC_BATCH, n_att, ATT_HEADS, HEAD_DIM), 1.0),
        'state_shift': nrm((DEPTH, DEC_BATCH, RWKV_PROJ), 1.0),
        'state_wkv': nrm((DEPTH, DEC_BATCH, RWKV_HEADS, HEAD_DIM, HEAD_DIM), 0.1),
        'norm1_g': 1.0 + nrm((DEPTH, D_MODEL), 0.02),
        'norm2_g': 1.0 + nrm((DEPTH, D_MODEL), 0.02),
        'final_g': 1.0 + nrm((D_MODEL,), 0.02),
        'w_in': nrm((DEPTH, D_MODEL, IN_WIDTH), D_MODEL ** -0.5),
        'w_out': nrm((DEPTH, MIX_WIDTH, D_MODEL), MIX_WIDTH ** -0.5),
        'pool_w': nrm((DEPTH, len(POOL_WINDOWS), POOL_GROUP, POOL_GROUP), POOL_GROUP ** -0.5),
        'pool_scale': 1.0 + nrm((DEPTH, POOL_WIDTH), 0.1),
        'rwkv_mu': uni((DEPTH, RWKV_PROJ), 0.0, 1.0),
        'rwkv_w0': uni((DEPTH, RWKV_WIDTH), -6.0, -1.0),
        'rwkv_w_up': nrm((DEPTH, DECAY_LORA, RWKV_WIDTH), 0.1),
        'rwkv_a0': nrm((DEPTH, RWKV_WIDTH), 0.1),
        'rwkv_a_up': nrm((DEPTH, ICLR_LORA, RWKV_WIDTH), ICLR_LORA ** -0.5),
        'rwkv_g_up': nrm((DEPTH, GATE_LORA, RWKV_WIDTH), GATE_LORA ** -0.5),
        'rwkv_k_k': 0.85 + nrm((DEPTH, RWKV_WIDTH), 0.02),
        'rwkv_k_a': 1.0 + nrm((DEPTH, RWKV_WIDTH), 0.02),
        'rwkv_r_k': nrm((DEPTH, RWKV_HEADS, HEAD_DIM), 0.1),
        'rwkv_ln_w': 1.0 + nrm((DEPTH, RWKV_WIDTH), 0.02),
        'rwkv_ln_b': nrm((DEPTH, RWKV_WIDTH), 0.02),
        'peer_wq': nrm((DEPTH, D_MODEL, PEER_HEADS * PEER_QDIM), D_MODEL ** -0.5),
        'peer_subkeys': nrm((DEPTH, PEER_HEADS, 2, N_KEYS, PEER_QDIM // 2), (PEER_QDIM // 2) ** -0.5),
        'peer_u': nrm((DEPTH, N_EXPERTS, D_MODEL), D_MODEL ** -0.5),
        'peer_v': nrm((DEPTH, N_EXPERTS, D_MODEL), (PEER_HEADS * PEER_TOPK) ** -0.5),
    }

def reference(x_prompt, x_sample, state_pool, cache_k, cache_v, state_shift, state_wkv,
              norm1_g, norm2_g, final_g, w_in, w_out, pool_w, pool_scale,
              rwkv_mu, rwkv_w0, rwkv_w_up, rwkv_a0, rwkv_a_up, rwkv_g_up, rwkv_k_k, rwkv_k_a,
              rwkv_r_k, rwkv_ln_w, rwkv_ln_b, peer_wq, peer_subkeys, peer_u, peer_v):
    bp = x_prompt.shape[0]
    hp, hs = x_prompt, x_sample
    pp, pk, pv, psh, pw = [], [], [], [], []
    sp, sk, sv, ssh, sw = [], [], [], [], []
    for l in range(DEPTH):
        lp = {
            'norm1_g': norm1_g[l], 'norm2_g': norm2_g[l], 'w_in': w_in[l], 'w_out': w_out[l],
            'pool_w': pool_w[l], 'pool_scale': pool_scale[l],
            'rwkv_mu': rwkv_mu[l], 'rwkv_w0': rwkv_w0[l], 'rwkv_w_up': rwkv_w_up[l],
            'rwkv_a0': rwkv_a0[l], 'rwkv_a_up': rwkv_a_up[l], 'rwkv_g_up': rwkv_g_up[l],
            'rwkv_k_k': rwkv_k_k[l], 'rwkv_k_a': rwkv_k_a[l], 'rwkv_r_k': rwkv_r_k[l],
            'rwkv_ln_w': rwkv_ln_w[l], 'rwkv_ln_b': rwkv_ln_b[l],
            'peer_wq': peer_wq[l], 'peer_subkeys': peer_subkeys[l], 'peer_u': peer_u[l], 'peer_v': peer_v[l],
        }
        hp, a0_, a1_, a2_, a3_, a4_ = trunk_layer(
            hp, lp, 0,
            jnp.zeros((bp, POOL_BUF, POOL_WIDTH), x_prompt.dtype), None, None,
            jnp.zeros((bp, RWKV_PROJ), x_prompt.dtype),
            jnp.zeros((bp, RWKV_HEADS, HEAD_DIM, HEAD_DIM), x_prompt.dtype))
        pp.append(a0_); pk.append(a1_); pv.append(a2_); psh.append(a3_); pw.append(a4_)
        hs, b0_, b1_, b2_, b3_, b4_ = trunk_layer(
            hs, lp, PAST_LEN, state_pool[l], cache_k[l], cache_v[l], state_shift[l], state_wkv[l])
        sp.append(b0_); sk.append(b1_); sv.append(b2_); ssh.append(b3_); sw.append(b4_)
    y_prompt = rms_norm(hp, final_g)
    y_sample = rms_norm(hs, final_g)
    return (y_prompt, y_sample,
            jnp.stack(pp), jnp.stack(pk), jnp.stack(pv), jnp.stack(psh), jnp.stack(pw),
            jnp.stack(sp), jnp.stack(sk), jnp.stack(sv), jnp.stack(ssh), jnp.stack(sw))


_drawn_inputs = setup_inputs


def setup_inputs(seed=0):
    import zlib

    import numpy as np

    out = dict(_drawn_inputs(seed))
    spreads = {}
    factors = {'norm2_g': 6.794,
     'final_g': 2.852,
     'rwkv_k_k': 2.746,
     'rwkv_ln_w': 6.188,
     'rwkv_ln_b': 6.043}
    for name, (base, spread) in spreads.items():
        noise = np.random.default_rng([zlib.crc32(name.encode()), seed]).standard_normal(out[name].shape)
        drawn = base * np.exp(spread * noise) if base else spread * noise
        out[name] = __import__('jax').numpy.asarray(drawn.astype(out[name].dtype))
    for name, factor in factors.items():
        out[name] = (out[name] * factor).astype(out[name].dtype)
    return out
```

```python
from contextlib import ExitStack, contextmanager
from collections import namedtuple

import numpy as np
import concourse.bass as bass
from concourse import mybir

F32 = mybir.dt.float32
U32 = mybir.dt.uint32
ALU = mybir.AluOpType
ACT = mybir.ActivationFunctionType
X = mybir.AxisListType.X

P = 128
LAYERS = 2
D = 1024
KD = D // P
TP_, TS_ = 512, 64
T = TP_ + TS_
HALF = T // 2
NT = 5
ROWS = [P, P, P, P, TS_]
REQ, STEPS = 8, 8
PAST = 1024
HD = 64
HEADS = 6
PAIRS = HEADS // 2
RMS_EPS = 1e-6
GN_EPS = HD * 1e-5
POOL_BUF = 15
NEG = -1e30
BQ, BK, BV, BR = 2, 5, 8, 11
NB_IN = 22
NB_RW = NB_IN - BR
CH = 32
NCH = TP_ // CH
DECAY = float(np.exp(-0.5))
PH, TOPK = 8, 16
NKEY = 128
NB_Q = 16
TPAD = NT * P
EG = 4
NG = NKEY // EG
UNIT = 64
NU = T // UNIT


def _count():
    n = 0
    while True:
        yield n
        n += 1


_serial = _count()


class Parts:
    pass


def sbuf(nc, name, shape, dt):
    return nc.sbuf_tensor(f"{name}_{next(_serial)}", shape, dt)


def psum(nc, name, shape, dt):
    return nc.psum_tensor(f"{name}_{next(_serial)}", shape, dt)


class Steps:

    def __init__(self, eng, sem):
        self.eng, self.sem, self.n = eng, sem, 0

    def link(self, ins):
        ins.then_inc(self.sem, 1)
        self.n += 1
        self.eng.wait_ge(self.sem, self.n)


@contextmanager
def stage(nc, *names):
    with ExitStack() as ctx:
        sems = namedtuple("Semaphores", names)(*(ctx.enter_context(nc.semaphore(f"{n}_{next(_serial)}")) for n in names))
        with nc.Block() as block:
            yield block, sems
        with nc.Block() as tidy:
            @tidy.sync
            def _(sp):
                for sem in sems:
                    sp.sem_clear(sem)


def load_constants(nc, c):
    with stage(nc, "loaded") as (block, s):
        @block.sync
        def _(sp):
            for n, (dst, src) in enumerate(c):
                sp.dma_start(dst, src).then_inc(s.loaded, 16)
            sp.wait_ge(s.loaded, 16 * len(c))


def norm_transpose(nc, m, gain):
    with ExitStack() as ctx:
        junk = ctx.enter_context(sbuf(nc, "norm_junk", [P, D], F32))
        ssq = ctx.enter_context(sbuf(nc, "norm_ssq", [P, NT], F32))
        std = ctx.enter_context(sbuf(nc, "norm_std", [P, NT], F32))
        inv = ctx.enter_context(sbuf(nc, "norm_inv", [P, NT], F32))
        xn = ctx.enter_context(sbuf(nc, "norm_xn", [P, NT, D], F32))
        ps = ctx.enter_context(psum(nc, "norm_ps", [P, 4, 4, P], F32))
        with stage(nc, "squares", "eps_added", "rooted", "act_step", "dve_step", "scaled",
                   "turned", "stored") as (block, s):
            @block.scalar
            def _(act):
                for i, r in enumerate(ROWS):
                    ins = nc.scalar.activation(junk[0:r, :], m.h[0:r, i, :], ACT.Square,
                                               accum_out=ssq[0:r, i:i + 1])
                    ins.then_inc(s.squares, 1)
                    act.wait_ge(s.squares, i + 1)
                for i, r in enumerate(ROWS):
                    act.wait_ge(s.eps_added, i + 1)
                    nc.scalar.activation(std[0:r, i:i + 1], ssq[0:r, i:i + 1], ACT.Sqrt).then_inc(s.rooted, 1)

            @block.vector
            def _(dve):
                st = Steps(dve, s.dve_step)
                for i, r in enumerate(ROWS):
                    dve.wait_ge(s.squares, i + 1)
                    nc.vector.tensor_scalar(ssq[0:r, i:i + 1], ssq[0:r, i:i + 1], 1.0 / D, RMS_EPS,
                                            ALU.mult, ALU.add).then_inc(s.eps_added, 1)
                for i, r in enumerate(ROWS):
                    dve.wait_ge(s.rooted, i + 1)
                    st.link(nc.vector.reciprocal(inv[0:r, i:i + 1], std[0:r, i:i + 1]))
                    nc.vector.tensor_scalar(xn[0:r, i, :], m.h[0:r, i, :], inv[0:r, i:i + 1], None,
                                            ALU.mult).then_inc(s.scaled, 1)
                for n in range(2 * NT):
                    i, r, k = n // 2, ROWS[n // 2], 4 * (n % 2)
                    dve.wait_ge(s.turned, n + 1)
                    nc.vector.tensor_tensor(m.xT[:, k:k + 4, i * P:i * P + r], ps[:, n % 4, :, 0:r],
                                            gain[:, k:k + 4].unsqueeze(2).to_broadcast([P, 4, r]),
                                            ALU.mult).then_inc(s.stored, 1)

            @block.tensor
            def _(pe):
                for n in range(2 * NT):
                    i, r = n // 2, ROWS[n // 2]
                    pe.wait_ge(s.scaled, i + 1)
                    if n >= 4:
                        pe.wait_ge(s.stored, n - 3)
                    for q in range(4):
                        k = 4 * (n % 2) + q
                        ins = nc.tensor.transpose(ps[:, n % 4, q, 0:r], xn[0:r, i, k * P:(k + 1) * P],
                                                  m.ident[0:r, 0:r])
                    ins.then_inc(s.turned, 1)


def project(nc, m, w, blocks, out):
    odd = blocks % 2
    with ExitStack() as ctx:
        wb = ctx.enter_context(sbuf(nc, "proj_w", [P, 2, KD, P], F32))
        ps = ctx.enter_context(psum(nc, "proj_ps", [P, 4, 512], F32))
        with stage(nc, "even_in", "odd_in", "made", "copied_lo", "copied_hi") as (block, s):
            landed = (s.even_in, s.odd_in)

            @block.sync
            def _(sp):
                for j in range(2):
                    sp.dma_start(wb[:, j], w[j]).then_inc(landed[j], 16)
                def refill(i, j):
                    sp.wait_ge(s.made, i * 4 + (2 * j + 2))
                    sp.dma_start(wb[:, j], w[i * 2 + (2 + j)]).then_inc(landed[j], 16)

                with sp.Fori(0, blocks // 2 - 1) as i:
                    for j in range(2):
                        refill(i, j)
                if odd:
                    refill(blocks // 2 - 1, 0)

            @block.tensor
            def _(pe):
                def body(i, first, js=(0, 1)):
                    for j in js:
                        pe.wait_ge(landed[j], i * 16 + 16)
                        for half in range(2):
                            if not first:
                                pe.wait_ge((s.copied_lo, s.copied_hi)[half], i * 2 + (j - 1))
                            for k in range(KD):
                                ins = nc.tensor.matmul(ps[:, 2 * j + half, 0:HALF], wb[:, j, k, :],
                                                       m.xT[:, k, half * HALF:(half + 1) * HALF],
                                                       start=(k == 0), stop=(k == KD - 1))
                            ins.then_inc(s.made, 1)

                body(0, True)
                with pe.Fori(1, blocks // 2) as i:
                    body(i, False)
                if odd:
                    body(blocks // 2, False, (0,))

            @block.scalar
            def _(act):
                def copy(i, j):
                    act.wait_ge(s.made, i * 4 + (2 * j + 1))
                    nc.scalar.activation(out[:, bass.ds(i * 2 + j, 1), 0:HALF],
                                         ps[:, 2 * j:2 * j + 1, 0:HALF], ACT.Copy).then_inc(s.copied_lo, 1)

                with act.Fori(0, blocks // 2) as i:
                    for j in range(2):
                        copy(i, j)
                if odd:
                    copy(blocks // 2, 0)

            @block.vector
            def _(dve):
                def copy(i, j):
                    dve.wait_ge(s.made, i * 4 + (2 * j + 2))
                    nc.vector.tensor_copy(out[:, bass.ds(i * 2 + j, 1), HALF:T],
                                          ps[:, 2 * j + 1:2 * j + 2, 0:HALF]).then_inc(s.copied_hi, 1)

                with dve.Fori(0, blocks // 2) as i:
                    for j in range(2):
                        copy(i, j)
                if odd:
                    copy(blocks // 2, 0)


def rotate(nc, m):
    with ExitStack() as ctx:
        tmp = ctx.enter_context(sbuf(nc, "rope_tmp", [P, T], F32))
        ps = ctx.enter_context(psum(nc, "rope_ps", [P, 4, 512], F32))
        vps = ctx.enter_context(psum(nc, "rope_vps", [P, 2, 512], F32))
        with stage(nc, "swapped", "mixed", "dve_step", "v_turned", "v_copied", "stored") as (block, s):
            @block.tensor
            def _(pe):
                for b in range(6):
                    for half in range(2):
                        n = 2 * b + half
                        if n >= 4:
                            pe.wait_ge(s.mixed, n // 2 - 1)
                        nc.tensor.matmul(ps[:, n % 4, 0:HALF], m.rope_swap[:],
                                         m.proj[:, BQ + b, half * HALF:(half + 1) * HALF],
                                         start=True, stop=True).then_inc(s.swapped, 1)
                for i, r in enumerate(ROWS):
                    if i >= 2:
                        pe.wait_ge(s.v_copied, i - 1)
                    for c in range(PAIRS):
                        ins = nc.tensor.transpose(vps[0:r, i % 2, c * P:(c + 1) * P],
                                                  m.proj[:, BV + c, i * P:i * P + r], m.ident[:])
                    ins.then_inc(s.v_turned, 1)

            @block.vector
            def _(dve):
                st = Steps(dve, s.dve_step)
                for b in range(6):
                    dve.wait_ge(s.swapped, 2 * b + 2)
                    src = ps[:, 2 * (b % 2):2 * (b % 2) + 2, 0:HALF]
                    st.link(nc.vector.tensor_tensor(tmp[:].rearrange("p (a t) -> p a t", a=2), src,
                                                    m.rope_sin[:].rearrange("p (a t) -> p a t", a=2), ALU.mult))
                    st.link(nc.vector.tensor_tensor(m.proj[:, BQ + b, :], m.proj[:, BQ + b, :], m.rope_cos[:],
                                                    ALU.mult))
                    nc.vector.tensor_tensor(m.proj[:, BQ + b, :], m.proj[:, BQ + b, :], tmp[:],
                                            ALU.add).then_inc(s.mixed, 1)
                    dve.wait_ge(s.mixed, b + 1)

            @block.scalar
            def _(act):
                for i, r in enumerate(ROWS):
                    act.wait_ge(s.v_turned, i + 1)
                    nc.scalar.activation(m.v_tok[0:r, i, :], vps[0:r, i % 2, 0:PAIRS * P], ACT.Copy).then_inc(s.v_copied, 1)

            @block.sync
            def _(sp):
                sp.wait_ge(s.mixed, 6)
                sp.dma_start(m.dram.out_k[m.l], m.proj[:, BK:BK + PAIRS, :]).then_inc(s.stored, 16)
                sp.dma_start(m.dram.out_v[m.l], m.proj[:, BV:BV + PAIRS, :]).then_inc(s.stored, 16)
                sp.wait_ge(s.stored, 32)


def pool(nc, m):
    WP = POOL_BUF + TP_
    WS = POOL_BUF + STEPS
    with ExitStack() as ctx:
        xp = ctx.enter_context(sbuf(nc, "pool_xp", [P, 2, 1, WP], F32))
        xs = ctx.enter_context(sbuf(nc, "pool_xs", [P, 2, REQ, WS], F32))
        sp_ = ctx.enter_context(sbuf(nc, "pool_sp", [P, 2, 1, WP], F32))
        ss_ = ctx.enter_context(sbuf(nc, "pool_ss", [P, 2, REQ, WS], F32))
        tp_ = ctx.enter_context(sbuf(nc, "pool_tp", [P, 1, WP], F32))
        ts_ = ctx.enter_context(sbuf(nc, "pool_ts", [P, REQ, WS], F32))
        diff = ctx.enter_context(sbuf(nc, "pool_diff", [P, 2, T], F32))
        w = ctx.enter_context(sbuf(nc, "pool_w", [P, 2, P], F32))
        scale = ctx.enter_context(sbuf(nc, "pool_scale", [P, 2], F32))
        ps = ctx.enter_context(psum(nc, "pool_ps", [P, 4, 512], F32))
        with stage(nc, "zeroed", "loaded", "dve_step", "differed", "mapped", "filled", "scaled",
                   "stored") as (block, s):
            @block.sync
            def _(sp):
                sp.dma_start(xs[:, :, :, 0:POOL_BUF].rearrange("p a b r -> p (a b) r"),
                             m.dram.state_pool[m.l]).then_inc(s.loaded, 16)
                sp.dma_start(scale[:], m.dram.pool_scale[m.l]).then_inc(s.loaded, 16)
                sp.wait_ge(s.zeroed, 1)
                for a in range(2):
                    for o in range(2):
                        sp.dma_start(w[64 * o:64 * o + 64, a, 64 * o:64 * o + 64],
                                     m.dram.pool_w[m.l, 2 * a + o]).then_inc(s.loaded, 16)
                sp.dma_start(m.dram.p_pool[m.l], m.proj[:, 0:2, TP_ - POOL_BUF:TP_]).then_inc(s.stored, 16)
                sp.wait_ge(s.filled, 1)
                sp.dma_start(m.dram.s_pool[m.l], xs[:, :, :, STEPS:WS].rearrange("p a b r -> p (a b) r")
                             ).then_inc(s.stored, 16)
                sp.wait_ge(s.stored, 32)

            @block.vector
            def _(dve):
                st = Steps(dve, s.dve_step)
                nc.vector.memset(w[:], 0.0).then_inc(s.zeroed, 1)
                st.link(nc.vector.memset(xp[:, :, :, 0:POOL_BUF], 0.0))
                dve.wait_ge(s.loaded, 96)
                st.link(nc.vector.tensor_copy(xp[:, :, 0, POOL_BUF:WP], m.proj[:, 0:2, 0:TP_]))
                for a in range(2):
                    ins = nc.vector.tensor_copy(xs[:, a, :, POOL_BUF:WS],
                                                m.proj[:, a, TP_:T].rearrange("p (b t) -> p b t", b=REQ))
                    st.link(ins)
                nc.vector.tensor_copy(ts_[:, 0, 0:1], xs[:, 0, 0, 0:1]).then_inc(s.filled, 1)
                dve.wait_ge(s.filled, 1)
                for x, sm, tm, wd in ((xp, sp_, tp_, WP), (xs, ss_, ts_, WS)):
                    for a in range(2):
                        for o in range(2):
                            q = slice(64 * o, 64 * o + 64)
                            win = 2 << (2 * a + o)
                            st.link(nc.vector.tensor_tensor(sm[q, a, :, 1:wd], x[q, a, :, 1:wd],
                                                            x[q, a, :, 0:wd - 1], ALU.add))
                            done, src, dst = 2, sm[:, a], tm[:]
                            while done < win:
                                lo = 2 * done - 1
                                st.link(nc.vector.tensor_tensor(dst[q, :, lo:wd], src[q, :, lo:wd],
                                                                src[q, :, lo - done:wd - done], ALU.add))
                                src, dst = dst, src
                                done *= 2
                            out = (diff[q, a, 0:TP_].unsqueeze(1) if x is xp else
                                   diff[q, a, TP_:T].rearrange("p (b t) -> p b t", b=REQ))
                            cnt = (m.pool_inv[q, a, 0:TP_].unsqueeze(1) if x is xp else
                                   m.pool_inv[q, a, TP_:T].rearrange("p (b t) -> p b t", b=REQ))
                            st.link(nc.vector.tensor_tensor(out, src[q, :, POOL_BUF:wd], cnt, ALU.mult))
                nc.vector.tensor_tensor(diff[:], diff[:], m.proj[:, 0:2, :], ALU.subtract).then_inc(s.differed, 1)
                for n in range(4):
                    a, half = n // 2, n % 2
                    dve.wait_ge(s.mapped, n + 1)
                    nc.vector.tensor_scalar(m.mixed[:, a, half * HALF:(half + 1) * HALF], ps[:, n, 0:HALF],
                                            scale[:, a:a + 1], None, ALU.mult).then_inc(s.scaled, 1)

            @block.tensor
            def _(pe):
                pe.wait_ge(s.differed, 1)
                for n in range(4):
                    a, half = n // 2, n % 2
                    nc.tensor.matmul(ps[:, n, 0:HALF], w[:, a, :], diff[:, a, half * HALF:(half + 1) * HALF],
                                     start=True, stop=True).then_inc(s.mapped, 1)


def attend_prompt(nc, m):
    units = [(qt, h) for qt in range(4) for h in range(HEADS)]
    with ExitStack() as ctx:
        sm = ctx.enter_context(sbuf(nc, "att_s", [P, 2, TP_], F32))
        pr = ctx.enter_context(sbuf(nc, "att_p", [P, 2, TP_], F32))
        pt = ctx.enter_context(sbuf(nc, "att_pt", [P, 2, 4, P], F32))
        st_ = ctx.enter_context(sbuf(nc, "att_stat", [P, 2, 4], F32))
        lc = ctx.enter_context(sbuf(nc, "att_lc", [P, 4, TP_], F32))
        s_ps = ctx.enter_context(psum(nc, "att_sps", [P, 2, TP_], F32))
        t_ps = ctx.enter_context(psum(nc, "att_tps", [P, 2, 4, P], F32))
        o_ps = ctx.enter_context(psum(nc, "att_ops", [P, 2, 512], F32))
        with stage(nc, "counts_in", "scored", "maxed", "expd", "normed", "turned", "turned_in", "valued",
                   "out_in", "dve_step") as (block, s):
            @block.sync
            def _(sp):
                sp.dma_start(lc[:], m.dram.count_prompt).then_inc(s.counts_in, 16)

            @block.tensor
            def _(pe):
                def scores(u):
                    qt, h = units[u]
                    c, o = h // 2, 64 * (h % 2)
                    n = (qt + 1) * P
                    if u >= 2:
                        pe.wait_ge(s.maxed, u - 1)
                    nc.tensor.matmul(s_ps[:, u % 2, 0:n], m.proj[o:o + 64, BQ + c, qt * P:(qt + 1) * P],
                                     m.proj[o:o + 64, BK + c, 0:n], start=True, stop=True).then_inc(s.scored, 1)

                scores(0)
                for u, (qt, h) in enumerate(units):
                    if u + 1 < len(units):
                        scores(u + 1)
                    c, o = h // 2, 64 * (h % 2)
                    pe.wait_ge(s.normed, u + 1)
                    if u >= 2:
                        pe.wait_ge(s.turned_in, u - 1)
                    for b in range(qt + 1):
                        ins = nc.tensor.transpose(t_ps[:, u % 2, b, :], pr[:, u % 2, b * P:(b + 1) * P], m.ident[:])
                    ins.then_inc(s.turned, 1)
                    pe.wait_ge(s.turned_in, u + 1)
                    if u >= 2:
                        pe.wait_ge(s.out_in, u - 1)
                    for b in range(qt + 1):
                        ins = nc.tensor.matmul(o_ps[o:o + 64, u % 2, 0:P], m.v_tok[:, b, h * HD:(h + 1) * HD],
                                               pt[:, u % 2, b, :], start=(b == 0), stop=(b == qt))
                    ins.then_inc(s.valued, 1)

            @block.scalar
            def _(act):
                for u, (qt, h) in enumerate(units):
                    n = (qt + 1) * P
                    act.wait_ge(s.maxed, u + 1)
                    if u >= 2:
                        act.wait_ge(s.turned, u - 1)
                    nc.scalar.activation(pr[:, u % 2, 0:n], sm[:, u % 2, 0:n], ACT.Exp, bias=st_[:, u % 2, 0:1],
                                         accum_out=st_[:, u % 2, 1:2]).then_inc(s.expd, 1)
                    act.wait_ge(s.turned, u + 1)
                    if u >= 2:
                        act.wait_ge(s.valued, u - 1)
                    nc.scalar.activation(pt[:, u % 2, 0:qt + 1, :], t_ps[:, u % 2, 0:qt + 1, :],
                                         ACT.Copy).then_inc(s.turned_in, 1)

            @block.vector
            def _(dve):
                st = Steps(dve, s.dve_step)
                dve.wait_ge(s.counts_in, 16)

                def mask_max(u):
                    qt = units[u][0]
                    n = (qt + 1) * P
                    dve.wait_ge(s.scored, u + 1)
                    if u >= 2:
                        dve.wait_ge(s.expd, u - 1)
                    st.link(nc.vector.scalar_tensor_tensor(out=sm[:, u % 2, 0:n], in0=s_ps[:, u % 2, 0:n],
                                                           scalar=HD ** -0.5, in1=lc[:, qt, 0:n],
                                                           op0=ALU.mult, op1=ALU.add))
                    nc.vector.tensor_reduce(st_[:, u % 2, 0:1], sm[:, u % 2, 0:n], X, ALU.max,
                                            negate=True).then_inc(s.maxed, 1)

                def collect(u):
                    qt, h = units[u]
                    c, o = h // 2, 64 * (h % 2)
                    dve.wait_ge(s.valued, u + 1)
                    nc.vector.tensor_copy(m.mixed[o:o + 64, 2 + c, qt * P:(qt + 1) * P],
                                          o_ps[o:o + 64, u % 2, 0:P]).then_inc(s.out_in, 1)

                mask_max(0)
                for u, (qt, h) in enumerate(units):
                    if u + 1 < len(units):
                        mask_max(u + 1)
                    n = (qt + 1) * P
                    dve.wait_ge(s.expd, u + 1)
                    st.link(nc.vector.reciprocal(st_[:, u % 2, 2:3], st_[:, u % 2, 1:2]))
                    nc.vector.tensor_scalar(pr[:, u % 2, 0:n], pr[:, u % 2, 0:n], st_[:, u % 2, 2:3], None,
                                            ALU.mult).then_inc(s.normed, 1)
                    if u >= 1:
                        collect(u - 1)
                collect(len(units) - 1)


def attend_sample(nc, m):
    R = HEADS * STEPS
    NKEYS = PAST + TS_
    NKB = PAST // P
    with ExitStack() as ctx:
        kc = ctx.enter_context(sbuf(nc, "dec_k", [P, 2, PAIRS, PAST], F32))
        vc = ctx.enter_context(sbuf(nc, "dec_v", [P, 2, NKB, HEADS * HD], F32))
        lcp = ctx.enter_context(sbuf(nc, "dec_lcp", [R, PAST], F32))
        lcn = ctx.enter_context(sbuf(nc, "dec_lcn", [R, REQ, TS_], F32))
        qbd = ctx.enter_context(sbuf(nc, "dec_q", [P, REQ, PAIRS, R], F32))
        sm = ctx.enter_context(sbuf(nc, "dec_s", [R, NKEYS], F32))
        pr = ctx.enter_context(sbuf(nc, "dec_p", [R, NKEYS], F32))
        pt = ctx.enter_context(sbuf(nc, "dec_pt", [P, NKB + 1, R], F32))
        st_ = ctx.enter_context(sbuf(nc, "dec_stat", [R, 4], F32))
        s_ps = ctx.enter_context(psum(nc, "dec_sps", [R, 3, 512], F32))
        t_bank = ctx.enter_context(psum(nc, "dec_tps", [P, 512], F32))
        t_ps = t_bank[:, 0:(NKB + 1) * R].rearrange("p (n r) -> p n r", r=R)
        o_ps = ctx.enter_context(psum(nc, "dec_ops", [P, PAIRS, 16], F32))
        with stage(nc, "counts_in", "kv_in0", "kv_in1", "q_in", "scored", "maxed", "expd", "normed", "turned",
                   "turned_in", "valued", "out_in", "dve_step") as (block, s):
            kv_in = (s.kv_in0, s.kv_in1)

            @block.sync
            def _(sp):
                sp.dma_start(lcp[:], m.dram.count_past).then_inc(s.counts_in, 16)
                sp.dma_start(lcn[:], m.dram.count_new).then_inc(s.counts_in, 16)
                for b in range(REQ):
                    if b >= 2:
                        sp.wait_ge(s.valued, b - 1)
                    sp.dma_start(kc[:, b % 2], m.dram.cache_kT[m.l, b]).then_inc(kv_in[b % 2], 16)
                    sp.dma_start(vc[:, b % 2], m.dram.cache_v[m.l, b]).then_inc(kv_in[b % 2], 16)

            @block.tensor
            def _(pe):
                pe.wait_ge(s.q_in, 1)
                for b in range(REQ):
                    pe.wait_ge(kv_in[b % 2], 32 * (b // 2 + 1))
                    if b:
                        pe.wait_ge(s.maxed, b)
                    for c in range(PAIRS):
                        for n in range(2):
                            nc.tensor.matmul(s_ps[:, n, :], qbd[:, b, c, :], kc[:, b % 2, c, n * 512:(n + 1) * 512],
                                             start=(c == 0), stop=(c == PAIRS - 1))
                        ins = nc.tensor.matmul(s_ps[:, 2, 0:TS_], qbd[:, b, c, :], m.proj[:, BK + c, TP_:T],
                                               start=(c == 0), stop=(c == PAIRS - 1))
                    ins.then_inc(s.scored, 1)
                    pe.wait_ge(s.normed, b + 1)
                    for n in range(NKB):
                        nc.tensor.transpose(t_ps[:, n, :], pr[:, n * P:(n + 1) * P], m.ident[0:R, 0:R])
                    nc.tensor.transpose(t_ps[0:TS_, NKB, :], pr[:, PAST:NKEYS], m.ident[0:R, 0:R]
                                        ).then_inc(s.turned, 1)
                    pe.wait_ge(s.turned_in, b + 1)
                    if b:
                        pe.wait_ge(s.out_in, b)
                    for c in range(PAIRS):
                        for n in range(NKB):
                            nc.tensor.matmul(o_ps[:, c, :], vc[:, b % 2, n, c * P:(c + 1) * P],
                                             pt[:, n, 16 * c:16 * c + 16], start=(n == 0), stop=False)
                        ins = nc.tensor.matmul(o_ps[:, c, :], m.v_tok[0:TS_, 4, c * P:(c + 1) * P],
                                               pt[0:TS_, NKB, 16 * c:16 * c + 16], start=False, stop=True)
                    ins.then_inc(s.valued, 1)

            @block.scalar
            def _(act):
                for b in range(REQ):
                    act.wait_ge(s.maxed, b + 1)
                    nc.scalar.activation(pr[:], sm[:], ACT.Exp, bias=st_[:, 0:1],
                                         accum_out=st_[:, 1:2]).then_inc(s.expd, 1)
                    act.wait_ge(s.turned, b + 1)
                    nc.scalar.activation(pt[:, 0:NKB, :], t_ps[:, 0:NKB, :], ACT.Copy)
                    nc.scalar.activation(pt[0:TS_, NKB, :], t_ps[0:TS_, NKB, :], ACT.Copy).then_inc(s.turned_in, 1)

            @block.vector
            def _(dve):
                st = Steps(dve, s.dve_step)
                st.link(nc.vector.memset(qbd[:], 0.0))
                for h in range(HEADS):
                    c, o = h // 2, 64 * (h % 2)
                    ins = nc.vector.tensor_copy(
                        qbd[o:o + 64, :, c, h * STEPS:(h + 1) * STEPS],
                        m.proj[o:o + 64, BQ + c, TP_:T].rearrange("p (b t) -> p b t", b=REQ))
                ins.then_inc(s.q_in, 1)
                dve.wait_ge(s.counts_in, 32)
                for b in range(REQ):
                    dve.wait_ge(s.scored, b + 1)
                    if b:
                        dve.wait_ge(s.expd, b)
                    nc.vector.scalar_tensor_tensor(
                        out=sm[:, 0:PAST], in0=s_ps[:, 0:2, :].rearrange("p a n -> p (a n)"),
                        scalar=HD ** -0.5, in1=lcp[:], op0=ALU.mult, op1=ALU.add)
                    st.link(nc.vector.scalar_tensor_tensor(out=sm[:, PAST:NKEYS], in0=s_ps[:, 2, 0:TS_],
                                                           scalar=HD ** -0.5, in1=lcn[:, b, :],
                                                           op0=ALU.mult, op1=ALU.add))
                    nc.vector.tensor_reduce(st_[:, 0:1], sm[:], X, ALU.max, negate=True).then_inc(s.maxed, 1)
                    dve.wait_ge(s.expd, b + 1)
                    st.link(nc.vector.reciprocal(st_[:, 2:3], st_[:, 1:2]))
                    nc.vector.tensor_scalar(pr[:], pr[:], st_[:, 2:3], None, ALU.mult).then_inc(s.normed, 1)
                    dve.wait_ge(s.valued, b + 1)
                    for o in range(2):
                        q = slice(64 * o, 64 * o + 64)
                        ins = nc.vector.tensor_copy(m.mixed[q, 2:5, TP_ + b * STEPS:TP_ + (b + 1) * STEPS],
                                                    o_ps[q, :, 8 * o:8 * o + 8])
                    ins.then_inc(s.out_in, 1)


def rwkv_prepare(nc, m, r):
    rw = m.proj_rw[:]
    halves = [(c, half, slice(half * HALF, (half + 1) * HALF)) for c in range(PAIRS) for half in range(2)]
    with ExitStack() as ctx:
        diff = ctx.enter_context(sbuf(nc, "rw_diff", [P, NB_RW, T], F32))
        wd = ctx.enter_context(sbuf(nc, "rw_wd", [P, T], F32))
        sq = ctx.enter_context(sbuf(nc, "rw_sq", [P, PAIRS, T], F32))
        tmp = ctx.enter_context(sbuf(nc, "rw_tmp", [P, PAIRS, T], F32))
        shift = ctx.enter_context(sbuf(nc, "rw_shift", [P, NB_RW, REQ], F32))
        last_p = ctx.enter_context(sbuf(nc, "rw_last_p", [P, NB_RW, 1], F32))
        last_s = ctx.enter_context(sbuf(nc, "rw_last_s", [P, NB_RW, REQ], F32))
        mu = ctx.enter_context(sbuf(nc, "rw_mu", [P, NB_RW], F32))
        vec = ctx.enter_context(sbuf(nc, "rw_vec", [P, 7, PAIRS], F32))
        wa_up = ctx.enter_context(sbuf(nc, "rw_wa", [P, PAIRS * P], F32))
        g_up = ctx.enter_context(sbuf(nc, "rw_g", [P, PAIRS * P], F32))
        ps = ctx.enter_context(psum(nc, "rw_ps", [P, 6, 512], F32))
        W0, A0, KK, KA, RK = 0, 1, 2, 3, 4

        def vecb(i):
            return vec[:, i, :].unsqueeze(2).to_broadcast([P, PAIRS, T])

        with stage(nc, "loaded", "shifted", "stored", "dve_step", "act_step", "gates_in", "w_up", "w_read",
                   "a_up", "a_read", "g_done", "g_read", "squared", "summed", "rooted", "prod", "bonus_sum",
                   "bonus_read", "decays", "scanned", "lasts") as (block, s):
            @block.sync
            def _(sp):
                for dst, src in ((shift[:], m.dram.state_shift[m.l]), (mu[:], m.dram.rwkv_mu[m.l]), (vec[:], m.dram.rwkv_vec[m.l]),
                                 (wa_up[:], m.dram.rwkv_wa[m.l]), (g_up[:], m.dram.rwkv_g[m.l])):
                    sp.dma_start(dst, src).then_inc(s.loaded, 16)
                sp.wait_ge(s.lasts, 2)
                sp.dma_start(m.dram.p_shift[m.l], last_p[:]).then_inc(s.stored, 16)
                sp.dma_start(m.dram.s_shift[m.l], last_s[:]).then_inc(s.stored, 16)
                sp.wait_ge(s.stored, 32)

            @block.tensor
            def _(pe):
                pe.wait_ge(s.gates_in, 1)
                for n, (c, half, t) in enumerate(halves):
                    ins = nc.tensor.matmul(ps[:, n, 0:HALF], wa_up[0:64, c * P:(c + 1) * P], wd[0:64, t],
                                           start=True, stop=True)
                ins.then_inc(s.w_up, 1)
                pe.wait_ge(s.w_read, 6)
                for n, (c, half, t) in enumerate(halves):
                    ins = nc.tensor.matmul(ps[:, n, 0:HALF], wa_up[64:P, c * P:(c + 1) * P], diff[64:P, 9, t],
                                           start=True, stop=True)
                ins.then_inc(s.a_up, 1)
                pe.wait_ge(s.a_read, 6)
                pe.wait_ge(s.gates_in, 2)
                for n, (c, half, t) in enumerate(halves):
                    ins = nc.tensor.matmul(ps[:, n, 0:HALF], g_up[:, c * P:(c + 1) * P], r.g[:, 0, t],
                                           start=True, stop=True)
                ins.then_inc(s.g_done, 1)
                pe.wait_ge(s.g_read, 6)
                pe.wait_ge(s.squared, 1)
                for n, (c, half, t) in enumerate(halves):
                    ins = nc.tensor.matmul(ps[:, n, 0:HALF], m.pair_ones[:], sq[:, c, t], start=True, stop=True)
                ins.then_inc(s.summed, 1)
                pe.wait_ge(s.rooted, 6)
                pe.wait_ge(s.prod, 1)
                for n, (c, half, t) in enumerate(halves):
                    ins = nc.tensor.matmul(ps[:, n, 0:HALF], m.pair_ones[:], tmp[:, c, t], start=True, stop=True)
                ins.then_inc(s.bonus_sum, 1)

            @block.scalar
            def _(act):
                nc.scalar.activation(last_p[:], rw[:, :, TP_ - 1:TP_], ACT.Copy).then_inc(s.lasts, 1)
                nc.scalar.activation(last_s[:], rw[:, :, TP_ + STEPS - 1:T:STEPS], ACT.Copy).then_inc(s.lasts, 1)
                act.wait_ge(s.shifted, 1)
                nc.scalar.activation(wd[0:64, :], diff[0:64, 9, :], ACT.Tanh).then_inc(s.gates_in, 1)
                nc.scalar.activation(r.g[:, 0, :], diff[:, 10, :], ACT.Sigmoid).then_inc(s.gates_in, 1)
                act.wait_ge(s.w_up, 1)
                for n, (c, half, t) in enumerate(halves):
                    nc.scalar.activation(r.ld[:, c, t], ps[:, n, 0:HALF], ACT.Sigmoid,
                                         bias=vec[:, W0, c:c + 1]).then_inc(s.w_read, 1)
                act.wait_ge(s.a_up, 1)
                for n, (c, half, t) in enumerate(halves):
                    nc.scalar.activation(r.b[:, c, t], ps[:, n, 0:HALF], ACT.Sigmoid,
                                         bias=vec[:, A0, c:c + 1]).then_inc(s.a_read, 1)
                act.wait_ge(s.g_done, 1)
                for n, (c, half, t) in enumerate(halves):
                    nc.scalar.activation(r.g[:, c, t], ps[:, n, 0:HALF], ACT.Copy).then_inc(s.g_read, 1)
                act.wait_ge(s.summed, 1)
                for n, (c, half, t) in enumerate(halves):
                    nc.scalar.activation(sq[:, c, t], ps[:, n, 0:HALF], ACT.Sqrt).then_inc(s.rooted, 1)
                act.wait_ge(s.scanned, 1)
                nc.scalar.activation(r.inv[:], r.cum[:], ACT.Exp, scale=-1.0).then_inc(s.decays, 1)
                nc.scalar.activation(r.end[:], r.end[:], ACT.Exp).then_inc(s.decays, 1)
                nc.scalar.activation(r.prev[:], r.prev[:], ACT.Exp).then_inc(s.decays, 1)
                act.wait_ge(s.decays, 1)
                nc.scalar.activation(r.cum[:], r.cum[:], ACT.Exp).then_inc(s.decays, 1)

            @block.vector
            def _(dve):
                st = Steps(dve, s.dve_step)

                def split(x, lo, hi):
                    return x[:, lo:hi, TP_:T].rearrange("p c (b t) -> p c b t", b=REQ)

                dve.wait_ge(s.loaded, 80)
                nc.vector.tensor_tensor(diff[:, :, 1:TP_], rw[:, :, 0:TP_ - 1], rw[:, :, 1:TP_], ALU.subtract)
                nc.vector.tensor_scalar(diff[:, :, 0:1], rw[:, :, 0:1], -1.0, None, ALU.mult)
                nc.vector.tensor_tensor(split(diff, 0, NB_RW)[:, :, :, 1:STEPS], split(rw, 0, NB_RW)[:, :, :, 0:STEPS - 1],
                                        split(rw, 0, NB_RW)[:, :, :, 1:STEPS], ALU.subtract)
                st.link(nc.vector.tensor_tensor(split(diff, 0, NB_RW)[:, :, :, 0], shift[:],
                                                split(rw, 0, NB_RW)[:, :, :, 0], ALU.subtract))
                st.link(nc.vector.tensor_tensor(diff[:], diff[:], mu[:].unsqueeze(2).to_broadcast([P, NB_RW, T]),
                                                ALU.mult))
                nc.vector.tensor_tensor(diff[:], diff[:], rw, ALU.add).then_inc(s.shifted, 1)
                dve.wait_ge(s.shifted, 1)
                r_, k_, v_ = diff[:, 0:3, :], diff[:, 3:6, :], diff[:, 6:9, :]
                st.link(nc.vector.tensor_copy(r.r[:], r_))
                st.link(nc.vector.tensor_copy(r.v[:], v_))
                st.link(nc.vector.tensor_tensor(r.kk[:], k_, vecb(KK), ALU.mult))
                nc.vector.tensor_tensor(sq[:], r.kk[:], r.kk[:], ALU.mult).then_inc(s.squared, 1)
                dve.wait_ge(s.w_read, 6)
                st.link(nc.vector.tensor_scalar(r.ld[:], r.ld[:], -DECAY, None, ALU.mult))
                for c in range(PAIRS):
                    ins = nc.vector.tensor_tensor_scan(r.cum[:, c, :], m.chunk_reset[:], r.ld[:, c, :], 0.0,
                                                       ALU.mult, ALU.add)
                    st.link(ins)
                nc.vector.tensor_tensor(r.prev[:], r.cum[:], r.ld[:], ALU.subtract)
                for lo, hi, n, w in ((0, TP_, NCH, CH), (TP_, T, REQ, STEPS)):
                    for c in range(PAIRS):
                        cum = r.cum[:, c, lo:hi].rearrange("p (n w) -> p n w", n=n)
                        ins = nc.vector.tensor_tensor(r.end[:, c, lo:hi].rearrange("p (n w) -> p n w", n=n),
                                                      cum[:, :, w - 1:w].to_broadcast([P, n, w]), cum, ALU.subtract)
                ins.then_inc(s.scanned, 1)
                dve.wait_ge(s.a_read, 6)
                st.link(nc.vector.scalar_tensor_tensor(out=tmp[:], in0=r.b[:], scalar=-1.0, in1=k_,
                                                       op0=ALU.add, op1=ALU.mult))
                st.link(nc.vector.tensor_tensor(tmp[:], tmp[:], vecb(KA), ALU.mult))
                st.link(nc.vector.tensor_tensor(r.k[:], tmp[:], k_, ALU.add))
                dve.wait_ge(s.rooted, 6)
                st.link(nc.vector.tensor_scalar(sq[:], sq[:], 1e-12, None, ALU.max))
                st.link(nc.vector.reciprocal(sq[:], sq[:]))
                st.link(nc.vector.tensor_tensor(r.kk[:], r.kk[:], sq[:], ALU.mult))
                st.link(nc.vector.tensor_tensor(r.b[:], r.b[:], r.kk[:], ALU.mult))
                st.link(nc.vector.tensor_tensor(tmp[:], r.r[:], r.k[:], ALU.mult))
                nc.vector.tensor_tensor(tmp[:], tmp[:], vecb(RK), ALU.mult).then_inc(s.prod, 1)
                dve.wait_ge(s.bonus_sum, 1)
                for n, (c, half, t) in enumerate(halves):
                    nc.vector.tensor_tensor(r.bonus[:, c, t], ps[:, n, 0:HALF], r.v[:, c, t], ALU.mult)
                dve.wait_ge(s.decays, 4)


def rwkv_tile(nc, m, r, lo, w, masks, chunks):
    sample = chunks == 0
    t = bass.ds(lo, w)
    H3 = HEADS * HD
    with ExitStack() as ctx:
        def sb(name, shape):
            return ctx.enter_context(sbuf(nc, name, shape, F32))

        kr = sb("rt_kr", [P, PAIRS, 2, w])
        ki, bi = sb("rt_ki", [P, PAIRS, w]), sb("rt_bi", [P, PAIRS, w])
        ke, be, vs = sb("rt_ke", [P, PAIRS, w]), sb("rt_be", [P, PAIRS, w]), sb("rt_vs", [P, PAIRS, w])
        dc = sb("rt_dc", [P, PAIRS, REQ])
        tok = sb("rt_tok", [w, 4, H3])
        n_m = sb("rt_n", [w, HEADS, 2, w])
        qb = sb("rt_qb", [w, HEADS, w])
        bq = sb("rt_bq", [w, HEADS, 2, w])
        mm_ = sb("rt_m", [w, HEADS, w])
        tt = sb("rt_tt", [w, HEADS, w])
        bv, uv = sb("rt_bv", [w, HEADS, HD]), sb("rt_uv", [w, HEADS, HD])
        wt = sb("rt_wt", [P, PAIRS, w])
        u = sb("rt_u", [w, HEADS, HD])
        o = sb("rt_o", [w, HEADS, HD])
        osq = sb("rt_osq", [w, HEADS, HD])
        stat = sb("rt_stat", [w, 4, HEADS])
        if sample:
            ux, vx = sb("rt_ux", [w, REQ, HD]), sb("rt_vx", [w, REQ, HD])
        ps = ctx.enter_context(psum(nc, "rt_ps", [P, 8, 512], F32))
        pos = lambda h: (h // 2, 64 * (h % 2))
        strict_incl, neg_strict_incl, neg_lower = masks
        names = ["staged", "turned", "turned_in", "gram", "gram_in", "powers", "powers_in", "last_power",
                 "folded", "bv_made", "bv_in", "uv_made", "uv_in", "wt_in", "u_made", "u_in", "st_made", "st_in",
                 "inter_in", "intra", "normed", "back", "back_in", "dve_step", "a_step"]
        with stage(nc, *names) as (block, s):
            @block.vector
            def _(dve):
                st = Steps(dve, s.dve_step)
                nc.vector.tensor_tensor(kr[:, :, 0, :], r.kk[:, :, t], r.prev[:, :, t], ALU.mult)
                nc.vector.tensor_tensor(kr[:, :, 1, :], r.r[:, :, t], r.cum[:, :, t], ALU.mult)
                nc.vector.tensor_tensor(ki[:], r.k[:, :, t], r.inv[:, :, t], ALU.mult)
                nc.vector.tensor_tensor(bi[:], r.b[:, :, t], r.inv[:, :, t], ALU.mult)
                nc.vector.tensor_tensor(ke[:], r.k[:, :, t], r.end[:, :, t], ALU.mult)
                nc.vector.scalar_tensor_tensor(out=be[:], in0=r.b[:, :, t], scalar=-1.0, in1=r.end[:, :, t],
                                               op0=ALU.mult, op1=ALU.mult)
                nc.vector.tensor_copy(vs[:], r.v[:, :, t])
                step = STEPS if sample else CH
                nch = w // step
                for c in range(PAIRS):
                    ins = nc.vector.tensor_copy(
                        dc[:, c, 0:nch].unsqueeze(2),
                        r.cum[:, c, t].rearrange("p (n w) -> p n w", w=step)[:, :, step - 1:step])
                ins.then_inc(s.staged, 1)
                for i in range(4):
                    dve.wait_ge(s.turned, i + 1)
                    nc.vector.tensor_copy(tok[:, i, :], ps[0:w, i, 0:H3]).then_inc(s.turned_in, 1)
                dve.wait_ge(s.gram, HEADS)
                for h in range(HEADS):
                    nc.vector.tensor_tensor(n_m[:, h, 0, :], ps[0:w, h, 0:w], neg_strict_incl[0:w, 0, 0:w], ALU.mult)
                    nc.vector.tensor_tensor(qb[:, h, :], ps[0:w, h, w:2 * w], neg_strict_incl[0:w, 1, 0:w], ALU.mult)
                    nc.vector.tensor_tensor(bq[:, h, :, :], ps[0:w, h, 2 * w:4 * w].rearrange("p (a w) -> p a w", a=2),
                                            strict_incl[0:w, :, 0:w], ALU.mult)
                    st.link(nc.vector.tensor_tensor(n_m[:, h, 1, :], ps[0:w, 6 + h % 2, (h // 2) * w:(h // 2 + 1) * w],
                                                    neg_lower[0:w, 0:w], ALU.mult))
                    nc.vector.tensor_tensor(tt[:, h, :], n_m[:, h, 0, :], m.ident[0:w, 0:w],
                                            ALU.add).then_inc(s.gram_in, 1)
                for k in range(4):
                    for h in range(HEADS):
                        dve.wait_ge(s.powers, 6 * k + h + 1)
                        nc.vector.tensor_copy(n_m[:, h, :, :].rearrange("p a w -> p (a w)"), ps[0:w, h, 0:2 * w]
                                              ).then_inc(s.powers_in, 1)
                    for h in range(HEADS):
                        dve.wait_ge(s.folded, 6 * k + h + 1)
                        nc.vector.tensor_tensor(tt[:, h, :], tt[:, h, :], ps[0:w, h, 2 * w:3 * w],
                                                ALU.add).then_inc(s.last_power, 1)
                for h in range(HEADS):
                    dve.wait_ge(s.uv_made, h + 1)
                    c, q = pos(h)
                    nc.vector.tensor_copy(uv[:, h, :], ps[0:w, h, 64:128])
                    nc.vector.tensor_copy(wt[q:q + 64, c, :], ps[q:q + 64, h, 256:256 + w]).then_inc(s.uv_in, 1)
                if not sample:
                    for n in range(chunks):
                        q = slice(n * CH, (n + 1) * CH)
                        dve.wait_ge(s.u_made, n + 1)
                        heads = lambda x: x[q, :, :].rearrange("p (c a) i -> p c a i", a=2)
                        banks = lambda k: ps[q, k:k + 2, 0:PAIRS * HD].rearrange("p a (c i) -> p c a i", c=PAIRS)
                        nc.vector.tensor_tensor(heads(u), heads(uv), banks(0), ALU.add).then_inc(s.u_in, 1)
                        nc.vector.tensor_copy(heads(o), banks(4))
                        st.link(nc.vector.tensor_tensor(r.state[:], r.state[:],
                                                        dc[:, :, n:n + 1].to_broadcast([P, PAIRS, HD]), ALU.mult))
                        dve.wait_ge(s.st_made, n + 1)
                        nc.vector.tensor_tensor(r.state[:], r.state[:],
                                                ps[:, 2, 0:PAIRS * HD].rearrange("p (c i) -> p c i", c=PAIRS),
                                                ALU.add).then_inc(s.st_in, 1)
                        dve.wait_ge(s.st_in, n + 1)
                else:
                    own = m.own_req[:, :].unsqueeze(2).to_broadcast([w, REQ, HD])
                    for h in range(HEADS):
                        c, q = pos(h)
                        cols = lambda bank: ps[0:w, bank, :].rearrange("p (b i) -> p b i", b=REQ)
                        dve.wait_ge(s.u_made, h + 1)
                        st.link(nc.vector.tensor_tensor(ux[:], cols(0),
                                                        uv[:, h, :].unsqueeze(1).to_broadcast([w, REQ, HD]), ALU.add))
                        st.link(nc.vector.tensor_tensor(ux[:], ux[:], own, ALU.mult))
                        nc.vector.tensor_tensor(vx[:], tok[:, 3, h * HD:(h + 1) * HD].unsqueeze(1)
                                                .to_broadcast([w, REQ, HD]), own, ALU.mult).then_inc(s.u_in, 1)
                        nc.vector.tensor_reduce(u[:, h, :], ux[:].rearrange("p b i -> p i b"), X, ALU.add)
                        dve.wait_ge(s.st_made, h + 1)
                        st.link(nc.vector.tensor_tensor(vx[:], cols(1), own, ALU.mult))
                        nc.vector.tensor_reduce(o[:, h, :], vx[:].rearrange("p b i -> p i b"), X, ALU.add)
                        state = r.states[q:q + 64, c, :, :]
                        st.link(nc.vector.tensor_tensor(state, state, dc[q:q + 64, c, :].unsqueeze(2)
                                                        .to_broadcast([64, REQ, HD]), ALU.mult))
                        nc.vector.tensor_tensor(state, state,
                                                ps[q:q + 64, 2, :].rearrange("p (b i) -> p b i", b=REQ),
                                                ALU.add).then_inc(s.st_in, 1)
                        dve.wait_ge(s.st_in, h + 1)
                dve.wait_ge(s.intra, 1)
                st.link(nc.vector.tensor_tensor(o[:], o[:], ps[0:w, 3, 0:H3].rearrange("p (h i) -> p h i", h=HEADS),
                                                ALU.add))
                st.link(nc.vector.tensor_reduce(stat[:, 0, :], o[:], X, ALU.add))
                st.link(nc.vector.tensor_scalar(stat[:, 0, :], stat[:, 0, :], -1.0 / HD, None, ALU.mult))
                st.link(nc.vector.tensor_tensor(o[:], o[:], stat[:, 0, :].unsqueeze(2).to_broadcast([w, HEADS, HD]),
                                                ALU.add))
                st.link(nc.vector.tensor_tensor(osq[:], o[:], o[:], ALU.mult))
                st.link(nc.vector.tensor_reduce(stat[:, 1, :], osq[:], X, ALU.add))
                nc.vector.tensor_scalar(stat[:, 1, :], stat[:, 1, :], 1.0 / HD, GN_EPS, ALU.mult,
                                        ALU.add).then_inc(s.a_step, 1)
                dve.wait_ge(s.a_step, 2)
                st.link(nc.vector.reciprocal(stat[:, 3, :], stat[:, 2, :]))
                nc.vector.tensor_tensor(o[:], o[:], stat[:, 3, :].unsqueeze(2).to_broadcast([w, HEADS, HD]),
                                        ALU.mult).then_inc(s.normed, 1)
                dve.wait_ge(s.back, 1)
                nc.vector.tensor_copy(m.mixed[:, 5:8, t], ps[:, 4, 0:PAIRS * w].rearrange("p (c w) -> p c w", c=PAIRS))

            @block.scalar
            def _(act):
                for h in range(HEADS):
                    act.wait_ge(s.bv_made, h + 1)
                    nc.scalar.activation(bv[:, h, :], ps[0:w, h, 0:64], ACT.Copy).then_inc(s.bv_in, 1)
                act.wait_ge(s.a_step, 1)
                nc.scalar.activation(stat[:, 2, :], stat[:, 1, :], ACT.Sqrt).then_inc(s.a_step, 1)

            @block.tensor
            def _(pe):
                pe.wait_ge(s.staged, 1)
                for i, src in enumerate((kr[:, :, 0, :], ke[:], be[:], vs[:])):
                    for c in range(PAIRS):
                        ins = nc.tensor.transpose(ps[0:w, i, c * P:(c + 1) * P], src[:, c, :], m.ident[:])
                    ins.then_inc(s.turned, 1)
                pe.wait_ge(s.turned_in, 4)
                for h in range(HEADS):
                    c, q = pos(h)
                    q = slice(q, q + 64)
                    both = kr[q, c, :, :].rearrange("p a w -> p (a w)")
                    nc.tensor.matmul(ps[0:w, h, 0:2 * w], bi[q, c, :], both, start=True, stop=True)
                    nc.tensor.matmul(ps[0:w, h, 2 * w:4 * w], ki[q, c, :], both, start=True, stop=True)
                    nc.tensor.matmul(ps[0:w, 6 + h % 2, (h // 2) * w:(h // 2 + 1) * w], kr[q, c, 0, :], bi[q, c, :],
                                     start=True, stop=True).then_inc(s.gram, 1)
                for k in range(4):
                    for h in range(HEADS):
                        if k == 0:
                            pe.wait_ge(s.gram_in, h + 1)
                        else:
                            pe.wait_ge(s.last_power, 6 * (k - 1) + h + 1)
                        nc.tensor.matmul(ps[0:w, h, 0:w], n_m[:, h, 1, :], n_m[:, h, 0, :], start=True, stop=True)
                        nc.tensor.matmul(ps[0:w, h, w:2 * w], n_m[:, h, 0, :], n_m[:, h, 1, :],
                                         start=True, stop=True).then_inc(s.powers, 1)
                    for h in range(HEADS):
                        pe.wait_ge(s.powers_in, 6 * k + h + 1)
                        nc.tensor.matmul(ps[0:w, h, 2 * w:3 * w], n_m[:, h, 1, :], tt[:, h, :],
                                         start=True, stop=True).then_inc(s.folded, 1)
                for h in range(HEADS):
                    pe.wait_ge(s.last_power, 18 + h + 1)
                    nc.tensor.matmul(ps[0:w, h, 0:64], bq[:, h, 0, :], tok[:, 3, h * HD:(h + 1) * HD],
                                     start=True, stop=True).then_inc(s.bv_made, 1)
                for h in range(HEADS):
                    c, q = pos(h)
                    pe.wait_ge(s.bv_in, h + 1)
                    nc.tensor.matmul(ps[0:w, h, 64:128], tt[:, h, :], bv[:, h, :], start=True, stop=True)
                    nc.tensor.matmul(ps[q:q + 64, h, 256:256 + w], tok[:, 0, h * HD:(h + 1) * HD], tt[:, h, :],
                                     start=True, stop=True).then_inc(s.uv_made, 1)
                pe.wait_ge(s.uv_in, HEADS)
                if not sample:
                    for n in range(chunks):
                        if n:
                            pe.wait_ge(s.st_in, n)
                        tc = slice(n * CH, (n + 1) * CH)
                        for h in range(HEADS):
                            c, q = pos(h)
                            q = slice(q, q + 64)
                            odd, ci = h % 2, slice(c * HD, (c + 1) * HD)
                            nc.tensor.matmul(ps[tc, odd, ci], wt[q, c, tc], r.state[q, c, :], start=True, stop=True)
                            ins = nc.tensor.matmul(ps[tc, 4 + odd, ci], kr[q, c, 1, tc], r.state[q, c, :],
                                                   start=True, stop=True)
                        ins.then_inc(s.u_made, 1)
                        pe.wait_ge(s.u_in, n + 1)
                        for h in range(HEADS):
                            c, q = pos(h)
                            out = ps[q:q + 64, 2, c * HD:(c + 1) * HD]
                            nc.tensor.matmul(out, tok[tc, 1, h * HD:(h + 1) * HD], tok[tc, 3, h * HD:(h + 1) * HD],
                                             start=True, stop=False)
                            ins = nc.tensor.matmul(out, tok[tc, 2, h * HD:(h + 1) * HD], u[tc, h, :],
                                                   start=False, stop=True)
                        ins.then_inc(s.st_made, 1)
                    pe.wait_ge(s.st_in, chunks)
                else:
                    for h in range(HEADS):
                        c, q = pos(h)
                        q = slice(q, q + 64)
                        if h:
                            pe.wait_ge(s.st_in, h)
                        state = r.states[q, c, :, :].rearrange("p b i -> p (b i)")
                        nc.tensor.matmul(ps[0:w, 0, :], wt[q, c, :], state, start=True, stop=True)
                        nc.tensor.matmul(ps[0:w, 1, :], kr[q, c, 1, :], state, start=True,
                                         stop=True).then_inc(s.u_made, 1)
                        pe.wait_ge(s.u_in, h + 1)
                        nc.tensor.matmul(ps[q, 2, :], tok[:, 1, h * HD:(h + 1) * HD],
                                         vx[:].rearrange("p b i -> p (b i)"), start=True, stop=False)
                        nc.tensor.matmul(ps[q, 2, :], tok[:, 2, h * HD:(h + 1) * HD],
                                         ux[:].rearrange("p b i -> p (b i)"), start=False,
                                         stop=True).then_inc(s.st_made, 1)
                    pe.wait_ge(s.st_in, HEADS)
                for h in range(HEADS):
                    out = ps[0:w, 3, h * HD:(h + 1) * HD]
                    nc.tensor.matmul(out, qb[:, h, :], u[:, h, :], start=True, stop=False)
                    ins = nc.tensor.matmul(out, bq[:, h, 1, :], tok[:, 3, h * HD:(h + 1) * HD],
                                           start=False, stop=True)
                ins.then_inc(s.intra, 1)
                pe.wait_ge(s.normed, 1)
                for c in range(PAIRS):
                    ins = nc.tensor.transpose(ps[:, 4, c * w:(c + 1) * w],
                                              o[:, 2 * c:2 * c + 2, :].rearrange("p h i -> p (h i)"),
                                              m.ident[0:w, 0:w])
                ins.then_inc(s.back, 1)


def rwkv(nc, m):
    with ExitStack() as ctx:
        def sb(name, shape):
            return ctx.enter_context(sbuf(nc, name, shape, F32))

        r = Parts()
        r.r, r.k, r.v, r.kk, r.b, r.g, r.bonus = (sb("rwkv_" + n, [P, PAIRS, T])
                                                  for n in ("r", "k", "v", "kk", "b", "g", "bonus"))
        r.ld, r.cum, r.prev, r.inv, r.end = (sb("rwkv_" + n, [P, PAIRS, T])
                                             for n in ("ld", "cum", "prev", "inv", "end"))
        rwkv_prepare(nc, m, r)
        r.state = sb("rwkv_state", [P, PAIRS, HD])
        r.states = sb("rwkv_states", [P, PAIRS, REQ, HD])
        ln = sb("rwkv_ln", [P, 7, PAIRS])
        with stage(nc, "loaded", "zeroed") as (block, s):
            @block.sync
            def _(sp):
                sp.dma_start(r.states[:], m.dram.state_wkv[m.l]).then_inc(s.loaded, 16)
                sp.dma_start(ln[:], m.dram.rwkv_vec[m.l]).then_inc(s.loaded, 16)
                sp.wait_ge(s.loaded, 32)

            @block.vector
            def _(dve):
                nc.vector.memset(r.state[:], 0.0)
        with nc.Fori(0, TP_ // P) as i:
            rwkv_tile(nc, m, r, i * P, P, m.masks_prompt, P // CH)
        rwkv_tile(nc, m, r, TP_, TS_, m.masks_sample, 0)
        with stage(nc, "stored", "dve_step") as (block, s):
            @block.sync
            def _(sp):
                sp.dma_start(m.dram.p_wkv[m.l], r.state[:]).then_inc(s.stored, 16)
                sp.dma_start(m.dram.s_wkv[m.l], r.states[:]).then_inc(s.stored, 16)
                sp.wait_ge(s.stored, 32)

            @block.vector
            def _(dve):
                st = Steps(dve, s.dve_step)
                out = m.mixed[:, 5:8, :]
                vecb = lambda n: ln[:, n, :].unsqueeze(2).to_broadcast([P, PAIRS, T])
                st.link(nc.vector.tensor_tensor(out, out, vecb(5), ALU.mult))
                st.link(nc.vector.tensor_tensor(out, out, vecb(6), ALU.add))
                st.link(nc.vector.tensor_tensor(out, out, r.bonus[:], ALU.add))
                st.link(nc.vector.tensor_tensor(out, out, r.g[:], ALU.mult))


def mix_out(nc, m):
    with ExitStack() as ctx:
        w = ctx.enter_context(sbuf(nc, "out_w", [P, KD, D], F32))
        ps = ctx.enter_context(psum(nc, "out_ps", [P, 4, 512], F32))
        with stage(nc, "loaded", "made", "added") as (block, s):
            @block.sync
            def _(sp):
                sp.dma_start(w[:], m.dram.w_out[m.l]).then_inc(s.loaded, 16)

            @block.tensor
            def _(pe):
                pe.wait_ge(s.loaded, 16)
                for n in range(2 * NT):
                    i, half, rows = n // 2, n % 2, ROWS[n // 2]
                    if n >= 4:
                        pe.wait_ge(s.added, n - 3)
                    for k in range(KD):
                        ins = nc.tensor.matmul(ps[0:rows, n % 4, :], m.mixed[:, k, i * P:i * P + rows],
                                               w[:, k, half * 512:(half + 1) * 512],
                                               start=(k == 0), stop=(k == KD - 1))
                    ins.then_inc(s.made, 1)

            @block.vector
            def _(dve):
                for n in range(2 * NT):
                    i, half, rows = n // 2, n % 2, ROWS[n // 2]
                    dve.wait_ge(s.made, n + 1)
                    hh = m.h[0:rows, i, half * 512:(half + 1) * 512]
                    nc.vector.tensor_tensor(hh, hh, ps[0:rows, n % 4, :], ALU.add).then_inc(s.added, 1)


def route(nc, m, qT, keys, i1T, i2T, gT):
    HK = PH * TOPK
    with ExitStack() as ctx:
        def sb(name, shape, dt=F32):
            return ctx.enter_context(sbuf(nc, name, shape, dt))

        qs = sb("rt_q", [P, NB_Q, P])
        sc = sb("rt_sc", [P, NB_Q, NKEY])
        sc2 = sb("rt_sc2", [P, NB_Q, NKEY])
        top = sb("rt_top", [P, NB_Q, TOPK])
        idx = sb("rt_idx", [P, NB_Q, TOPK], U32)
        idxf = sb("rt_idxf", [P, NB_Q, TOPK])
        cand = sb("rt_cand", [P, PH, TOPK * TOPK])
        cand2 = sb("rt_cand2", [P, PH, TOPK * TOPK])
        best = sb("rt_best", [P, PH, TOPK])
        bpos = sb("rt_bpos", [P, PH, TOPK], U32)
        slot = sb("rt_slot", [P, 2, PH, TOPK], U32)
        slotf = sb("rt_slotf", [P, 2, PH, TOPK])
        eq = sb("rt_eq", [P, TOPK, TOPK])
        out = sb("rt_out", [P, 3, PH, TOPK])
        gs = sb("rt_gs", [P, 2, PH])
        ps = ctx.enter_context(psum(nc, "rt_ps", [P, 4, 4, NKEY], F32))
        tps = ctx.enter_context(psum(nc, "rt_tps", [P, 3, P], F32))
        with nc.Fori(0, NT) as i:
            t = bass.ds(i * P, P)
            with stage(nc, "q_in", "scored", "sc_in", "dve_step", "centred", "expd", "outs", "turned") as (block, s):
                @block.gpsimd
                def _(pool_):
                    nc.gpsimd.tensor_copy(qs[:], qT[:, :, t]).then_inc(s.q_in, 1)

                @block.tensor
                def _(pe):
                    pe.wait_ge(s.q_in, 1)
                    for b in range(NB_Q):
                        ins = nc.tensor.matmul(ps[:, b // 4, b % 4, :], qs[:, b, :], keys[:, b, :],
                                               start=True, stop=True)
                        if b % 4 == 3:
                            ins.then_inc(s.scored, 1)
                    pe.wait_ge(s.outs, 1)
                    for n in range(3):
                        ins = nc.tensor.transpose(tps[:, n, :], out[:, n].rearrange("p h k -> p (h k)"), m.ident[:])
                    ins.then_inc(s.turned, 1)

                @block.scalar
                def _(act):
                    for n in range(4):
                        act.wait_ge(s.scored, n + 1)
                        nc.scalar.activation(sc[:, 4 * n:4 * n + 4, :], ps[:, n], ACT.Copy).then_inc(s.sc_in, 1)
                    act.wait_ge(s.centred, 1)
                    nc.scalar.activation(out[:, 2], best[:], ACT.Exp).then_inc(s.expd, 1)

                @block.vector
                def _(dve):
                    st = Steps(dve, s.dve_step)
                    L = st.link

                    def top16(values, spare, best_, where):
                        L(nc.vector.max(best_[:, 0:8], values))
                        nc.vector.max_index(where[:, 0:8], best_[:, 0:8], values)
                        L(nc.vector.match_replace(spare, best_[:, 0:8], values, -3.0e38))
                        L(nc.vector.max(best_[:, 8:16], spare))
                        L(nc.vector.max_index(where[:, 8:16], best_[:, 8:16], spare))

                    for b in range(NB_Q):
                        if b % 4 == 0:
                            dve.wait_ge(s.sc_in, b // 4 + 1)
                        top16(sc[:, b, :], sc2[:, b, :], top[:, b, :], idx[:, b, :])
                    L(nc.vector.tensor_copy(idxf[:], idx[:]))
                    for h in range(PH):
                        L(nc.vector.tensor_tensor(
                            cand[:, h, :].rearrange("p (a b) -> p a b", a=TOPK),
                            top[:, 2 * h, :].unsqueeze(2).to_broadcast([P, TOPK, TOPK]),
                            top[:, 2 * h + 1, :].unsqueeze(1).to_broadcast([P, TOPK, TOPK]), ALU.add))
                        top16(cand[:, h, :], cand2[:, h, :], best[:, h, :], bpos[:, h, :])
                    nc.vector.tensor_scalar(slot[:, 0], bpos[:], 4, None, ALU.logical_shift_right)
                    L(nc.vector.tensor_scalar(slot[:, 1], bpos[:], TOPK - 1, None, ALU.bitwise_and))
                    L(nc.vector.tensor_copy(slotf[:], slot[:]))
                    for h in range(PH):
                        for a in range(2):
                            L(nc.vector.tensor_tensor(eq[:], slotf[:, a, h, :].unsqueeze(2).to_broadcast([P, TOPK, TOPK]),
                                                      m.iota[:, 0:TOPK].unsqueeze(1).to_broadcast([P, TOPK, TOPK]),
                                                      ALU.is_equal))
                            L(nc.vector.tensor_tensor(eq[:], eq[:], idxf[:, 2 * h + a, :].unsqueeze(1)
                                                      .to_broadcast([P, TOPK, TOPK]), ALU.mult))
                            L(nc.vector.tensor_reduce(out[:, a, h, :], eq[:], X, ALU.add))
                    L(nc.vector.tensor_copy(gs[:, 0, :].unsqueeze(2), best[:, :, 0:1]))
                    nc.vector.tensor_tensor(best[:], best[:], gs[:, 0, :].unsqueeze(2).to_broadcast([P, PH, TOPK]),
                                            ALU.subtract).then_inc(s.centred, 1)
                    dve.wait_ge(s.expd, 1)
                    L(nc.vector.tensor_reduce(gs[:, 0, :], out[:, 2], X, ALU.add))
                    L(nc.vector.reciprocal(gs[:, 1, :], gs[:, 0, :]))
                    nc.vector.tensor_tensor(out[:, 2], out[:, 2], gs[:, 1, :].unsqueeze(2).to_broadcast([P, PH, TOPK]),
                                            ALU.mult).then_inc(s.outs, 1)
                    dve.wait_ge(s.turned, 1)
                    for n, dst in enumerate((i1T, i2T, gT)):
                        nc.vector.tensor_copy(dst[:, t], tps[:, n, :])


def gates(nc, m, i1T, i2T, gT):
    TB, BUFS = 4, 3
    NB = UNIT // TB
    with ExitStack() as ctx:
        a1 = ctx.enter_context(sbuf(nc, "g_a1", [P, 2, TB, P], F32))
        a2 = ctx.enter_context(sbuf(nc, "g_a2", [P, 2, TB, P], F32))
        gst = ctx.enter_context(sbuf(nc, "g_stage", [P, BUFS, NKEY, UNIT], F32))
        ps = ctx.enter_context(psum(nc, "g_ps", [P, 4, TB, P], F32))
        names = ["hot", "slots_free", "made", "banks_free", "moved", "unit_free0", "unit_free1", "unit_free2"]
        with stage(nc, *names) as (block, s):
            unit_free = (s.unit_free0, s.unit_free1, s.unit_free2)

            @block.vector
            def _(dve):
                with dve.Fori(0, T // (4 * TB)) as n:
                    for b in range(4):
                        dve.wait_ge(s.slots_free, n * 4 + (b + 1))
                        for j in range(TB):
                            t = bass.ds(n * (4 * TB) + (b * TB + j), 1)
                            nc.vector.tensor_scalar(a2[:, b % 2, j, :], m.iota[:], i2T[:, t], None, ALU.is_equal)
                            ins = nc.vector.tensor_scalar(a1[:, b % 2, j, :], m.iota[:], i1T[:, t], gT[:, t],
                                                          ALU.is_equal, ALU.mult)
                        ins.then_inc(s.hot, 1)

            @block.tensor
            def _(pe):
                pe.sem_inc(s.slots_free, 2)
                with pe.Fori(0, T // (4 * TB)) as n:
                    for b in range(4):
                        pe.wait_ge(s.hot, n * 4 + (b + 1))
                        pe.wait_ge(s.banks_free, n * 4 + (b + 1))
                        for j in range(TB):
                            ins = nc.tensor.matmul(ps[:, b, j, :], a2[:, b % 2, j, :], a1[:, b % 2, j, :],
                                                   start=True, stop=True)
                        ins.then_inc(s.made, 1)
                        pe.wait_ge(s.made, n * 4 + (b + 1))
                        pe.sem_inc(s.slots_free, 1)

            @block.scalar
            def _(act):
                act.sem_inc(s.banks_free, 4)
                for k in range(BUFS):
                    act.sem_inc(unit_free[k], 16)
                with act.Fori(0, NU // BUFS) as n:
                    for k in range(BUFS):
                        act.wait_ge(unit_free[k], n * 16 + 16)
                        with act.Fori(0, NB // 4) as q:
                            for b in range(4):
                                act.wait_ge(s.made, n * (BUFS * NB) + q * 4 + (k * NB + b + 1))
                                nc.scalar.activation(
                                    gst[:, k, :, bass.ds(q * (4 * TB) + b * TB, TB)].rearrange("p i t -> p t i"),
                                    ps[:, b], ACT.Copy).then_inc(s.banks_free, 1)
                        act.wait_ge(s.banks_free, n * (BUFS * NB) + ((k + 1) * NB + 4))
                        act.sem_inc(s.moved, 1)

            @block.sync
            def _(sp):
                with sp.Fori(0, NU // BUFS) as n:
                    for k in range(BUFS):
                        sp.wait_ge(s.moved, n * BUFS + (k + 1))
                        sp.dma_start(m.dram.gate_dram[n * BUFS + k].rearrange("g p c -> p g c"),
                                     gst[:, k].rearrange("p (g e) t -> p g (e t)", e=EG)
                                     ).then_inc(unit_free[k], 16)
                for k in range(BUFS):
                    sp.wait_ge(unit_free[k], 16 * (NU // BUFS) + 16)


def experts(nc, m):
    with ExitStack() as ctx:
        ub = ctx.enter_context(sbuf(nc, "ex_u", [P, 2, KD, EG * P], F32))
        vb = ctx.enter_context(sbuf(nc, "ex_v", [P, 2, EG, D], F32))
        gb = ctx.enter_context(sbuf(nc, "ex_g", [P, 2, NU, EG, UNIT], F32))
        ab = ctx.enter_context(sbuf(nc, "ex_a", [P, 2, EG, T], F32))
        hp = ctx.enter_context(psum(nc, "ex_hp", [P, 2, 2, 512], F32))
        op = ctx.enter_context(psum(nc, "ex_op", [P, 4, 512], F32))
        names = ["u_in0", "u_in1", "v_in0", "v_in1", "g_in0", "g_in1", "h_made", "gelud", "gated", "out_made", "added"]
        NO = 2 * NT
        with stage(nc, *names) as (block, s):
            u_in, v_in, g_in = (s.u_in0, s.u_in1), (s.v_in0, s.v_in1), (s.g_in0, s.g_in1)

            @block.sync
            def _(sp):
                def load(g, j, first):
                    if not first:
                        sp.wait_ge(s.h_made, g * EG - EG)
                    sp.dma_start(ub[:, j], m.dram.peer_uT[m.l, g]).then_inc(u_in[j], 16)
                    if not first:
                        sp.wait_ge(s.gated, g * EG - EG)
                    sp.dma_start(gb[:, j].rearrange("p u e t -> p u (e t)"),
                                 m.dram.gate_dram[:, g].rearrange("u p c -> p u c")).then_inc(g_in[j], 16)
                    if not first:
                        sp.wait_ge(s.out_made, g * NO - NO)
                    sp.dma_start(vb[:, j], m.dram.peer_v[m.l, g]).then_inc(v_in[j], 16)

                load(0, 0, True)
                load(1, 1, True)
                with sp.Fori(1, NG // 2) as i:
                    for j in range(2):
                        load(i * 2 + j, j, False)

            @block.tensor
            def _(pe):
                def first_product(g, turn, j, first=False):
                    pe.wait_ge(u_in[j], turn * 16 + 16)
                    for e in range(EG):
                        if not (first and e < 2):
                            pe.wait_ge(s.gelud, g * EG + (e - 1))
                        for half in range(2):
                            for k in range(KD):
                                ins = nc.tensor.matmul(hp[:, e % 2, half, 0:HALF], ub[:, j, k, e * P:(e + 1) * P],
                                                       m.xT[:, k, half * HALF:(half + 1) * HALF],
                                                       start=(k == 0), stop=(k == KD - 1))
                        ins.then_inc(s.h_made, 1)

                def second_product(g, turn, j, first=False):
                    pe.wait_ge(s.gated, g * EG + EG)
                    pe.wait_ge(v_in[j], turn * 16 + 16)
                    for n in range(NO):
                        i, half, rows = n // 2, n % 2, ROWS[n // 2]
                        if not (first and n < 4):
                            pe.wait_ge(s.added, g * NO + (n - 3))
                        for e in range(EG):
                            ins = nc.tensor.matmul(op[0:rows, (n + 2 * j) % 4, :], ab[:, j, e, i * P:i * P + rows],
                                                   vb[:, j, e, half * 512:(half + 1) * 512],
                                                   start=(e == 0), stop=(e == EG - 1))
                        ins.then_inc(s.out_made, 1)

                first_product(0, 0, 0, True)
                first_product(1, 0, 1)
                second_product(0, 0, 0, True)
                with pe.Fori(1, NG // 2) as i:
                    first_product(i * 2, i, 0)
                    second_product(i * 2 - 1, i - 1, 1)
                    first_product(i * 2 + 1, i, 1)
                    second_product(i * 2, i, 0)
                second_product(NG - 1, NG // 2 - 1, 1)

            @block.scalar
            def _(act):
                def gelu(g, j, first):
                    if not first:
                        act.wait_ge(s.out_made, g * NO - NO)
                    for e in range(EG):
                        act.wait_ge(s.h_made, g * EG + (e + 1))
                        nc.scalar.activation(ab[:, j, e, :].rearrange("p (a t) -> p a t", a=2),
                                             hp[:, e % 2, :, 0:HALF], ACT.Gelu).then_inc(s.gelud, 1)

                gelu(0, 0, True)
                gelu(1, 1, True)
                with act.Fori(1, NG // 2) as i:
                    for j in range(2):
                        gelu(i * 2 + j, j, False)

            @block.vector
            def _(dve):
                def gate(g, turn, j):
                    dve.wait_ge(g_in[j], turn * 16 + 16)
                    for e in range(EG):
                        dve.wait_ge(s.gelud, g * EG + (e + 1))
                        a = ab[:, j, e, :].rearrange("p (u t) -> p u t", u=NU)
                        nc.vector.tensor_tensor(a, a, gb[:, j, :, e, :], ALU.mult).then_inc(s.gated, 1)

                def add(g, j):
                    for n in range(NO):
                        i, half, rows = n // 2, n % 2, ROWS[n // 2]
                        dve.wait_ge(s.out_made, g * NO + (n + 1))
                        hh = m.h[0:rows, i, half * 512:(half + 1) * 512]
                        nc.vector.tensor_tensor(hh, hh, op[0:rows, (n + 2 * j) % 4, :],
                                                ALU.add).then_inc(s.added, 1)

                gate(0, 0, 0)
                gate(1, 0, 1)
                add(0, 0)
                with dve.Fori(1, NG // 2) as i:
                    gate(i * 2, i, 0)
                    add(i * 2 - 1, 1)
                    gate(i * 2 + 1, i, 1)
                    add(i * 2, 0)
                add(NG - 1, 1)


def final_norm(nc, m):
    with ExitStack() as ctx:
        junk = ctx.enter_context(sbuf(nc, "fin_junk", [P, D], F32))
        st_ = ctx.enter_context(sbuf(nc, "fin_stat", [P, 3, NT], F32))
        y = ctx.enter_context(sbuf(nc, "fin_y", [P, NT, D], F32))
        g = ctx.enter_context(sbuf(nc, "fin_g", [P, D], F32))
        with stage(nc, "loaded", "squares", "eps_added", "rooted", "dve_step", "done", "stored") as (block, s):
            @block.sync
            def _(sp):
                sp.dma_start(g[:], m.dram.final_g).then_inc(s.loaded, 16)
                for i, r in enumerate(ROWS):
                    sp.wait_ge(s.done, i + 1)
                    sp.dma_start(m.dram.y[i * P:i * P + r, :], y[0:r, i, :]).then_inc(s.stored, 16)
                sp.wait_ge(s.stored, 16 * NT)

            @block.scalar
            def _(act):
                for i, r in enumerate(ROWS):
                    nc.scalar.activation(junk[0:r, :], m.h[0:r, i, :], ACT.Square,
                                         accum_out=st_[0:r, 0, i:i + 1]).then_inc(s.squares, 1)
                    act.wait_ge(s.squares, i + 1)
                for i, r in enumerate(ROWS):
                    act.wait_ge(s.eps_added, i + 1)
                    nc.scalar.activation(st_[0:r, 1, i:i + 1], st_[0:r, 0, i:i + 1], ACT.Sqrt).then_inc(s.rooted, 1)

            @block.vector
            def _(dve):
                st = Steps(dve, s.dve_step)
                dve.wait_ge(s.loaded, 16)
                for i, r in enumerate(ROWS):
                    dve.wait_ge(s.squares, i + 1)
                    nc.vector.tensor_scalar(st_[0:r, 0, i:i + 1], st_[0:r, 0, i:i + 1], 1.0 / D, RMS_EPS,
                                            ALU.mult, ALU.add).then_inc(s.eps_added, 1)
                for i, r in enumerate(ROWS):
                    dve.wait_ge(s.rooted, i + 1)
                    st.link(nc.vector.reciprocal(st_[0:r, 2, i:i + 1], st_[0:r, 1, i:i + 1]))
                    nc.vector.scalar_tensor_tensor(out=y[0:r, i, :], in0=m.h[0:r, i, :], scalar=st_[0:r, 2, i:i + 1],
                                                   in1=g[0:r, :], op0=ALU.mult, op1=ALU.mult).then_inc(s.done, 1)


def program(nc, d):
    m = Parts()
    m.dram = namedtuple("Dram", sorted(d))(*(d[n] for n in sorted(d)))
    with ExitStack() as ctx:
        def sb(name, shape):
            return ctx.enter_context(sbuf(nc, name, shape, F32))

        m.h = sb("h", [P, NT, D])
        m.ident, m.iota = sb("ident", [P, P]), sb("iota", [P, P])
        m.g1, m.g2 = sb("g1", [P, KD]), sb("g2", [P, KD])
        with stage(nc, "loaded", "kept") as (block, s):
            @block.sync
            def _(sp):
                loads = [(m.h[:, 0:4, :], m.dram.x_prompt), (m.h[0:TS_, 4, :], m.dram.x_sample),
                         (m.ident[:], m.dram.c_ident), (m.iota[:], m.dram.c_iota)]
                for dst, src in loads:
                    sp.dma_start(dst, src).then_inc(s.loaded, 16)
                sp.wait_ge(s.loaded, 16 * len(loads))

            @block.scalar
            def _(act):
                for l in range(LAYERS):
                    act.dma_start(m.dram.s_k[l], m.dram.cache_k_kept[l]).then_inc(s.kept, 16)
                    act.dma_start(m.dram.s_v[l], m.dram.cache_v_kept[l]).then_inc(s.kept, 16)
                act.wait_ge(s.kept, 32 * LAYERS)
        with nc.Fori(0, LAYERS) as l:
            m.l = l
            with ExitStack() as mixer:
                def mb(name, shape):
                    return mixer.enter_context(sbuf(nc, name, shape, F32))

                m.mixed = mb("mixed", [P, KD, T])
                m.pair_ones = mb("pair_ones", [P, P])
                m.chunk_reset = mb("chunk_reset", [P, T])
                mk = mb("masks", [P, 2, 5, P])
                m.own_req = mb("own_req", [TS_, REQ])
                m.masks_prompt = (mk[:, 0, 0:2], mk[:, 0, 2:4], mk[:, 0, 4])
                m.masks_sample = (mk[:, 1, 0:2], mk[:, 1, 2:4], mk[:, 1, 4])
                load_constants(nc, [(m.pair_ones[:], m.dram.c_pair_ones), (m.chunk_reset[:], m.dram.c_chunk_reset),
                                    (mk[:], m.dram.c_masks), (m.own_req[:], m.dram.c_own_req),
                                    (m.g1[:], m.dram.norm1_g[l]), (m.g2[:], m.dram.norm2_g[l])])
                with ExitStack() as pb:
                    m.proj_rw = pb.enter_context(sbuf(nc, "proj_rw", [P, NB_RW, T], F32))
                    with ExitStack() as px:
                        m.xT = px.enter_context(sbuf(nc, "xT", [P, KD, T], F32))
                        norm_transpose(nc, m, m.g1)
                        project(nc, m, m.dram.w_in[l, BR:NB_IN], NB_RW, m.proj_rw)
                        with ExitStack() as pa:
                            m.proj = pa.enter_context(sbuf(nc, "proj", [P, BR, T], F32))
                            m.v_tok = pa.enter_context(sbuf(nc, "v_tok", [P, NT, HEADS * HD], F32))
                            project(nc, m, m.dram.w_in[l, 0:BR], BR, m.proj)
                            with ExitStack() as rp:
                                m.rope_cos = rp.enter_context(sbuf(nc, "rope_cos", [P, T], F32))
                                m.rope_sin = rp.enter_context(sbuf(nc, "rope_sin", [P, T], F32))
                                m.rope_swap = rp.enter_context(sbuf(nc, "rope_swap", [P, P], F32))
                                m.pool_inv = rp.enter_context(sbuf(nc, "pool_inv", [P, 2, T], F32))
                                load_constants(nc, [(m.rope_cos[:], m.dram.c_cos), (m.rope_sin[:], m.dram.c_sin),
                                                    (m.rope_swap[:], m.dram.c_swap), (m.pool_inv[:], m.dram.c_pool_inv)])
                                rotate(nc, m)
                                pool(nc, m)
                            attend_prompt(nc, m)
                            attend_sample(nc, m)
                    rwkv(nc, m)
                mix_out(nc, m)
            with ExitStack() as peer:
                m.xT = peer.enter_context(sbuf(nc, "xT", [P, KD, T], F32))
                norm_transpose(nc, m, m.g2)
                with ExitStack() as pi:
                    i1T, i2T, gT = (pi.enter_context(sbuf(nc, n, [P, TPAD], F32)) for n in ("i1T", "i2T", "gT"))
                    with ExitStack() as pq:
                        qT = pq.enter_context(sbuf(nc, "qT", [P, NB_Q, TPAD], F32))
                        keys = pq.enter_context(sbuf(nc, "keys", [P, NB_Q, NKEY], F32))
                        load_constants(nc, [(keys[:], m.dram.peer_keys[l])])
                        with stage(nc) as (block, s):
                            @block.vector
                            def _(dve):
                                nc.vector.memset(qT[:, :, T:TPAD], 0.0)
                        project(nc, m, m.dram.peer_wq[l], NB_Q, qT)
                        route(nc, m, qT, keys, i1T, i2T, gT)
                    gates(nc, m, i1T, i2T, gT)
                experts(nc, m)
        final_norm(nc, m)


def _constants():
    c = {}
    c["c_ident"] = np.eye(P, dtype=np.float32)
    c["c_iota"] = np.tile(np.arange(P, dtype=np.float32), (P, 1))
    c["c_pair_ones"] = np.kron(np.eye(2, dtype=np.float32), np.ones((HD, HD), np.float32))
    reset = np.ones((P, T), np.float32)
    reset[:, 0:TP_:CH] = 0
    reset[:, TP_::STEPS] = 0
    c["c_chunk_reset"] = reset
    masks = np.zeros((P, 2, 5, P), np.float32)
    s_, t_ = np.arange(P)[:, None], np.arange(P)[None, :]
    for n, w in enumerate((CH, STEPS)):
        same = s_ // w == t_ // w
        masks[:, n, 0] = same & (s_ < t_)
        masks[:, n, 1] = same & (s_ <= t_)
        masks[:, n, 2] = -masks[:, n, 0]
        masks[:, n, 3] = -masks[:, n, 1]
        masks[:, n, 4] = -(same & (t_ < s_)).astype(np.float32)
    c["c_masks"] = masks
    c["c_own_req"] = (np.arange(TS_)[:, None] // STEPS == np.arange(REQ)[None]).astype(np.float32)
    pos = np.concatenate([np.arange(TP_), PAST + np.tile(np.arange(STEPS), REQ)]).astype(np.float32)
    half = HD // 8
    inv = (np.float32(500000.0) ** (-np.arange(half, dtype=np.float32) * np.float32(2.0) / np.float32(2 * half)))
    ang = (pos[:, None] * inv.astype(np.float32)[None]).astype(np.float32)
    cos, sin, swap = np.ones((P, T), np.float32), np.zeros((P, T), np.float32), np.zeros((P, P), np.float32)
    for o in (0, HD):
        for j in range(half):
            cos[o + j] = cos[o + half + j] = np.cos(ang[:, j])
            sin[o + j] = sin[o + half + j] = np.sin(ang[:, j])
            swap[o + half + j, o + j] = -1
            swap[o + j, o + half + j] = 1
    c["c_cos"], c["c_sin"], c["c_swap"] = cos, sin, swap
    pinv = np.zeros((P, 2, T), np.float32)
    for a in range(2):
        for o in range(2):
            win = 2 << (2 * a + o)
            pinv[64 * o:64 * o + 64, a, 0:TP_] = np.float32(1) / np.minimum(win, np.arange(TP_) + 1).astype(np.float32)
            pinv[64 * o:64 * o + 64, a, TP_:] = np.float32(1) / np.float32(win)
    c["c_pool_inv"] = pinv

    def count(rel):
        n = sum(((rel >= 0) & (rel <= w) & (rel % d == 0)).astype(int) for w, d in ((128, 1), (512, 4), (2048, 16)))
        return np.where(n > 0, np.log(np.maximum(n, 1)), NEG).astype(np.float32)

    c["count_prompt"] = np.ascontiguousarray(
        count(np.arange(TP_)[:, None] - np.arange(TP_)[None]).reshape(4, P, TP_).transpose(1, 0, 2))
    q = np.tile(np.arange(STEPS), HEADS)
    c["count_past"] = count(PAST + q[:, None] - np.arange(PAST)[None])
    new = count(q[:, None] - np.tile(np.arange(STEPS), REQ)[None])
    own = np.arange(TS_)[None, None] // STEPS == np.arange(REQ)[None, :, None]
    c["count_new"] = np.ascontiguousarray(np.where(own, new[:, None], np.float32(NEG)).astype(np.float32))
    return c


def _layouts(i):
    i = {k: np.asarray(v) for k, v in i.items()}
    L = LAYERS
    cc = np.ascontiguousarray
    fm = lambda a: cc(a.reshape(L, -1, P).transpose(0, 2, 1))
    a = {}
    a["x_prompt"] = cc(i["x_prompt"].reshape(4, P, D).transpose(1, 0, 2))
    a["x_sample"] = i["x_sample"].reshape(TS_, D)
    blocks = lambda w: cc(w.reshape(L, KD, P, -1, P).transpose(0, 3, 2, 1, 4))
    a["w_in"], a["peer_wq"] = blocks(i["w_in"]), blocks(i["peer_wq"])
    a["w_out"] = cc(i["w_out"].reshape(L, KD, P, D).transpose(0, 2, 1, 3))
    for n in ("norm1_g", "norm2_g"):
        a[n] = fm(i[n])
    a["pool_scale"] = fm(i["pool_scale"])
    a["final_g"] = cc(np.broadcast_to(i["final_g"], (P, D)))
    a["state_pool"] = cc(i["state_pool"].transpose(0, 3, 1, 2).reshape(L, 2, P, REQ, POOL_BUF)
                         .transpose(0, 2, 1, 3, 4).reshape(L, P, 2 * REQ, POOL_BUF))
    a["pool_w"] = i["pool_w"]
    a["cache_kT"] = cc(i["cache_k"].reshape(L, REQ, PAST, PAIRS, P).transpose(0, 1, 4, 3, 2))
    a["cache_v"] = cc(i["cache_v"].reshape(L, REQ, PAST // P, P, HEADS * HD).transpose(0, 1, 3, 2, 4))
    for n in ("k", "v"):
        a[f"cache_{n}_kept"] = cc(i[f"cache_{n}"][:, :, STEPS:].reshape(L, P, -1))
    a["state_shift"] = cc(i["state_shift"].reshape(L, REQ, NB_RW, P).transpose(0, 3, 2, 1))
    a["state_wkv"] = cc(i["state_wkv"].reshape(L, REQ, PAIRS, 2, HD, HD).transpose(0, 3, 5, 2, 1, 4)
                        .reshape(L, P, PAIRS, REQ, HD))
    a["rwkv_mu"] = fm(i["rwkv_mu"])
    vecs = [i["rwkv_" + n].reshape(L, HEADS * HD) for n in ("w0", "a0", "k_k", "k_a", "r_k", "ln_w", "ln_b")]
    a["rwkv_vec"] = cc(np.stack([fm(v) for v in vecs], 2))
    a["rwkv_wa"] = np.concatenate([i["rwkv_w_up"], i["rwkv_a_up"]], 1)
    a["rwkv_g"] = i["rwkv_g_up"]
    a["peer_keys"] = cc(i["peer_subkeys"].reshape(L, NB_Q, NKEY, P).transpose(0, 3, 1, 2))
    a["peer_uT"] = cc(i["peer_u"].reshape(L, NG, EG * P, KD, P).transpose(0, 1, 4, 3, 2))
    a["peer_v"] = cc(i["peer_v"].reshape(L, NG, EG, P, D).transpose(0, 1, 3, 2, 4))
    return a


_OUTS = {
    "y": (T, D), "p_pool": (LAYERS, P, 2, POOL_BUF), "s_pool": (LAYERS, P, 2 * REQ, POOL_BUF),
    "out_k": (LAYERS, P, PAIRS, T), "out_v": (LAYERS, P, PAIRS, T),
    "p_shift": (LAYERS, P, NB_RW, 1), "s_shift": (LAYERS, P, NB_RW, REQ),
    "p_wkv": (LAYERS, P, PAIRS, HD), "s_wkv": (LAYERS, P, PAIRS, REQ, HD),
    "s_k": (LAYERS, P, REQ * (PAST - STEPS) * HEADS * HD // P), "s_v": (LAYERS, P, REQ * (PAST - STEPS) * HEADS * HD // P),
}


def _build(nc, arrays):
    d = {n: nc.dram_tensor("in_" + n, a.shape, F32, kind="ExternalInput").ap() for n, a in arrays.items()}
    for n, shape in _OUTS.items():
        d[n] = nc.dram_tensor("out_" + n, shape, F32, kind="ExternalOutput").ap()
    d["gate_dram"] = nc.dram_tensor("gate_matrix", (NU, NG, P, EG * UNIT), F32, kind="Internal").ap()
    program(nc, d)


def _returned(o):
    L = LAYERS
    tok = lambda a: a.transpose(0, 3, 2, 1).reshape(L, T, HEADS, HD)
    k, v = tok(o["out_k"]), tok(o["out_v"])
    kept = lambda a: a.reshape(L, REQ, PAST - STEPS, HEADS, HD)
    new = lambda a: a[:, TP_:].reshape(L, REQ, STEPS, HEADS, HD)
    pool_ = lambda a, b: a.reshape(L, P, 2, b, POOL_BUF).transpose(0, 3, 4, 2, 1).reshape(L, b, POOL_BUF, 2 * P)
    shift = lambda a: a.transpose(0, 3, 2, 1).reshape(L, a.shape[3], NB_RW * P)
    wkv = lambda a, b: (a.reshape(L, 2, HD, PAIRS, b, HD).transpose(0, 4, 3, 1, 5, 2)
                        .reshape(L, b, HEADS, HD, HD))
    out = (o["y"][:TP_].reshape(1, TP_, D), o["y"][TP_:].reshape(REQ, STEPS, D),
           pool_(o["p_pool"], 1), k[:, None, :TP_], v[:, None, :TP_], shift(o["p_shift"]), wkv(o["p_wkv"], 1),
           pool_(o["s_pool"], REQ), np.concatenate([kept(o["s_k"]), new(k)], 2),
           np.concatenate([kept(o["s_v"]), new(v)], 2), shift(o["s_shift"]), wkv(o["s_wkv"], REQ))
    return tuple(np.ascontiguousarray(x) for x in out)


def kernel(**inputs):
    import concourse.bacc as _bacc
    from concourse.bass_utils import run_bass_kernel_spmd as _run

    nc = _bacc.Bacc("TRN2", target_bir_lowering=False, num_devices=1)
    arrays = {**_layouts(inputs), **_constants()}
    _build(nc, arrays)
    r = _run(nc, [{"in_" + n: a for n, a in arrays.items()}], core_ids=[0])
    return _returned({n: r.results[0]["out_" + n] for n in _OUTS})
```

```python
from contextlib import ExitStack, contextmanager
from collections import namedtuple

import numpy as np
import concourse.bass as bass
from concourse import mybir

F32 = mybir.dt.float32
F32R = mybir.dt.float32r
U32 = mybir.dt.uint32
ALU = mybir.AluOpType
ACT = mybir.ActivationFunctionType
X = mybir.AxisListType.X

P = 128
LAYERS = 2
D = 1024
KD = D // P
TP_, TS_ = 512, 64
T = TP_ + TS_
HALF = T // 2
NT = 5
ROWS = [P, P, P, P, TS_]
REQ, STEPS = 8, 8
PAST = 1024
HD = 64
HEADS = 6
PAIRS = HEADS // 2
RMS_EPS = 1e-6
GN_EPS = HD * 1e-5
POOL_BUF = 15
NEG = -1e30
BQ, BK, BV, BR = 2, 5, 8, 11
NB_IN = 22
NB_RW = NB_IN - BR
CH = 32
NCH = TP_ // CH
DECAY = float(np.exp(-0.5))
PH, TOPK = 8, 16
NKEY = 128
NB_Q = 16
TPAD = NT * P
EG = 2
NG = NKEY // EG
UNIT = 64
NU = T // UNIT


def _count():
    n = 0
    while True:
        yield n
        n += 1


_serial = _count()


class Parts:
    pass


def sbuf(nc, name, shape, dt):
    return nc.sbuf_tensor(f"{name}_{next(_serial)}", shape, dt)


def psum(nc, name, shape, dt):
    return nc.psum_tensor(f"{name}_{next(_serial)}", shape, dt)


class Steps:

    def __init__(self, eng, sem):
        self.eng, self.sem, self.n = eng, sem, 0

    def link(self, ins):
        ins.then_inc(self.sem, 1)
        self.n += 1
        self.eng.wait_ge(self.sem, self.n)


@contextmanager
def stage(nc, *names):
    with ExitStack() as ctx:
        sems = namedtuple("Semaphores", names)(*(ctx.enter_context(nc.semaphore(f"{n}_{next(_serial)}")) for n in names))
        with nc.Block() as block:
            yield block, sems
        with nc.Block() as tidy:
            @tidy.sync
            def _(sp):
                for sem in sems:
                    sp.sem_clear(sem)


def load_constants(nc, c):
    with stage(nc, "loaded") as (block, s):
        @block.sync
        def _(sp):
            for n, (dst, src) in enumerate(c):
                sp.dma_start(dst, src).then_inc(s.loaded, 16)
            sp.wait_ge(s.loaded, 16 * len(c))


def norm_transpose(nc, m, gain):
    with ExitStack() as ctx:
        junk = ctx.enter_context(sbuf(nc, "norm_junk", [P, D], F32))
        ssq = ctx.enter_context(sbuf(nc, "norm_ssq", [P, NT], F32))
        std = ctx.enter_context(sbuf(nc, "norm_std", [P, NT], F32))
        inv = ctx.enter_context(sbuf(nc, "norm_inv", [P, NT], F32))
        xn = ctx.enter_context(sbuf(nc, "norm_xn", [P, NT, D], F32))
        xg = ctx.enter_context(sbuf(nc, "norm_xg", [P, 2, 4, P], F32))
        ps = ctx.enter_context(psum(nc, "norm_ps", [P, 4, 4, P], F32))
        with stage(nc, "squares", "eps_added", "rooted", "dve_step", "scaled", "turned", "gained", "hi",
                   "lo") as (block, s):
            @block.scalar
            def _(act):
                for i, r in enumerate(ROWS):
                    ins = nc.scalar.activation(junk[0:r, :], m.h[0:r, i, :], ACT.Square,
                                               accum_out=ssq[0:r, i:i + 1])
                    ins.then_inc(s.squares, 1)
                    act.wait_ge(s.squares, i + 1)
                for i, r in enumerate(ROWS):
                    act.wait_ge(s.eps_added, i + 1)
                    nc.scalar.activation(std[0:r, i:i + 1], ssq[0:r, i:i + 1], ACT.Sqrt).then_inc(s.rooted, 1)
                for n in range(2 * NT):
                    i, r, k = n // 2, ROWS[n // 2], 4 * (n % 2)
                    act.wait_ge(s.gained, n + 1)
                    nc.scalar.activation(m.x_hi[:, k:k + 4, i * P:i * P + r], xg[:, n % 2, :, 0:r],
                                         ACT.Copy).then_inc(s.hi, 1)

            @block.vector
            def _(dve):
                st = Steps(dve, s.dve_step)
                for i, r in enumerate(ROWS):
                    dve.wait_ge(s.squares, i + 1)
                    nc.vector.tensor_scalar(ssq[0:r, i:i + 1], ssq[0:r, i:i + 1], 1.0 / D, RMS_EPS,
                                            ALU.mult, ALU.add).then_inc(s.eps_added, 1)
                for i, r in enumerate(ROWS):
                    dve.wait_ge(s.rooted, i + 1)
                    st.link(nc.vector.reciprocal(inv[0:r, i:i + 1], std[0:r, i:i + 1]))
                    nc.vector.tensor_scalar(xn[0:r, i, :], m.h[0:r, i, :], inv[0:r, i:i + 1], None,
                                            ALU.mult).then_inc(s.scaled, 1)

                def low(n):
                    i, r, k = n // 2, ROWS[n // 2], 4 * (n % 2)
                    dve.wait_ge(s.hi, n + 1)
                    nc.vector.tensor_tensor(m.x_lo[:, k:k + 4, i * P:i * P + r], xg[:, n % 2, :, 0:r],
                                            m.x_hi[:, k:k + 4, i * P:i * P + r].bitcast(F32), ALU.subtract
                                            ).then_inc(s.lo, 1)

                for n in range(2 * NT):
                    i, r, k = n // 2, ROWS[n // 2], 4 * (n % 2)
                    dve.wait_ge(s.turned, n + 1)
                    if n >= 2:
                        dve.wait_ge(s.lo, n - 1)
                    nc.vector.tensor_tensor(xg[:, n % 2, :, 0:r], ps[:, n % 4, :, 0:r],
                                            gain[:, k:k + 4].unsqueeze(2).to_broadcast([P, 4, r]),
                                            ALU.mult).then_inc(s.gained, 1)
                    if n:
                        low(n - 1)
                low(2 * NT - 1)

            @block.tensor
            def _(pe):
                for n in range(2 * NT):
                    i, r = n // 2, ROWS[n // 2]
                    pe.wait_ge(s.scaled, i + 1)
                    if n >= 4:
                        pe.wait_ge(s.gained, n - 3)
                    for q in range(4):
                        k = 4 * (n % 2) + q
                        ins = nc.tensor.transpose(ps[:, n % 4, q, 0:r], xn[0:r, i, k * P:(k + 1) * P],
                                                  m.ident[0:r, 0:r])
                    ins.then_inc(s.turned, 1)


def three_passes(nc, out, w_hi, w_lo, x_hi, x_lo, first, last):
    nc.tensor.matmul(out, w_lo, x_hi, start=first, stop=False)
    nc.tensor.matmul(out, w_hi, x_lo, start=False, stop=False)
    return nc.tensor.matmul(out, w_hi, x_hi, start=False, stop=last)


def project(nc, m, w, blocks, out):
    odd = blocks % 2
    with ExitStack() as ctx:
        wb = ctx.enter_context(sbuf(nc, "proj_w", [P, 2, KD, P], F32))
        w_hi = ctx.enter_context(sbuf(nc, "proj_w_hi", [P, 2, KD, P], F32R))
        w_lo = ctx.enter_context(sbuf(nc, "proj_w_lo", [P, 2, KD, P], F32R))
        ps = ctx.enter_context(psum(nc, "proj_ps", [P, 4, 512], F32))
        with stage(nc, "even_in", "odd_in", "hi", "lo", "made", "copied_lo", "copied_hi") as (block, s):
            landed = (s.even_in, s.odd_in)

            @block.sync
            def _(sp):
                for j in range(2):
                    sp.dma_start(wb[:, j], w[j]).then_inc(landed[j], 16)
                def refill(i, j):
                    sp.wait_ge(s.lo, i * 2 + (j + 1))
                    sp.dma_start(wb[:, j], w[i * 2 + (2 + j)]).then_inc(landed[j], 16)

                with sp.Fori(0, blocks // 2 - 1) as i:
                    for j in range(2):
                        refill(i, j)
                if odd:
                    refill(blocks // 2 - 1, 0)

            @block.tensor
            def _(pe):
                def body(i, first, js=(0, 1)):
                    for j in js:
                        pe.wait_ge(s.lo, i * 2 + (j + 1))
                        for half in range(2):
                            t = slice(half * HALF, (half + 1) * HALF)
                            if not first:
                                pe.wait_ge((s.copied_lo, s.copied_hi)[half], i * 2 + (j - 1))
                            for k in range(KD):
                                ins = three_passes(nc, ps[:, 2 * j + half, 0:HALF], w_hi[:, j, k, :], w_lo[:, j, k, :],
                                                   m.x_hi[:, k, t], m.x_lo[:, k, t], k == 0, k == KD - 1)
                            ins.then_inc(s.made, 1)

                body(0, True)
                with pe.Fori(1, blocks // 2) as i:
                    body(i, False)
                if odd:
                    body(blocks // 2, False, (0,))

            @block.scalar
            def _(act):
                def split(i, j, first=False):
                    act.wait_ge(landed[j], i * 16 + 16)
                    if not first:
                        act.wait_ge(s.made, i * 4 + (2 * j - 2))
                    nc.scalar.activation(w_hi[:, j], wb[:, j], ACT.Copy).then_inc(s.hi, 1)

                def copy(i, j):
                    act.wait_ge(s.made, i * 4 + (2 * j + 1))
                    nc.scalar.activation(out[:, bass.ds(i * 2 + j, 1), 0:HALF],
                                         ps[:, 2 * j:2 * j + 1, 0:HALF], ACT.Copy).then_inc(s.copied_lo, 1)

                split(0, 0, True)
                split(0, 1, True)
                with act.Fori(0, blocks // 2 - 1) as i:
                    for j in range(2):
                        copy(i, j)
                        split(i + 1, j)
                copy(blocks // 2 - 1, 0)
                if odd:
                    split(blocks // 2, 0)
                copy(blocks // 2 - 1, 1)
                if odd:
                    copy(blocks // 2, 0)

            @block.vector
            def _(dve):
                def split(i, j):
                    dve.wait_ge(s.hi, i * 2 + (j + 1))
                    nc.vector.tensor_tensor(w_lo[:, j], wb[:, j], w_hi[:, j].bitcast(F32),
                                            ALU.subtract).then_inc(s.lo, 1)

                def copy(i, j):
                    dve.wait_ge(s.made, i * 4 + (2 * j + 2))
                    nc.vector.tensor_copy(out[:, bass.ds(i * 2 + j, 1), HALF:T],
                                          ps[:, 2 * j + 1:2 * j + 2, 0:HALF]).then_inc(s.copied_hi, 1)

                split(0, 0)
                split(0, 1)
                with dve.Fori(0, blocks // 2 - 1) as i:
                    for j in range(2):
                        copy(i, j)
                        split(i + 1, j)
                copy(blocks // 2 - 1, 0)
                if odd:
                    split(blocks // 2, 0)
                copy(blocks // 2 - 1, 1)
                if odd:
                    copy(blocks // 2, 0)


def rotate(nc, m):
    with ExitStack() as ctx:
        tmp = ctx.enter_context(sbuf(nc, "rope_tmp", [P, T], F32))
        ps = ctx.enter_context(psum(nc, "rope_ps", [P, 4, 512], F32))
        vps = ctx.enter_context(psum(nc, "rope_vps", [P, 2, 512], F32))
        with stage(nc, "swapped", "mixed", "dve_step", "v_turned", "v_copied", "stored") as (block, s):
            @block.tensor
            def _(pe):
                for b in range(6):
                    for half in range(2):
                        n = 2 * b + half
                        if n >= 4:
                            pe.wait_ge(s.mixed, n // 2 - 1)
                        nc.tensor.matmul(ps[:, n % 4, 0:HALF], m.rope_swap[:],
                                         m.proj[:, BQ + b, half * HALF:(half + 1) * HALF],
                                         start=True, stop=True).then_inc(s.swapped, 1)
                for i, r in enumerate(ROWS):
                    if i >= 2:
                        pe.wait_ge(s.v_copied, i - 1)
                    for c in range(PAIRS):
                        ins = nc.tensor.transpose(vps[0:r, i % 2, c * P:(c + 1) * P],
                                                  m.proj[:, BV + c, i * P:i * P + r], m.ident[:])
                    ins.then_inc(s.v_turned, 1)

            @block.vector
            def _(dve):
                st = Steps(dve, s.dve_step)
                for b in range(6):
                    dve.wait_ge(s.swapped, 2 * b + 2)
                    src = ps[:, 2 * (b % 2):2 * (b % 2) + 2, 0:HALF]
                    st.link(nc.vector.tensor_tensor(tmp[:].rearrange("p (a t) -> p a t", a=2), src,
                                                    m.rope_sin[:].rearrange("p (a t) -> p a t", a=2), ALU.mult))
                    st.link(nc.vector.tensor_tensor(m.proj[:, BQ + b, :], m.proj[:, BQ + b, :], m.rope_cos[:],
                                                    ALU.mult))
                    nc.vector.tensor_tensor(m.proj[:, BQ + b, :], m.proj[:, BQ + b, :], tmp[:],
                                            ALU.add).then_inc(s.mixed, 1)
                    dve.wait_ge(s.mixed, b + 1)

            @block.scalar
            def _(act):
                for i, r in enumerate(ROWS):
                    act.wait_ge(s.v_turned, i + 1)
                    nc.scalar.activation(m.v_tok[0:r, i, :], vps[0:r, i % 2, 0:PAIRS * P], ACT.Copy).then_inc(s.v_copied, 1)

            @block.sync
            def _(sp):
                sp.wait_ge(s.mixed, 6)
                sp.dma_start(m.dram.out_k[m.l], m.proj[:, BK:BK + PAIRS, :]).then_inc(s.stored, 16)
                sp.dma_start(m.dram.out_v[m.l], m.proj[:, BV:BV + PAIRS, :]).then_inc(s.stored, 16)
                sp.wait_ge(s.stored, 32)


def pool(nc, m):
    WP = POOL_BUF + TP_
    WS = POOL_BUF + STEPS
    with ExitStack() as ctx:
        xp = ctx.enter_context(sbuf(nc, "pool_xp", [P, 2, 1, WP], F32))
        xs = ctx.enter_context(sbuf(nc, "pool_xs", [P, 2, REQ, WS], F32))
        sp_ = ctx.enter_context(sbuf(nc, "pool_sp", [P, 2, 1, WP], F32))
        ss_ = ctx.enter_context(sbuf(nc, "pool_ss", [P, 2, REQ, WS], F32))
        tp_ = ctx.enter_context(sbuf(nc, "pool_tp", [P, 1, WP], F32))
        ts_ = ctx.enter_context(sbuf(nc, "pool_ts", [P, REQ, WS], F32))
        diff = ctx.enter_context(sbuf(nc, "pool_diff", [P, 2, T], F32))
        w = ctx.enter_context(sbuf(nc, "pool_w", [P, 2, P], F32))
        scale = ctx.enter_context(sbuf(nc, "pool_scale", [P, 2], F32))
        ps = ctx.enter_context(psum(nc, "pool_ps", [P, 4, 512], F32))
        with stage(nc, "zeroed", "loaded", "dve_step", "differed", "mapped", "filled", "scaled",
                   "stored") as (block, s):
            @block.sync
            def _(sp):
                sp.dma_start(xs[:, :, :, 0:POOL_BUF].rearrange("p a b r -> p (a b) r"),
                             m.dram.state_pool[m.l]).then_inc(s.loaded, 16)
                sp.dma_start(scale[:], m.dram.pool_scale[m.l]).then_inc(s.loaded, 16)
                sp.wait_ge(s.zeroed, 1)
                for a in range(2):
                    for o in range(2):
                        sp.dma_start(w[64 * o:64 * o + 64, a, 64 * o:64 * o + 64],
                                     m.dram.pool_w[m.l, 2 * a + o]).then_inc(s.loaded, 16)
                sp.dma_start(m.dram.p_pool[m.l], m.proj[:, 0:2, TP_ - POOL_BUF:TP_]).then_inc(s.stored, 16)
                sp.wait_ge(s.filled, 1)
                sp.dma_start(m.dram.s_pool[m.l], xs[:, :, :, STEPS:WS].rearrange("p a b r -> p (a b) r")
                             ).then_inc(s.stored, 16)
                sp.wait_ge(s.stored, 32)

            @block.vector
            def _(dve):
                st = Steps(dve, s.dve_step)
                nc.vector.memset(w[:], 0.0).then_inc(s.zeroed, 1)
                st.link(nc.vector.memset(xp[:, :, :, 0:POOL_BUF], 0.0))
                dve.wait_ge(s.loaded, 96)
                st.link(nc.vector.tensor_copy(xp[:, :, 0, POOL_BUF:WP], m.proj[:, 0:2, 0:TP_]))
                for a in range(2):
                    ins = nc.vector.tensor_copy(xs[:, a, :, POOL_BUF:WS],
                                                m.proj[:, a, TP_:T].rearrange("p (b t) -> p b t", b=REQ))
                    st.link(ins)
                nc.vector.tensor_copy(ts_[:, 0, 0:1], xs[:, 0, 0, 0:1]).then_inc(s.filled, 1)
                dve.wait_ge(s.filled, 1)
                for x, sm, tm, wd in ((xp, sp_, tp_, WP), (xs, ss_, ts_, WS)):
                    for a in range(2):
                        for o in range(2):
                            q = slice(64 * o, 64 * o + 64)
                            win = 2 << (2 * a + o)
                            st.link(nc.vector.tensor_tensor(sm[q, a, :, 1:wd], x[q, a, :, 1:wd],
                                                            x[q, a, :, 0:wd - 1], ALU.add))
                            done, src, dst = 2, sm[:, a], tm[:]
                            while done < win:
                                lo = 2 * done - 1
                                st.link(nc.vector.tensor_tensor(dst[q, :, lo:wd], src[q, :, lo:wd],
                                                                src[q, :, lo - done:wd - done], ALU.add))
                                src, dst = dst, src
                                done *= 2
                            out = (diff[q, a, 0:TP_].unsqueeze(1) if x is xp else
                                   diff[q, a, TP_:T].rearrange("p (b t) -> p b t", b=REQ))
                            cnt = (m.pool_inv[q, a, 0:TP_].unsqueeze(1) if x is xp else
                                   m.pool_inv[q, a, TP_:T].rearrange("p (b t) -> p b t", b=REQ))
                            st.link(nc.vector.tensor_tensor(out, src[q, :, POOL_BUF:wd], cnt, ALU.mult))
                nc.vector.tensor_tensor(diff[:], diff[:], m.proj[:, 0:2, :], ALU.subtract).then_inc(s.differed, 1)
                for n in range(4):
                    a, half = n // 2, n % 2
                    dve.wait_ge(s.mapped, n + 1)
                    nc.vector.tensor_scalar(m.mixed[:, a, half * HALF:(half + 1) * HALF], ps[:, n, 0:HALF],
                                            scale[:, a:a + 1], None, ALU.mult).then_inc(s.scaled, 1)

            @block.tensor
            def _(pe):
                pe.wait_ge(s.differed, 1)
                for n in range(4):
                    a, half = n // 2, n % 2
                    nc.tensor.matmul(ps[:, n, 0:HALF], w[:, a, :], diff[:, a, half * HALF:(half + 1) * HALF],
                                     start=True, stop=True).then_inc(s.mapped, 1)


def attend_prompt(nc, m):
    units = [(qt, h) for qt in range(4) for h in range(HEADS)]
    with ExitStack() as ctx:
        sm = ctx.enter_context(sbuf(nc, "att_s", [P, 2, TP_], F32))
        pr = ctx.enter_context(sbuf(nc, "att_p", [P, 2, TP_], F32))
        pt = ctx.enter_context(sbuf(nc, "att_pt", [P, 2, 4, P], F32))
        st_ = ctx.enter_context(sbuf(nc, "att_stat", [P, 2, 4], F32))
        lc = ctx.enter_context(sbuf(nc, "att_lc", [P, 4, TP_], F32))
        s_ps = ctx.enter_context(psum(nc, "att_sps", [P, 2, TP_], F32))
        t_ps = ctx.enter_context(psum(nc, "att_tps", [P, 2, 4, P], F32))
        o_ps = ctx.enter_context(psum(nc, "att_ops", [P, 2, 512], F32))
        with stage(nc, "counts_in", "scored", "maxed", "expd", "normed", "turned", "turned_in", "valued",
                   "out_in", "dve_step") as (block, s):
            @block.sync
            def _(sp):
                sp.dma_start(lc[:], m.dram.count_prompt).then_inc(s.counts_in, 16)

            @block.tensor
            def _(pe):
                def scores(u):
                    qt, h = units[u]
                    c, o = h // 2, 64 * (h % 2)
                    n = (qt + 1) * P
                    if u >= 2:
                        pe.wait_ge(s.maxed, u - 1)
                    nc.tensor.matmul(s_ps[:, u % 2, 0:n], m.proj[o:o + 64, BQ + c, qt * P:(qt + 1) * P],
                                     m.proj[o:o + 64, BK + c, 0:n], start=True, stop=True).then_inc(s.scored, 1)

                scores(0)
                scores(1)
                for u, (qt, h) in enumerate(units):
                    c, o = h // 2, 64 * (h % 2)
                    pe.wait_ge(s.normed, u + 1)
                    if u >= 2:
                        pe.wait_ge(s.turned_in, u - 1)
                    for b in range(qt + 1):
                        ins = nc.tensor.transpose(t_ps[:, u % 2, b, :], pr[:, u % 2, b * P:(b + 1) * P], m.ident[:])
                    ins.then_inc(s.turned, 1)
                    if u + 2 < len(units):
                        scores(u + 2)
                    pe.wait_ge(s.turned_in, u + 1)
                    if u >= 2:
                        pe.wait_ge(s.out_in, u - 1)
                    for b in range(qt + 1):
                        ins = nc.tensor.matmul(o_ps[o:o + 64, u % 2, 0:P], m.v_tok[:, b, h * HD:(h + 1) * HD],
                                               pt[:, u % 2, b, :], start=(b == 0), stop=(b == qt))
                    ins.then_inc(s.valued, 1)

            @block.scalar
            def _(act):
                def exps(u):
                    n = (units[u][0] + 1) * P
                    act.wait_ge(s.maxed, u + 1)
                    if u >= 2:
                        act.wait_ge(s.turned, u - 1)
                    nc.scalar.activation(pr[:, u % 2, 0:n], sm[:, u % 2, 0:n], ACT.Exp, bias=st_[:, u % 2, 0:1],
                                         accum_out=st_[:, u % 2, 1:2]).then_inc(s.expd, 1)

                exps(0)
                for u, (qt, h) in enumerate(units):
                    if u + 1 < len(units):
                        exps(u + 1)
                    act.wait_ge(s.turned, u + 1)
                    if u >= 2:
                        act.wait_ge(s.valued, u - 1)
                    nc.scalar.activation(pt[:, u % 2, 0:qt + 1, :], t_ps[:, u % 2, 0:qt + 1, :],
                                         ACT.Copy).then_inc(s.turned_in, 1)

            @block.vector
            def _(dve):
                st = Steps(dve, s.dve_step)
                dve.wait_ge(s.counts_in, 16)

                def mask_max(u):
                    qt = units[u][0]
                    n = (qt + 1) * P
                    dve.wait_ge(s.scored, u + 1)
                    if u >= 2:
                        dve.wait_ge(s.expd, u - 1)
                    st.link(nc.vector.scalar_tensor_tensor(out=sm[:, u % 2, 0:n], in0=s_ps[:, u % 2, 0:n],
                                                           scalar=HD ** -0.5, in1=lc[:, qt, 0:n],
                                                           op0=ALU.mult, op1=ALU.add))
                    nc.vector.tensor_reduce(st_[:, u % 2, 0:1], sm[:, u % 2, 0:n], X, ALU.max,
                                            negate=True).then_inc(s.maxed, 1)

                def collect(u):
                    qt, h = units[u]
                    c, o = h // 2, 64 * (h % 2)
                    dve.wait_ge(s.valued, u + 1)
                    nc.vector.tensor_copy(m.mixed[o:o + 64, 2 + c, qt * P:(qt + 1) * P],
                                          o_ps[o:o + 64, u % 2, 0:P]).then_inc(s.out_in, 1)

                mask_max(0)
                mask_max(1)
                for u, (qt, h) in enumerate(units):
                    n = (qt + 1) * P
                    dve.wait_ge(s.expd, u + 1)
                    st.link(nc.vector.reciprocal(st_[:, u % 2, 2:3], st_[:, u % 2, 1:2]))
                    nc.vector.tensor_scalar(pr[:, u % 2, 0:n], pr[:, u % 2, 0:n], st_[:, u % 2, 2:3], None,
                                            ALU.mult).then_inc(s.normed, 1)
                    if u + 2 < len(units):
                        mask_max(u + 2)
                    if u >= 1:
                        collect(u - 1)
                collect(len(units) - 1)


def attend_sample(nc, m):
    R = HEADS * STEPS
    NKEYS = PAST + TS_
    NKB = PAST // P
    with ExitStack() as ctx:
        kc = ctx.enter_context(sbuf(nc, "dec_k", [P, 2, PAIRS, PAST], F32))
        vc = ctx.enter_context(sbuf(nc, "dec_v", [P, 2, NKB, HEADS * HD], F32))
        lcp = ctx.enter_context(sbuf(nc, "dec_lcp", [R, PAST], F32))
        lcn = ctx.enter_context(sbuf(nc, "dec_lcn", [R, REQ, TS_], F32))
        qbd = ctx.enter_context(sbuf(nc, "dec_q", [P, REQ, PAIRS, R], F32))
        sm = ctx.enter_context(sbuf(nc, "dec_s", [R, 2, NKEYS], F32))
        pr = ctx.enter_context(sbuf(nc, "dec_p", [R, 2, NKEYS], F32))
        pt = ctx.enter_context(sbuf(nc, "dec_pt", [P, NKB + 1, R], F32))
        st_ = ctx.enter_context(sbuf(nc, "dec_stat", [R, 2, 4], F32))
        s_ps = ctx.enter_context(psum(nc, "dec_sps", [R, 2, 3, 512], F32))
        t_bank = ctx.enter_context(psum(nc, "dec_tps", [P, 512], F32))
        t_ps = t_bank[:, 0:(NKB + 1) * R].rearrange("p (n r) -> p n r", r=R)
        o_ps = ctx.enter_context(psum(nc, "dec_ops", [P, PAIRS, 16], F32))
        with stage(nc, "counts_in", "kv_in0", "kv_in1", "q_in", "scored", "maxed", "expd", "normed", "turned",
                   "turned_in", "valued", "out_in", "dve_step") as (block, s):
            kv_in = (s.kv_in0, s.kv_in1)

            @block.sync
            def _(sp):
                sp.dma_start(lcp[:], m.dram.count_past).then_inc(s.counts_in, 16)
                sp.dma_start(lcn[:], m.dram.count_new).then_inc(s.counts_in, 16)
                for b in range(REQ):
                    if b >= 2:
                        sp.wait_ge(s.valued, b - 1)
                    sp.dma_start(kc[:, b % 2], m.dram.cache_kT[m.l, b]).then_inc(kv_in[b % 2], 16)
                    sp.dma_start(vc[:, b % 2], m.dram.cache_v[m.l, b]).then_inc(kv_in[b % 2], 16)

            @block.tensor
            def _(pe):
                def scores(b):
                    pe.wait_ge(kv_in[b % 2], 32 * (b // 2 + 1))
                    if b >= 2:
                        pe.wait_ge(s.maxed, b - 1)
                    for c in range(PAIRS):
                        for n in range(2):
                            nc.tensor.matmul(s_ps[:, b % 2, n, :], qbd[:, b, c, :],
                                             kc[:, b % 2, c, n * 512:(n + 1) * 512],
                                             start=(c == 0), stop=(c == PAIRS - 1))
                        ins = nc.tensor.matmul(s_ps[:, b % 2, 2, 0:TS_], qbd[:, b, c, :], m.proj[:, BK + c, TP_:T],
                                               start=(c == 0), stop=(c == PAIRS - 1))
                    ins.then_inc(s.scored, 1)

                pe.wait_ge(s.q_in, 1)
                scores(0)
                for b in range(REQ):
                    if b + 1 < REQ:
                        scores(b + 1)
                    pe.wait_ge(s.normed, b + 1)
                    for n in range(NKB):
                        nc.tensor.transpose(t_ps[:, n, :], pr[:, b % 2, n * P:(n + 1) * P], m.ident[0:R, 0:R])
                    nc.tensor.transpose(t_ps[0:TS_, NKB, :], pr[:, b % 2, PAST:NKEYS], m.ident[0:R, 0:R]
                                        ).then_inc(s.turned, 1)
                    pe.wait_ge(s.turned_in, b + 1)
                    if b:
                        pe.wait_ge(s.out_in, b)
                    for c in range(PAIRS):
                        for n in range(NKB):
                            nc.tensor.matmul(o_ps[:, c, :], vc[:, b % 2, n, c * P:(c + 1) * P],
                                             pt[:, n, 16 * c:16 * c + 16], start=(n == 0), stop=False)
                        ins = nc.tensor.matmul(o_ps[:, c, :], m.v_tok[0:TS_, 4, c * P:(c + 1) * P],
                                               pt[0:TS_, NKB, 16 * c:16 * c + 16], start=False, stop=True)
                    ins.then_inc(s.valued, 1)

            @block.scalar
            def _(act):
                def exps(b):
                    act.wait_ge(s.maxed, b + 1)
                    if b >= 2:
                        act.wait_ge(s.turned, b - 1)
                    nc.scalar.activation(pr[:, b % 2, :], sm[:, b % 2, :], ACT.Exp, bias=st_[:, b % 2, 0:1],
                                         accum_out=st_[:, b % 2, 1:2]).then_inc(s.expd, 1)

                exps(0)
                for b in range(REQ):
                    if b + 1 < REQ:
                        exps(b + 1)
                    act.wait_ge(s.turned, b + 1)
                    if b:
                        act.wait_ge(s.valued, b)
                    nc.scalar.activation(pt[:, 0:NKB, :], t_ps[:, 0:NKB, :], ACT.Copy)
                    nc.scalar.activation(pt[0:TS_, NKB, :], t_ps[0:TS_, NKB, :], ACT.Copy).then_inc(s.turned_in, 1)

            @block.vector
            def _(dve):
                st = Steps(dve, s.dve_step)
                st.link(nc.vector.memset(qbd[:], 0.0))
                for h in range(HEADS):
                    c, o = h // 2, 64 * (h % 2)
                    ins = nc.vector.tensor_copy(
                        qbd[o:o + 64, :, c, h * STEPS:(h + 1) * STEPS],
                        m.proj[o:o + 64, BQ + c, TP_:T].rearrange("p (b t) -> p b t", b=REQ))
                ins.then_inc(s.q_in, 1)
                dve.wait_ge(s.counts_in, 32)

                def mask_max(b):
                    dve.wait_ge(s.scored, b + 1)
                    if b >= 2:
                        dve.wait_ge(s.expd, b - 1)
                    nc.vector.scalar_tensor_tensor(
                        out=sm[:, b % 2, 0:PAST], in0=s_ps[:, b % 2, 0:2, :].rearrange("p a n -> p (a n)"),
                        scalar=HD ** -0.5, in1=lcp[:], op0=ALU.mult, op1=ALU.add)
                    st.link(nc.vector.scalar_tensor_tensor(out=sm[:, b % 2, PAST:NKEYS], in0=s_ps[:, b % 2, 2, 0:TS_],
                                                           scalar=HD ** -0.5, in1=lcn[:, b, :],
                                                           op0=ALU.mult, op1=ALU.add))
                    nc.vector.tensor_reduce(st_[:, b % 2, 0:1], sm[:, b % 2, :], X, ALU.max,
                                            negate=True).then_inc(s.maxed, 1)

                def collect(b):
                    dve.wait_ge(s.valued, b + 1)
                    for o in range(2):
                        q = slice(64 * o, 64 * o + 64)
                        ins = nc.vector.tensor_copy(m.mixed[q, 2:5, TP_ + b * STEPS:TP_ + (b + 1) * STEPS],
                                                    o_ps[q, :, 8 * o:8 * o + 8])
                    ins.then_inc(s.out_in, 1)

                mask_max(0)
                for b in range(REQ):
                    if b + 1 < REQ:
                        mask_max(b + 1)
                    dve.wait_ge(s.expd, b + 1)
                    st.link(nc.vector.reciprocal(st_[:, b % 2, 2:3], st_[:, b % 2, 1:2]))
                    nc.vector.tensor_scalar(pr[:, b % 2, :], pr[:, b % 2, :], st_[:, b % 2, 2:3], None,
                                            ALU.mult).then_inc(s.normed, 1)
                    if b:
                        collect(b - 1)
                collect(REQ - 1)


def rwkv_prepare(nc, m, r):
    rw = m.proj_rw[:]
    halves = [(c, half, slice(half * HALF, (half + 1) * HALF)) for c in range(PAIRS) for half in range(2)]
    with ExitStack() as ctx:
        diff = ctx.enter_context(sbuf(nc, "rw_diff", [P, NB_RW, T], F32))
        wd = ctx.enter_context(sbuf(nc, "rw_wd", [P, T], F32))
        sq = ctx.enter_context(sbuf(nc, "rw_sq", [P, PAIRS, T], F32))
        tmp = ctx.enter_context(sbuf(nc, "rw_tmp", [P, PAIRS, T], F32))
        shift = ctx.enter_context(sbuf(nc, "rw_shift", [P, NB_RW, REQ], F32))
        last_p = ctx.enter_context(sbuf(nc, "rw_last_p", [P, NB_RW, 1], F32))
        last_s = ctx.enter_context(sbuf(nc, "rw_last_s", [P, NB_RW, REQ], F32))
        mu = ctx.enter_context(sbuf(nc, "rw_mu", [P, NB_RW], F32))
        vec = ctx.enter_context(sbuf(nc, "rw_vec", [P, 7, PAIRS], F32))
        wa_up = ctx.enter_context(sbuf(nc, "rw_wa", [P, PAIRS * P], F32))
        g_up = ctx.enter_context(sbuf(nc, "rw_g", [P, PAIRS * P], F32))
        ps = ctx.enter_context(psum(nc, "rw_ps", [P, 6, 512], F32))
        W0, A0, KK, KA, RK = 0, 1, 2, 3, 4

        def vecb(i):
            return vec[:, i, :].unsqueeze(2).to_broadcast([P, PAIRS, T])

        with stage(nc, "loaded", "shifted", "stored", "dve_step", "act_step", "gates_in", "w_up", "w_read",
                   "a_up", "a_read", "g_done", "g_read", "squared", "summed", "rooted", "prod", "bonus_sum",
                   "bonus_read", "decays", "scanned", "lasts") as (block, s):
            @block.sync
            def _(sp):
                for dst, src in ((shift[:], m.dram.state_shift[m.l]), (mu[:], m.dram.rwkv_mu[m.l]), (vec[:], m.dram.rwkv_vec[m.l]),
                                 (wa_up[:], m.dram.rwkv_wa[m.l]), (g_up[:], m.dram.rwkv_g[m.l])):
                    sp.dma_start(dst, src).then_inc(s.loaded, 16)
                sp.wait_ge(s.lasts, 2)
                sp.dma_start(m.dram.p_shift[m.l], last_p[:]).then_inc(s.stored, 16)
                sp.dma_start(m.dram.s_shift[m.l], last_s[:]).then_inc(s.stored, 16)
                sp.wait_ge(s.stored, 32)

            @block.tensor
            def _(pe):
                pe.wait_ge(s.gates_in, 1)
                for n, (c, half, t) in enumerate(halves):
                    ins = nc.tensor.matmul(ps[:, n, 0:HALF], wa_up[0:64, c * P:(c + 1) * P], wd[0:64, t],
                                           start=True, stop=True)
                ins.then_inc(s.w_up, 1)
                pe.wait_ge(s.w_read, 6)
                for n, (c, half, t) in enumerate(halves):
                    ins = nc.tensor.matmul(ps[:, n, 0:HALF], wa_up[64:P, c * P:(c + 1) * P], diff[64:P, 9, t],
                                           start=True, stop=True)
                ins.then_inc(s.a_up, 1)
                pe.wait_ge(s.a_read, 6)
                pe.wait_ge(s.gates_in, 2)
                for n, (c, half, t) in enumerate(halves):
                    ins = nc.tensor.matmul(ps[:, n, 0:HALF], g_up[:, c * P:(c + 1) * P], r.g[:, 0, t],
                                           start=True, stop=True)
                ins.then_inc(s.g_done, 1)
                pe.wait_ge(s.g_read, 6)
                pe.wait_ge(s.squared, 1)
                for n, (c, half, t) in enumerate(halves):
                    ins = nc.tensor.matmul(ps[:, n, 0:HALF], m.pair_ones[:], sq[:, c, t], start=True, stop=True)
                ins.then_inc(s.summed, 1)
                pe.wait_ge(s.rooted, 6)
                pe.wait_ge(s.prod, 1)
                for n, (c, half, t) in enumerate(halves):
                    ins = nc.tensor.matmul(ps[:, n, 0:HALF], m.pair_ones[:], tmp[:, c, t], start=True, stop=True)
                ins.then_inc(s.bonus_sum, 1)

            @block.scalar
            def _(act):
                nc.scalar.activation(last_p[:], rw[:, :, TP_ - 1:TP_], ACT.Copy).then_inc(s.lasts, 1)
                nc.scalar.activation(last_s[:], rw[:, :, TP_ + STEPS - 1:T:STEPS], ACT.Copy).then_inc(s.lasts, 1)
                act.wait_ge(s.shifted, 1)
                nc.scalar.activation(wd[0:64, :], diff[0:64, 9, :], ACT.Tanh).then_inc(s.gates_in, 1)
                nc.scalar.activation(r.g[:, 0, :], diff[:, 10, :], ACT.Sigmoid).then_inc(s.gates_in, 1)
                act.wait_ge(s.w_up, 1)
                for n, (c, half, t) in enumerate(halves):
                    nc.scalar.activation(r.ld[:, c, t], ps[:, n, 0:HALF], ACT.Sigmoid,
                                         bias=vec[:, W0, c:c + 1]).then_inc(s.w_read, 1)
                act.wait_ge(s.a_up, 1)
                for n, (c, half, t) in enumerate(halves):
                    nc.scalar.activation(r.b[:, c, t], ps[:, n, 0:HALF], ACT.Sigmoid,
                                         bias=vec[:, A0, c:c + 1]).then_inc(s.a_read, 1)
                act.wait_ge(s.g_done, 1)
                for n, (c, half, t) in enumerate(halves):
                    nc.scalar.activation(r.g[:, c, t], ps[:, n, 0:HALF], ACT.Copy).then_inc(s.g_read, 1)
                act.wait_ge(s.summed, 1)
                for n, (c, half, t) in enumerate(halves):
                    nc.scalar.activation(sq[:, c, t], ps[:, n, 0:HALF], ACT.Sqrt).then_inc(s.rooted, 1)
                act.wait_ge(s.scanned, 1)
                nc.scalar.activation(r.inv[:], r.cum[:], ACT.Exp, scale=-1.0).then_inc(s.decays, 1)
                nc.scalar.activation(r.end[:], r.end[:], ACT.Exp).then_inc(s.decays, 1)
                nc.scalar.activation(r.prev[:], r.prev[:], ACT.Exp).then_inc(s.decays, 1)
                act.wait_ge(s.decays, 1)
                nc.scalar.activation(r.cum[:], r.cum[:], ACT.Exp).then_inc(s.decays, 1)

            @block.vector
            def _(dve):
                st = Steps(dve, s.dve_step)

                def split(x, lo, hi):
                    return x[:, lo:hi, TP_:T].rearrange("p c (b t) -> p c b t", b=REQ)

                dve.wait_ge(s.loaded, 80)
                nc.vector.tensor_tensor(diff[:, :, 1:TP_], rw[:, :, 0:TP_ - 1], rw[:, :, 1:TP_], ALU.subtract)
                nc.vector.tensor_scalar(diff[:, :, 0:1], rw[:, :, 0:1], -1.0, None, ALU.mult)
                nc.vector.tensor_tensor(split(diff, 0, NB_RW)[:, :, :, 1:STEPS], split(rw, 0, NB_RW)[:, :, :, 0:STEPS - 1],
                                        split(rw, 0, NB_RW)[:, :, :, 1:STEPS], ALU.subtract)
                st.link(nc.vector.tensor_tensor(split(diff, 0, NB_RW)[:, :, :, 0], shift[:],
                                                split(rw, 0, NB_RW)[:, :, :, 0], ALU.subtract))
                st.link(nc.vector.tensor_tensor(diff[:], diff[:], mu[:].unsqueeze(2).to_broadcast([P, NB_RW, T]),
                                                ALU.mult))
                nc.vector.tensor_tensor(diff[:], diff[:], rw, ALU.add).then_inc(s.shifted, 1)
                dve.wait_ge(s.shifted, 1)
                r_, k_, v_ = diff[:, 0:3, :], diff[:, 3:6, :], diff[:, 6:9, :]
                st.link(nc.vector.tensor_copy(r.r[:], r_))
                st.link(nc.vector.tensor_copy(r.v[:], v_))
                st.link(nc.vector.tensor_tensor(r.kk[:], k_, vecb(KK), ALU.mult))
                nc.vector.tensor_tensor(sq[:], r.kk[:], r.kk[:], ALU.mult).then_inc(s.squared, 1)
                dve.wait_ge(s.w_read, 6)
                st.link(nc.vector.tensor_scalar(r.ld[:], r.ld[:], -DECAY, None, ALU.mult))
                for c in range(PAIRS):
                    ins = nc.vector.tensor_tensor_scan(r.cum[:, c, :], m.chunk_reset[:], r.ld[:, c, :], 0.0,
                                                       ALU.mult, ALU.add)
                    st.link(ins)
                nc.vector.tensor_tensor(r.prev[:], r.cum[:], r.ld[:], ALU.subtract)
                for lo, hi, n, w in ((0, TP_, NCH, CH), (TP_, T, REQ, STEPS)):
                    for c in range(PAIRS):
                        cum = r.cum[:, c, lo:hi].rearrange("p (n w) -> p n w", n=n)
                        ins = nc.vector.tensor_tensor(r.end[:, c, lo:hi].rearrange("p (n w) -> p n w", n=n),
                                                      cum[:, :, w - 1:w].to_broadcast([P, n, w]), cum, ALU.subtract)
                ins.then_inc(s.scanned, 1)
                dve.wait_ge(s.a_read, 6)
                st.link(nc.vector.scalar_tensor_tensor(out=tmp[:], in0=r.b[:], scalar=-1.0, in1=k_,
                                                       op0=ALU.add, op1=ALU.mult))
                st.link(nc.vector.tensor_tensor(tmp[:], tmp[:], vecb(KA), ALU.mult))
                st.link(nc.vector.tensor_tensor(r.k[:], tmp[:], k_, ALU.add))
                dve.wait_ge(s.rooted, 6)
                st.link(nc.vector.tensor_scalar(sq[:], sq[:], 1e-12, None, ALU.max))
                st.link(nc.vector.reciprocal(sq[:], sq[:]))
                st.link(nc.vector.tensor_tensor(r.kk[:], r.kk[:], sq[:], ALU.mult))
                st.link(nc.vector.tensor_tensor(r.b[:], r.b[:], r.kk[:], ALU.mult))
                st.link(nc.vector.tensor_tensor(tmp[:], r.r[:], r.k[:], ALU.mult))
                nc.vector.tensor_tensor(tmp[:], tmp[:], vecb(RK), ALU.mult).then_inc(s.prod, 1)
                dve.wait_ge(s.bonus_sum, 1)
                for n, (c, half, t) in enumerate(halves):
                    nc.vector.tensor_tensor(r.bonus[:, c, t], ps[:, n, 0:HALF], r.v[:, c, t], ALU.mult)
                dve.wait_ge(s.decays, 4)


def rwkv_tile(nc, m, r, lo, w, masks, chunks):
    sample = chunks == 0
    t = bass.ds(lo, w)
    H3 = HEADS * HD
    with ExitStack() as ctx:
        def sb(name, shape):
            return ctx.enter_context(sbuf(nc, name, shape, F32))

        kr = sb("rt_kr", [P, PAIRS, 2, w])
        ki, bi = sb("rt_ki", [P, PAIRS, w]), sb("rt_bi", [P, PAIRS, w])
        ke, be, vs = sb("rt_ke", [P, PAIRS, w]), sb("rt_be", [P, PAIRS, w]), sb("rt_vs", [P, PAIRS, w])
        dc = sb("rt_dc", [P, PAIRS, REQ])
        tok = sb("rt_tok", [w, 4, H3])
        n_m = sb("rt_n", [w, HEADS, 2, w])
        qb = sb("rt_qb", [w, HEADS, w])
        bq = sb("rt_bq", [w, HEADS, 2, w])
        mm_ = sb("rt_m", [w, HEADS, w])
        tt = sb("rt_tt", [w, HEADS, w])
        bv, uv = sb("rt_bv", [w, HEADS, HD]), sb("rt_uv", [w, HEADS, HD])
        wt = sb("rt_wt", [P, PAIRS, w])
        u = sb("rt_u", [w, HEADS, HD])
        o = sb("rt_o", [w, HEADS, HD])
        osq = sb("rt_osq", [w, HEADS, HD])
        stat = sb("rt_stat", [w, 4, HEADS])
        if sample:
            ux, vx = sb("rt_ux", [w, REQ, HD]), sb("rt_vx", [w, REQ, HD])
        ps = ctx.enter_context(psum(nc, "rt_ps", [P, 8, 512], F32))
        pos = lambda h: (h // 2, 64 * (h % 2))
        strict_incl, neg_strict_incl, neg_lower = masks
        names = ["staged", "turned", "turned_in", "gram", "gram_in", "powers", "powers_in", "last_power",
                 "folded", "bv_made", "bv_in", "uv_made", "uv_in", "wt_in", "u_made", "u_in", "st_made", "st_in",
                 "inter_in", "intra", "normed", "back", "back_in", "dve_step", "a_step"]
        with stage(nc, *names) as (block, s):
            @block.vector
            def _(dve):
                st = Steps(dve, s.dve_step)
                nc.vector.tensor_tensor(kr[:, :, 0, :], r.kk[:, :, t], r.prev[:, :, t], ALU.mult)
                nc.vector.tensor_tensor(kr[:, :, 1, :], r.r[:, :, t], r.cum[:, :, t], ALU.mult)
                nc.vector.tensor_tensor(ki[:], r.k[:, :, t], r.inv[:, :, t], ALU.mult)
                nc.vector.tensor_tensor(bi[:], r.b[:, :, t], r.inv[:, :, t], ALU.mult)
                nc.vector.tensor_tensor(ke[:], r.k[:, :, t], r.end[:, :, t], ALU.mult)
                nc.vector.scalar_tensor_tensor(out=be[:], in0=r.b[:, :, t], scalar=-1.0, in1=r.end[:, :, t],
                                               op0=ALU.mult, op1=ALU.mult)
                nc.vector.tensor_copy(vs[:], r.v[:, :, t])
                step = STEPS if sample else CH
                nch = w // step
                for c in range(PAIRS):
                    ins = nc.vector.tensor_copy(
                        dc[:, c, 0:nch].unsqueeze(2),
                        r.cum[:, c, t].rearrange("p (n w) -> p n w", w=step)[:, :, step - 1:step])
                ins.then_inc(s.staged, 1)
                for i in range(4):
                    dve.wait_ge(s.turned, i + 1)
                    nc.vector.tensor_copy(tok[:, i, :], ps[0:w, i, 0:H3]).then_inc(s.turned_in, 1)
                dve.wait_ge(s.gram, HEADS)
                for h in range(HEADS):
                    nc.vector.tensor_tensor(n_m[:, h, 0, :], ps[0:w, h, 0:w], neg_strict_incl[0:w, 0, 0:w], ALU.mult)
                    nc.vector.tensor_tensor(qb[:, h, :], ps[0:w, h, w:2 * w], neg_strict_incl[0:w, 1, 0:w], ALU.mult)
                    nc.vector.tensor_tensor(bq[:, h, :, :], ps[0:w, h, 2 * w:4 * w].rearrange("p (a w) -> p a w", a=2),
                                            strict_incl[0:w, :, 0:w], ALU.mult)
                    st.link(nc.vector.tensor_tensor(n_m[:, h, 1, :], ps[0:w, 6 + h % 2, (h // 2) * w:(h // 2 + 1) * w],
                                                    neg_lower[0:w, 0:w], ALU.mult))
                    nc.vector.tensor_tensor(tt[:, h, :], n_m[:, h, 0, :], m.ident[0:w, 0:w],
                                            ALU.add).then_inc(s.gram_in, 1)
                for k in range(4):
                    for h in range(HEADS):
                        dve.wait_ge(s.powers, 6 * k + h + 1)
                        nc.vector.tensor_copy(n_m[:, h, :, :].rearrange("p a w -> p (a w)"), ps[0:w, h, 0:2 * w]
                                              ).then_inc(s.powers_in, 1)
                    for h in range(HEADS):
                        dve.wait_ge(s.folded, 6 * k + h + 1)
                        nc.vector.tensor_tensor(tt[:, h, :], tt[:, h, :], ps[0:w, h, 2 * w:3 * w],
                                                ALU.add).then_inc(s.last_power, 1)
                for h in range(HEADS):
                    dve.wait_ge(s.uv_made, h + 1)
                    c, q = pos(h)
                    nc.vector.tensor_copy(uv[:, h, :], ps[0:w, h, 64:128])
                    nc.vector.tensor_copy(wt[q:q + 64, c, :], ps[q:q + 64, h, 256:256 + w]).then_inc(s.uv_in, 1)
                if not sample:
                    for n in range(chunks):
                        q = slice(n * CH, (n + 1) * CH)
                        dve.wait_ge(s.u_made, n + 1)
                        heads = lambda x: x[q, :, :].rearrange("p (c a) i -> p c a i", a=2)
                        banks = lambda k: ps[q, k:k + 2, 0:PAIRS * HD].rearrange("p a (c i) -> p c a i", c=PAIRS)
                        nc.vector.tensor_tensor(heads(u), heads(uv), banks(0), ALU.add).then_inc(s.u_in, 1)
                        nc.vector.tensor_copy(heads(o), banks(4))
                        st.link(nc.vector.tensor_tensor(r.state[:], r.state[:],
                                                        dc[:, :, n:n + 1].to_broadcast([P, PAIRS, HD]), ALU.mult))
                        dve.wait_ge(s.st_made, n + 1)
                        nc.vector.tensor_tensor(r.state[:], r.state[:],
                                                ps[:, 2, 0:PAIRS * HD].rearrange("p (c i) -> p c i", c=PAIRS),
                                                ALU.add).then_inc(s.st_in, 1)
                        dve.wait_ge(s.st_in, n + 1)
                else:
                    own = m.own_req[:, :].unsqueeze(2).to_broadcast([w, REQ, HD])
                    for h in range(HEADS):
                        c, q = pos(h)
                        cols = lambda bank: ps[0:w, bank, :].rearrange("p (b i) -> p b i", b=REQ)
                        dve.wait_ge(s.u_made, h + 1)
                        st.link(nc.vector.tensor_tensor(ux[:], cols(0),
                                                        uv[:, h, :].unsqueeze(1).to_broadcast([w, REQ, HD]), ALU.add))
                        st.link(nc.vector.tensor_tensor(ux[:], ux[:], own, ALU.mult))
                        nc.vector.tensor_tensor(vx[:], tok[:, 3, h * HD:(h + 1) * HD].unsqueeze(1)
                                                .to_broadcast([w, REQ, HD]), own, ALU.mult).then_inc(s.u_in, 1)
                        nc.vector.tensor_reduce(u[:, h, :], ux[:].rearrange("p b i -> p i b"), X, ALU.add)
                        dve.wait_ge(s.st_made, h + 1)
                        st.link(nc.vector.tensor_tensor(vx[:], cols(1), own, ALU.mult))
                        nc.vector.tensor_reduce(o[:, h, :], vx[:].rearrange("p b i -> p i b"), X, ALU.add)
                        state = r.states[q:q + 64, c, :, :]
                        st.link(nc.vector.tensor_tensor(state, state, dc[q:q + 64, c, :].unsqueeze(2)
                                                        .to_broadcast([64, REQ, HD]), ALU.mult))
                        nc.vector.tensor_tensor(state, state,
                                                ps[q:q + 64, 2, :].rearrange("p (b i) -> p b i", b=REQ),
                                                ALU.add).then_inc(s.st_in, 1)
                        dve.wait_ge(s.st_in, h + 1)
                dve.wait_ge(s.intra, 1)
                st.link(nc.vector.tensor_tensor(o[:], o[:], ps[0:w, 3, 0:H3].rearrange("p (h i) -> p h i", h=HEADS),
                                                ALU.add))
                st.link(nc.vector.tensor_reduce(stat[:, 0, :], o[:], X, ALU.add))
                st.link(nc.vector.tensor_scalar(stat[:, 0, :], stat[:, 0, :], -1.0 / HD, None, ALU.mult))
                st.link(nc.vector.tensor_tensor(o[:], o[:], stat[:, 0, :].unsqueeze(2).to_broadcast([w, HEADS, HD]),
                                                ALU.add))
                st.link(nc.vector.tensor_tensor(osq[:], o[:], o[:], ALU.mult))
                st.link(nc.vector.tensor_reduce(stat[:, 1, :], osq[:], X, ALU.add))
                nc.vector.tensor_scalar(stat[:, 1, :], stat[:, 1, :], 1.0 / HD, GN_EPS, ALU.mult,
                                        ALU.add).then_inc(s.a_step, 1)
                dve.wait_ge(s.a_step, 2)
                st.link(nc.vector.reciprocal(stat[:, 3, :], stat[:, 2, :]))
                nc.vector.tensor_tensor(o[:], o[:], stat[:, 3, :].unsqueeze(2).to_broadcast([w, HEADS, HD]),
                                        ALU.mult).then_inc(s.normed, 1)
                dve.wait_ge(s.back, 1)
                nc.vector.tensor_copy(m.mixed[:, 5:8, t], ps[:, 4, 0:PAIRS * w].rearrange("p (c w) -> p c w", c=PAIRS))

            @block.scalar
            def _(act):
                for h in range(HEADS):
                    act.wait_ge(s.bv_made, h + 1)
                    nc.scalar.activation(bv[:, h, :], ps[0:w, h, 0:64], ACT.Copy).then_inc(s.bv_in, 1)
                act.wait_ge(s.a_step, 1)
                nc.scalar.activation(stat[:, 2, :], stat[:, 1, :], ACT.Sqrt).then_inc(s.a_step, 1)

            @block.tensor
            def _(pe):
                pe.wait_ge(s.staged, 1)
                for i, src in enumerate((kr[:, :, 0, :], ke[:], be[:], vs[:])):
                    for c in range(PAIRS):
                        ins = nc.tensor.transpose(ps[0:w, i, c * P:(c + 1) * P], src[:, c, :], m.ident[:])
                    ins.then_inc(s.turned, 1)
                pe.wait_ge(s.turned_in, 4)
                for h in range(HEADS):
                    c, q = pos(h)
                    q = slice(q, q + 64)
                    both = kr[q, c, :, :].rearrange("p a w -> p (a w)")
                    nc.tensor.matmul(ps[0:w, h, 0:2 * w], bi[q, c, :], both, start=True, stop=True)
                    nc.tensor.matmul(ps[0:w, h, 2 * w:4 * w], ki[q, c, :], both, start=True, stop=True)
                    nc.tensor.matmul(ps[0:w, 6 + h % 2, (h // 2) * w:(h // 2 + 1) * w], kr[q, c, 0, :], bi[q, c, :],
                                     start=True, stop=True).then_inc(s.gram, 1)
                for k in range(4):
                    for h in range(HEADS):
                        if k == 0:
                            pe.wait_ge(s.gram_in, h + 1)
                        else:
                            pe.wait_ge(s.last_power, 6 * (k - 1) + h + 1)
                        nc.tensor.matmul(ps[0:w, h, 0:w], n_m[:, h, 1, :], n_m[:, h, 0, :], start=True, stop=True)
                        nc.tensor.matmul(ps[0:w, h, w:2 * w], n_m[:, h, 0, :], n_m[:, h, 1, :],
                                         start=True, stop=True).then_inc(s.powers, 1)
                    for h in range(HEADS):
                        pe.wait_ge(s.powers_in, 6 * k + h + 1)
                        nc.tensor.matmul(ps[0:w, h, 2 * w:3 * w], n_m[:, h, 1, :], tt[:, h, :],
                                         start=True, stop=True).then_inc(s.folded, 1)
                for h in range(HEADS):
                    pe.wait_ge(s.last_power, 18 + h + 1)
                    nc.tensor.matmul(ps[0:w, h, 0:64], bq[:, h, 0, :], tok[:, 3, h * HD:(h + 1) * HD],
                                     start=True, stop=True).then_inc(s.bv_made, 1)
                for h in range(HEADS):
                    c, q = pos(h)
                    pe.wait_ge(s.bv_in, h + 1)
                    nc.tensor.matmul(ps[0:w, h, 64:128], tt[:, h, :], bv[:, h, :], start=True, stop=True)
                    nc.tensor.matmul(ps[q:q + 64, h, 256:256 + w], tok[:, 0, h * HD:(h + 1) * HD], tt[:, h, :],
                                     start=True, stop=True).then_inc(s.uv_made, 1)
                pe.wait_ge(s.uv_in, HEADS)
                if not sample:
                    for n in range(chunks):
                        if n:
                            pe.wait_ge(s.st_in, n)
                        tc = slice(n * CH, (n + 1) * CH)
                        for h in range(HEADS):
                            c, q = pos(h)
                            q = slice(q, q + 64)
                            odd, ci = h % 2, slice(c * HD, (c + 1) * HD)
                            nc.tensor.matmul(ps[tc, odd, ci], wt[q, c, tc], r.state[q, c, :], start=True, stop=True)
                            ins = nc.tensor.matmul(ps[tc, 4 + odd, ci], kr[q, c, 1, tc], r.state[q, c, :],
                                                   start=True, stop=True)
                        ins.then_inc(s.u_made, 1)
                        pe.wait_ge(s.u_in, n + 1)
                        for h in range(HEADS):
                            c, q = pos(h)
                            out = ps[q:q + 64, 2, c * HD:(c + 1) * HD]
                            nc.tensor.matmul(out, tok[tc, 1, h * HD:(h + 1) * HD], tok[tc, 3, h * HD:(h + 1) * HD],
                                             start=True, stop=False)
                            ins = nc.tensor.matmul(out, tok[tc, 2, h * HD:(h + 1) * HD], u[tc, h, :],
                                                   start=False, stop=True)
                        ins.then_inc(s.st_made, 1)
                    pe.wait_ge(s.st_in, chunks)
                else:
                    for h in range(HEADS):
                        c, q = pos(h)
                        q = slice(q, q + 64)
                        if h:
                            pe.wait_ge(s.st_in, h)
                        state = r.states[q, c, :, :].rearrange("p b i -> p (b i)")
                        nc.tensor.matmul(ps[0:w, 0, :], wt[q, c, :], state, start=True, stop=True)
                        nc.tensor.matmul(ps[0:w, 1, :], kr[q, c, 1, :], state, start=True,
                                         stop=True).then_inc(s.u_made, 1)
                        pe.wait_ge(s.u_in, h + 1)
                        nc.tensor.matmul(ps[q, 2, :], tok[:, 1, h * HD:(h + 1) * HD],
                                         vx[:].rearrange("p b i -> p (b i)"), start=True, stop=False)
                        nc.tensor.matmul(ps[q, 2, :], tok[:, 2, h * HD:(h + 1) * HD],
                                         ux[:].rearrange("p b i -> p (b i)"), start=False,
                                         stop=True).then_inc(s.st_made, 1)
                    pe.wait_ge(s.st_in, HEADS)
                for h in range(HEADS):
                    out = ps[0:w, 3, h * HD:(h + 1) * HD]
                    nc.tensor.matmul(out, qb[:, h, :], u[:, h, :], start=True, stop=False)
                    ins = nc.tensor.matmul(out, bq[:, h, 1, :], tok[:, 3, h * HD:(h + 1) * HD],
                                           start=False, stop=True)
                ins.then_inc(s.intra, 1)
                pe.wait_ge(s.normed, 1)
                for c in range(PAIRS):
                    ins = nc.tensor.transpose(ps[:, 4, c * w:(c + 1) * w],
                                              o[:, 2 * c:2 * c + 2, :].rearrange("p h i -> p (h i)"),
                                              m.ident[0:w, 0:w])
                ins.then_inc(s.back, 1)


def rwkv(nc, m):
    with ExitStack() as ctx:
        def sb(name, shape):
            return ctx.enter_context(sbuf(nc, name, shape, F32))

        r = Parts()
        r.r, r.k, r.v, r.kk, r.b, r.g, r.bonus = (sb("rwkv_" + n, [P, PAIRS, T])
                                                  for n in ("r", "k", "v", "kk", "b", "g", "bonus"))
        r.ld, r.cum, r.prev, r.inv, r.end = (sb("rwkv_" + n, [P, PAIRS, T])
                                             for n in ("ld", "cum", "prev", "inv", "end"))
        rwkv_prepare(nc, m, r)
        r.state = sb("rwkv_state", [P, PAIRS, HD])
        r.states = sb("rwkv_states", [P, PAIRS, REQ, HD])
        ln = sb("rwkv_ln", [P, 7, PAIRS])
        with stage(nc, "loaded", "zeroed") as (block, s):
            @block.sync
            def _(sp):
                sp.dma_start(r.states[:], m.dram.state_wkv[m.l]).then_inc(s.loaded, 16)
                sp.dma_start(ln[:], m.dram.rwkv_vec[m.l]).then_inc(s.loaded, 16)
                sp.wait_ge(s.loaded, 32)

            @block.vector
            def _(dve):
                nc.vector.memset(r.state[:], 0.0)
        with nc.Fori(0, TP_ // P) as i:
            rwkv_tile(nc, m, r, i * P, P, m.masks_prompt, P // CH)
        rwkv_tile(nc, m, r, TP_, TS_, m.masks_sample, 0)
        with stage(nc, "stored", "dve_step") as (block, s):
            @block.sync
            def _(sp):
                sp.dma_start(m.dram.p_wkv[m.l], r.state[:]).then_inc(s.stored, 16)
                sp.dma_start(m.dram.s_wkv[m.l], r.states[:]).then_inc(s.stored, 16)
                sp.wait_ge(s.stored, 32)

            @block.vector
            def _(dve):
                st = Steps(dve, s.dve_step)
                out = m.mixed[:, 5:8, :]
                vecb = lambda n: ln[:, n, :].unsqueeze(2).to_broadcast([P, PAIRS, T])
                st.link(nc.vector.tensor_tensor(out, out, vecb(5), ALU.mult))
                st.link(nc.vector.tensor_tensor(out, out, vecb(6), ALU.add))
                st.link(nc.vector.tensor_tensor(out, out, r.bonus[:], ALU.add))
                st.link(nc.vector.tensor_tensor(out, out, r.g[:], ALU.mult))


def mix_out(nc, m):
    with ExitStack() as ctx:
        w = ctx.enter_context(sbuf(nc, "out_w", [P, KD, D], F32))
        w_hi = ctx.enter_context(sbuf(nc, "out_w_hi", [P, KD, D], F32R))
        w_lo = ctx.enter_context(sbuf(nc, "out_w_lo", [P, KD, D], F32R))
        x_hi = ctx.enter_context(sbuf(nc, "out_x_hi", [P, KD, T], F32R))
        x_lo = ctx.enter_context(sbuf(nc, "out_x_lo", [P, KD, T], F32R))
        ps = ctx.enter_context(psum(nc, "out_ps", [P, 8, 512], F32))
        with stage(nc, "loaded0", "loaded1", "hi", "lo", "made", "added") as (block, s):
            loaded = (s.loaded0, s.loaded1)

            @block.sync
            def _(sp):
                for n in range(2):
                    q = slice(4 * n, 4 * n + 4)
                    sp.dma_start(w[:, q], m.dram.w_out[m.l, :, q]).then_inc(loaded[n], 16)

            @block.scalar
            def _(act):
                for k in range(KD):
                    nc.scalar.activation(x_hi[:, k], m.mixed[:, k], ACT.Copy)
                    act.wait_ge(loaded[k // 4], 16)
                    nc.scalar.activation(w_hi[:, k], w[:, k], ACT.Copy).then_inc(s.hi, 1)

            @block.tensor
            def _(pe):
                def products(n, k):
                    i, half, rows = n // 2, n % 2, ROWS[n // 2]
                    t, c = slice(i * P, i * P + rows), slice(half * 512, (half + 1) * 512)
                    return three_passes(nc, ps[0:rows, n % 8, :], x_hi[:, k, t], x_lo[:, k, t],
                                        w_hi[:, k, c], w_lo[:, k, c], k == 0, k == KD - 1)

                for k in range(KD):
                    pe.wait_ge(s.lo, k + 1)
                    for n in range(8):
                        ins = products(n, k)
                        if k == KD - 1:
                            ins.then_inc(s.made, 1)
                for n in range(8, 2 * NT):
                    pe.wait_ge(s.added, n - 7)
                    for k in range(KD):
                        ins = products(n, k)
                    ins.then_inc(s.made, 1)

            @block.vector
            def _(dve):
                for k in range(KD):
                    dve.wait_ge(s.hi, k + 1)
                    nc.vector.tensor_tensor(x_lo[:, k], m.mixed[:, k], x_hi[:, k].bitcast(F32), ALU.subtract)
                    nc.vector.tensor_tensor(w_lo[:, k], w[:, k], w_hi[:, k].bitcast(F32),
                                            ALU.subtract).then_inc(s.lo, 1)
                for n in range(2 * NT):
                    i, half, rows = n // 2, n % 2, ROWS[n // 2]
                    dve.wait_ge(s.made, n + 1)
                    hh = m.h[0:rows, i, half * 512:(half + 1) * 512]
                    nc.vector.tensor_tensor(hh, hh, ps[0:rows, n % 8, :], ALU.add).then_inc(s.added, 1)


def query_scores(nc, m, block, s, l, h, r, par):
    @block.sync
    def _(sp):
        sp.dma_start(r.w[:], m.dram.peer_wq[l, bass.ds(h * 2, 2)].rearrange("b p k c -> p b k c")
                     ).then_inc(s.w_in, 16)
        sp.dma_start(r.keys[:], m.dram.peer_keys[l, h]).then_inc(s.keys_in, 16)

    @block.scalar
    def _(act):
        act.wait_ge(s.w_in, 16)
        for j in range(2):
            nc.scalar.activation(r.w_hi[:, j], r.w[:, j], ACT.Copy).then_inc(s.w_hi, 1)
        for n in range(4):
            act.wait_ge(s.made, n + 1)
            nc.scalar.activation(r.q[:, n // 2, (n % 2) * HALF:(n % 2 + 1) * HALF], r.q_ps[:, n, 0:HALF],
                                 ACT.Copy).then_inc(s.q_in, 1)
        for n in range(3):
            c = slice(4 * n, min(4 * n + 4, 2 * NT))
            act.wait_ge(s.scored, n + 1)
            nc.scalar.activation(r.sc[par][:, c, :], r.s_ps[:, c, :], ACT.Copy)

    @block.tensor
    def _(pe):
        for j in range(2):
            pe.wait_ge(s.w_lo, j + 1)
            for half in range(2):
                t = slice(half * HALF, (half + 1) * HALF)
                for k in range(KD):
                    ins = three_passes(nc, r.q_ps[:, 2 * j + half, 0:HALF], r.w_hi[:, j, k, :], r.w_lo[:, j, k, :],
                                       m.x_hi[:, k, t], m.x_lo[:, k, t], k == 0, k == KD - 1)
                ins.then_inc(s.made, 1)
        pe.wait_ge(s.q_in, 4)
        pe.wait_ge(s.keys_in, 16)
        for n in range(2 * NT):
            i, a = n // 2, n % 2
            ins = nc.tensor.matmul(r.s_ps[:, n, :], r.q[:, a, i * P:(i + 1) * P], r.keys[:, a, :],
                                   start=True, stop=True)
            if n % 4 == 3 or n == 2 * NT - 1:
                ins.then_inc(s.scored, 1)

    def split_low(dve):
        for j in range(2):
            dve.wait_ge(s.w_hi, j + 1)
            nc.vector.tensor_tensor(r.w_lo[:, j], r.w[:, j], r.w_hi[:, j].bitcast(F32),
                                    ALU.subtract).then_inc(s.w_lo, 1)
    return split_low


def top_keys(nc, m, dve, s, r, h, par, between):
    st = Steps(dve, s.dve_step)
    L = st.link

    def top16(n, values, spare, best, where, between=None):
        for u in range(n):
            ins = nc.vector.max(best(u)[:, 0:8], values(u))
        L(ins)
        for u in range(n):
            nc.vector.max_index(where(u)[:, 0:8], best(u)[:, 0:8], values(u))
            ins = nc.vector.match_replace(spare(u), best(u)[:, 0:8], values(u), -3.0e38)
        L(ins)
        if between is not None:
            between(dve)
        for u in range(n):
            ins = nc.vector.max(best(u)[:, 8:16], spare(u))
        L(ins)
        for u in range(n):
            ins = nc.vector.max_index(where(u)[:, 8:16], best(u)[:, 8:16], spare(u))
        L(ins)

    top16(2 * NT, lambda u: r.sc[par][:, u, :], lambda u: r.spare[:, u, :],
          lambda u: r.top[:, u // 2, u % 2, :], lambda u: r.idx[:, u // 2, u % 2, :], between)
    nc.vector.tensor_copy(r.idxf[:], r.idx[:])
    L(nc.vector.tensor_tensor(r.cand[:].rearrange("p i (a b) -> p i a b", a=TOPK),
                              r.top[:, :, 0, :].unsqueeze(3).to_broadcast([P, NT, TOPK, TOPK]),
                              r.top[:, :, 1, :].unsqueeze(2).to_broadcast([P, NT, TOPK, TOPK]), ALU.add))
    top16(NT, lambda u: r.cand[:, u, :], lambda u: r.cand2[:, u, :],
          lambda u: r.best[:, u, :], lambda u: r.place[:, u, :])
    nc.vector.tensor_copy(r.out[:, 2, :, bass.ds(h, 1), :], r.best[:].unsqueeze(2))
    nc.vector.tensor_scalar(r.slot[:, 0], r.place[:], 4, None, ALU.logical_shift_right)
    L(nc.vector.tensor_scalar(r.slot[:, 1], r.place[:], TOPK - 1, None, ALU.bitwise_and))
    L(nc.vector.tensor_copy(r.slotf[:], r.slot[:]))
    for a in range(2):
        ins = nc.vector.tensor_tensor(r.eq[:, a].rearrange("p i k n -> p (i k) n"),
                                      r.slotf[:, a].rearrange("p i k -> p (i k)").unsqueeze(2)
                                      .to_broadcast([P, NT * TOPK, TOPK]),
                                      m.iota[:, 0:TOPK].unsqueeze(1).to_broadcast([P, NT * TOPK, TOPK]),
                                      ALU.is_equal)
    L(ins)
    for a in range(2):
        ins = nc.vector.tensor_tensor(r.eq[:, a], r.eq[:, a],
                                      r.idxf[:, :, a, :].unsqueeze(2).to_broadcast([P, NT, TOPK, TOPK]), ALU.mult)
    L(ins)
    for a in range(2):
        nc.vector.tensor_reduce(r.out[:, a, :, bass.ds(h, 1), :], r.eq[:, a], X, ALU.add)


def route(nc, m, i1T, i2T, gT):
    with ExitStack() as ctx:
        def sb(name, shape, dt=F32):
            return ctx.enter_context(sbuf(nc, name, shape, dt))

        r = Parts()
        r.w, r.w_hi, r.w_lo = (sb("rt_w" + n, [P, 2, KD, P], dt) for n, dt in (("", F32), ("h", F32R), ("l", F32R)))
        r.keys = sb("rt_keys", [P, 2, NKEY])
        r.q = sb("rt_q", [P, 2, TPAD])
        r.sc = [sb("rt_sc", [P, 2 * NT, NKEY]) for _ in range(2)]
        r.spare = sb("rt_spare", [P, 2 * NT, NKEY])
        r.top = sb("rt_top", [P, NT, 2, TOPK])
        r.idx, r.idxf = sb("rt_idx", [P, NT, 2, TOPK], U32), sb("rt_idxf", [P, NT, 2, TOPK])
        r.cand, r.cand2 = sb("rt_cand", [P, NT, TOPK * TOPK]), sb("rt_cand2", [P, NT, TOPK * TOPK])
        r.best, r.place = sb("rt_best", [P, NT, TOPK]), sb("rt_place", [P, NT, TOPK], U32)
        r.slot, r.slotf = sb("rt_slot", [P, 2, NT, TOPK], U32), sb("rt_slotf", [P, 2, NT, TOPK])
        r.eq = sb("rt_eq", [P, 2, NT, TOPK, TOPK])
        r.out = sb("rt_out", [P, 3, NT, PH, TOPK])
        gs = sb("rt_gs", [P, 2, NT * PH])
        r.q_ps = ctx.enter_context(psum(nc, "rt_qps", [P, 4, 512], F32))
        r.s_ps = ctx.enter_context(psum(nc, "rt_sps", [P, 12, NKEY], F32))
        tps = ctx.enter_context(psum(nc, "rt_tps", [P, 3, P], F32))
        names = ["w_in", "keys_in", "w_hi", "w_lo", "made", "q_in", "scored", "dve_step"]

        def turn(find, make, par):
            with stage(nc, *names) as (block, s):
                if make is not None:
                    split_low = query_scores(nc, m, block, s, m.l, make, r, 1 - par)

                @block.vector
                def _(dve):
                    if find is None:
                        nc.vector.memset(r.q[:, :, T:TPAD], 0.0)
                        split_low(dve)
                    else:
                        top_keys(nc, m, dve, s, r, find, par, None if make is None else split_low)

        turn(None, 0, 1)
        with nc.Fori(0, PH // 2 - 1) as i:
            turn(i * 2, i * 2 + 1, 0)
            turn(i * 2 + 1, i * 2 + 2, 1)
        turn(PH - 2, PH - 1, 0)
        turn(PH - 1, None, 1)
        with stage(nc, "dve_step", "centred", "expd", "outs", "turned", "turned_in") as (block, s):
            score = r.out[:, 2].rearrange("p i h k -> p (i h) k")

            def bank(i):
                return tps[:, :, :] if i % 2 == 0 else r.q_ps[:, 0, 0:3 * P].rearrange("p (n c) -> p n c", n=3)

            @block.scalar
            def _(act):
                act.wait_ge(s.centred, 1)
                nc.scalar.activation(score, score, ACT.Exp).then_inc(s.expd, 1)
                for i in range(NT):
                    act.wait_ge(s.turned, i + 1)
                    for n, dst in enumerate((i1T, i2T, gT)):
                        ins = nc.scalar.activation(dst[:, i * P:(i + 1) * P], bank(i)[:, n, :], ACT.Copy)
                    ins.then_inc(s.turned_in, 1)

            @block.vector
            def _(dve):
                st = Steps(dve, s.dve_step)
                L = st.link
                L(nc.vector.tensor_copy(gs[:, 0, :].unsqueeze(2), score[:, :, 0:1]))
                nc.vector.tensor_tensor(score, score, gs[:, 0, :].unsqueeze(2).to_broadcast([P, NT * PH, TOPK]),
                                        ALU.subtract).then_inc(s.centred, 1)
                dve.wait_ge(s.expd, 1)
                L(nc.vector.tensor_reduce(gs[:, 0, :], score, X, ALU.add))
                L(nc.vector.reciprocal(gs[:, 1, :], gs[:, 0, :]))
                nc.vector.tensor_tensor(score, score, gs[:, 1, :].unsqueeze(2).to_broadcast([P, NT * PH, TOPK]),
                                        ALU.mult).then_inc(s.outs, 1)

            @block.tensor
            def _(pe):
                pe.wait_ge(s.outs, 1)
                for i in range(NT):
                    if i >= 2:
                        pe.wait_ge(s.turned_in, i - 1)
                    for n in range(3):
                        ins = nc.tensor.transpose(bank(i)[:, n, :], r.out[:, n, i].rearrange("p h k -> p (h k)"),
                                                  m.ident[:])
                    ins.then_inc(s.turned, 1)


def gates(nc, m, i1T, i2T, gT):
    TB, BUFS = 4, 3
    NB = UNIT // TB
    with ExitStack() as ctx:
        a1 = ctx.enter_context(sbuf(nc, "g_a1", [P, 2, TB, P], F32))
        a2 = ctx.enter_context(sbuf(nc, "g_a2", [P, 2, TB, P], F32))
        gst = ctx.enter_context(sbuf(nc, "g_stage", [P, BUFS, NKEY, UNIT], F32))
        ps = ctx.enter_context(psum(nc, "g_ps", [P, 4, TB, P], F32))
        names = ["hot", "slots_free", "made", "banks_free", "moved", "unit_free0", "unit_free1", "unit_free2"]
        with stage(nc, *names) as (block, s):
            unit_free = (s.unit_free0, s.unit_free1, s.unit_free2)

            @block.vector
            def _(dve):
                with dve.Fori(0, T // (4 * TB)) as n:
                    for b in range(4):
                        dve.wait_ge(s.slots_free, n * 4 + (b + 1))
                        nc.vector.tensor_tensor(a2[:, b % 2], m.iota[:].unsqueeze(1).to_broadcast([P, TB, P]),
                                                i2T[:, bass.ds(n * (4 * TB) + b * TB, TB)].unsqueeze(2)
                                                .to_broadcast([P, TB, P]), ALU.is_equal)
                        for j in range(TB):
                            t = bass.ds(n * (4 * TB) + (b * TB + j), 1)
                            ins = nc.vector.tensor_scalar(a1[:, b % 2, j, :], m.iota[:], i1T[:, t], gT[:, t],
                                                          ALU.is_equal, ALU.mult)
                        ins.then_inc(s.hot, 1)

            @block.tensor
            def _(pe):
                pe.sem_inc(s.slots_free, 2)
                with pe.Fori(0, T // (4 * TB)) as n:
                    for b in range(4):
                        pe.wait_ge(s.hot, n * 4 + (b + 1))
                        pe.wait_ge(s.banks_free, n * 4 + (b + 1))
                        for j in range(TB):
                            ins = nc.tensor.matmul(ps[:, b, j, :], a2[:, b % 2, j, :], a1[:, b % 2, j, :],
                                                   start=True, stop=True)
                        ins.then_inc(s.made, 1)
                        pe.wait_ge(s.made, n * 4 + (b + 1))
                        pe.sem_inc(s.slots_free, 1)

            @block.scalar
            def _(act):
                act.sem_inc(s.banks_free, 4)
                for k in range(BUFS):
                    act.sem_inc(unit_free[k], 16)
                with act.Fori(0, NU // BUFS) as n:
                    for k in range(BUFS):
                        act.wait_ge(unit_free[k], n * 16 + 16)
                        with act.Fori(0, NB // 4) as q:
                            for b in range(4):
                                act.wait_ge(s.made, n * (BUFS * NB) + q * 4 + (k * NB + b + 1))
                                nc.scalar.activation(
                                    gst[:, k, :, bass.ds(q * (4 * TB) + b * TB, TB)].rearrange("p i t -> p t i"),
                                    ps[:, b], ACT.Copy).then_inc(s.banks_free, 1)
                        act.wait_ge(s.banks_free, n * (BUFS * NB) + ((k + 1) * NB + 4))
                        act.sem_inc(s.moved, 1)

            @block.sync
            def _(sp):
                with sp.Fori(0, NU // BUFS) as n:
                    for k in range(BUFS):
                        sp.wait_ge(s.moved, n * BUFS + (k + 1))
                        sp.dma_start(m.dram.gate_dram[n * BUFS + k].rearrange("g p c -> p g c"),
                                     gst[:, k].rearrange("p (g e) t -> p g (e t)", e=EG)
                                     ).then_inc(unit_free[k], 16)
                for k in range(BUFS):
                    sp.wait_ge(unit_free[k], 16 * (NU // BUFS) + 16)


def experts(nc, m):
    with ExitStack() as ctx:
        def sb(name, shape, dt=F32):
            return ctx.enter_context(sbuf(nc, name, shape, dt))

        acc = sb("ex_acc", [P, KD, T])
        u_raw, u_hi, u_lo = (sb("ex_u" + n, [P, 2, KD, EG * P], dt) for n, dt in (("", F32), ("h", F32R), ("l", F32R)))
        v_raw, v_hi, v_lo = (sb("ex_v" + n, [P, 2, EG, D], dt) for n, dt in (("", F32), ("h", F32R), ("l", F32R)))
        gb = sb("ex_g", [P, 2, NU, EG, UNIT])
        a_raw = sb("ex_a", [P, EG, T])
        a_hi, a_lo = (sb("ex_a" + n, [P, 2, EG, T], F32R) for n in "hl")
        hp = ctx.enter_context(psum(nc, "ex_hp", [P, EG, 2, 512], F32))
        op = ctx.enter_context(psum(nc, "ex_op", [P, 2, 2, 512], F32))
        names = ["u_in0", "u_in1", "v_in0", "v_in1", "g_in0", "g_in1", "kept", "uh", "ul", "vh", "vl", "h_made",
                 "gelud", "gated", "ah", "al", "out_made", "added", "zeroed"]
        with stage(nc, *names) as (block, s):
            u_in, v_in, g_in = (s.u_in0, s.u_in1), (s.v_in0, s.v_in1), (s.g_in0, s.g_in1)

            @block.sync
            def _(sp):
                def load(g, j, first=False):
                    if not first:
                        sp.wait_ge(s.ul, g - 1)
                    sp.dma_start(u_raw[:, j], m.dram.peer_uT[m.l, g]).then_inc(u_in[j], 16)
                    if not first:
                        sp.wait_ge(s.gated, g * EG - EG)
                    sp.dma_start(gb[:, j].rearrange("p u e t -> p u (e t)"),
                                 m.dram.gate_dram[:, g].rearrange("u p c -> p u c")).then_inc(g_in[j], 16)
                    if not first:
                        sp.wait_ge(s.vl, g - 1)
                    sp.dma_start(v_raw[:, j], m.dram.peer_v[m.l, g]).then_inc(v_in[j], 16)
                    sp.dma_start(m.dram.s_k[m.l, g], m.dram.cache_k_kept[m.l, g]).then_inc(s.kept, 16)
                    sp.dma_start(m.dram.s_v[m.l, g], m.dram.cache_v_kept[m.l, g]).then_inc(s.kept, 16)

                load(0, 0, True)
                load(1, 1, True)
                with sp.Fori(1, NG // 2) as i:
                    for j in range(2):
                        load(i * 2 + j, j)
                sp.wait_ge(s.kept, 32 * NG)

            @block.tensor
            def _(pe):
                def first_product(g, j, first=False):
                    pe.wait_ge(s.ul, g + 1)
                    for e in range(EG):
                        if not first:
                            pe.wait_ge(s.gelud, g * EG + (e - 1))
                        for half in range(2):
                            t = slice(half * HALF, (half + 1) * HALF)
                            c = slice(e * P, (e + 1) * P)
                            for k in range(KD):
                                ins = three_passes(nc, hp[:, e, half, 0:HALF], u_hi[:, j, k, c], u_lo[:, j, k, c],
                                                   m.x_hi[:, k, t], m.x_lo[:, k, t], k == 0, k == KD - 1)
                        ins.then_inc(s.h_made, 1)

                def second_product(g, j, first=False):
                    pe.wait_ge(s.al, g * EG + EG)
                    pe.wait_ge(s.vl, g + 1)
                    for n in range(KD):
                        if not (first and n < 2):
                            pe.wait_ge(s.added, g * KD + (n - 1))
                        for half in range(2):
                            t = slice(half * HALF, (half + 1) * HALF)
                            c = slice(n * P, (n + 1) * P)
                            for e in range(EG):
                                ins = three_passes(nc, op[:, n % 2, half, 0:HALF], v_hi[:, j, e, c], v_lo[:, j, e, c],
                                                   a_hi[:, j, e, t], a_lo[:, j, e, t], e == 0, e == EG - 1)
                        ins.then_inc(s.out_made, 1)

                first_product(0, 0, True)
                first_product(1, 1)
                second_product(0, 0, True)
                with pe.Fori(1, NG // 2) as i:
                    first_product(i * 2, 0)
                    second_product(i * 2 - 1, 1)
                    first_product(i * 2 + 1, 1)
                    second_product(i * 2, 0)
                second_product(NG - 1, 1)

            @block.scalar
            def _(act):
                def split_u(g, j, turn, first=False):
                    act.wait_ge(u_in[j], turn * 16 + 16)
                    if not first:
                        act.wait_ge(s.h_made, g * EG - EG)
                    nc.scalar.activation(u_hi[:, j], u_raw[:, j], ACT.Copy).then_inc(s.uh, 1)

                def step(g, j, turn, first=False, last=False):
                    if not last:
                        split_u(g + 1, 1 - j, turn + j, first and j == 0)
                    act.wait_ge(v_in[j], turn * 16 + 16)
                    if not first:
                        act.wait_ge(s.out_made, g * KD - KD)
                    nc.scalar.activation(v_hi[:, j], v_raw[:, j], ACT.Copy).then_inc(s.vh, 1)
                    for e in range(EG):
                        act.wait_ge(s.h_made, g * EG + (e + 1))
                        if not (first and j == 0):
                            act.wait_ge(s.al, g * EG + (e - 1))
                        nc.scalar.activation(a_raw[:, e, :].rearrange("p (a t) -> p a t", a=2),
                                             hp[:, e, :, 0:HALF], ACT.Gelu).then_inc(s.gelud, 1)
                        act.wait_ge(s.gated, g * EG + (e + 1))
                        nc.scalar.activation(a_hi[:, j, e, :], a_raw[:, e, :], ACT.Copy).then_inc(s.ah, 1)

                split_u(0, 0, 0, True)
                step(0, 0, 0, first=True)
                step(1, 1, 0, first=True)
                with act.Fori(1, NG // 2 - 1) as i:
                    step(i * 2, 0, i)
                    step(i * 2 + 1, 1, i)
                step(NG - 2, 0, NG // 2 - 1)
                step(NG - 1, 1, NG // 2 - 1, last=True)

            @block.vector
            def _(dve):
                def split_u(g, j):
                    dve.wait_ge(s.uh, g + 1)
                    nc.vector.tensor_tensor(u_lo[:, j], u_raw[:, j], u_hi[:, j].bitcast(F32),
                                            ALU.subtract).then_inc(s.ul, 1)

                def split_v(g, j):
                    dve.wait_ge(s.vh, g + 1)
                    nc.vector.tensor_tensor(v_lo[:, j], v_raw[:, j], v_hi[:, j].bitcast(F32),
                                            ALU.subtract).then_inc(s.vl, 1)

                def add(g, ns):
                    for n in ns:
                        dve.wait_ge(s.out_made, g * KD + (n + 1))
                        a = acc[:, n, :].rearrange("p (a t) -> p a t", a=2)
                        nc.vector.tensor_tensor(a, a, op[:, n % 2, :, 0:HALF], ALU.add).then_inc(s.added, 1)

                def step(g, j, turn, first=False, last=False):
                    if not last:
                        split_u(g + 1, 1 - j)
                    dve.wait_ge(g_in[j], turn * 16 + 16)
                    for e in range(EG):
                        dve.wait_ge(s.gelud, g * EG + (e + 1))
                        a = a_raw[:, e, :].rearrange("p (u t) -> p u t", u=NU)
                        nc.vector.tensor_tensor(a, a, gb[:, j, :, e, :], ALU.mult).then_inc(s.gated, 1)
                        if e == 0:
                            split_v(g, j)
                        elif not first:
                            add(g - 1, (0,))
                        dve.wait_ge(s.ah, g * EG + (e + 1))
                        nc.vector.tensor_tensor(a_lo[:, j, e, :], a_raw[:, e, :], a_hi[:, j, e, :].bitcast(F32),
                                                ALU.subtract).then_inc(s.al, 1)
                    if not first:
                        add(g - 1, range(1, KD))

                nc.vector.memset(acc[:], 0.0).then_inc(s.zeroed, 1)
                dve.wait_ge(s.zeroed, 1)
                split_u(0, 0)
                step(0, 0, 0, first=True)
                step(1, 1, 0)
                with dve.Fori(1, NG // 2 - 1) as i:
                    step(i * 2, 0, i)
                    step(i * 2 + 1, 1, i)
                step(NG - 2, 0, NG // 2 - 1)
                step(NG - 1, 1, NG // 2 - 1, last=True)
                add(NG - 1, range(KD))
        ps = op[:, :, :, :].rearrange("p a b c -> p (a b) c")
        with stage(nc, "turned", "added") as (block, s):
            @block.tensor
            def _(pe):
                for n in range(2 * NT):
                    i, rows = n // 2, ROWS[n // 2]
                    if n >= 4:
                        pe.wait_ge(s.added, n - 3)
                    for q in range(4):
                        ins = nc.tensor.transpose(ps[0:rows, n % 4, q * P:(q + 1) * P],
                                                  acc[:, 4 * (n % 2) + q, i * P:i * P + rows], m.ident[:])
                    ins.then_inc(s.turned, 1)

            @block.vector
            def _(dve):
                for n in range(2 * NT):
                    i, rows = n // 2, ROWS[n // 2]
                    dve.wait_ge(s.turned, n + 1)
                    hh = m.h[0:rows, i, (n % 2) * 512:(n % 2 + 1) * 512]
                    nc.vector.tensor_tensor(hh, hh, ps[0:rows, n % 4, :], ALU.add).then_inc(s.added, 1)


def final_norm(nc, m):
    with ExitStack() as ctx:
        junk = ctx.enter_context(sbuf(nc, "fin_junk", [P, D], F32))
        st_ = ctx.enter_context(sbuf(nc, "fin_stat", [P, 3, NT], F32))
        y = ctx.enter_context(sbuf(nc, "fin_y", [P, NT, D], F32))
        g = ctx.enter_context(sbuf(nc, "fin_g", [P, D], F32))
        with stage(nc, "loaded", "squares", "eps_added", "rooted", "dve_step", "done", "stored") as (block, s):
            @block.sync
            def _(sp):
                sp.dma_start(g[:], m.dram.final_g).then_inc(s.loaded, 16)
                for i, r in enumerate(ROWS):
                    sp.wait_ge(s.done, i + 1)
                    sp.dma_start(m.dram.y[i * P:i * P + r, :], y[0:r, i, :]).then_inc(s.stored, 16)
                sp.wait_ge(s.stored, 16 * NT)

            @block.scalar
            def _(act):
                for i, r in enumerate(ROWS):
                    nc.scalar.activation(junk[0:r, :], m.h[0:r, i, :], ACT.Square,
                                         accum_out=st_[0:r, 0, i:i + 1]).then_inc(s.squares, 1)
                    act.wait_ge(s.squares, i + 1)
                for i, r in enumerate(ROWS):
                    act.wait_ge(s.eps_added, i + 1)
                    nc.scalar.activation(st_[0:r, 1, i:i + 1], st_[0:r, 0, i:i + 1], ACT.Sqrt).then_inc(s.rooted, 1)

            @block.vector
            def _(dve):
                st = Steps(dve, s.dve_step)
                dve.wait_ge(s.loaded, 16)
                for i, r in enumerate(ROWS):
                    dve.wait_ge(s.squares, i + 1)
                    nc.vector.tensor_scalar(st_[0:r, 0, i:i + 1], st_[0:r, 0, i:i + 1], 1.0 / D, RMS_EPS,
                                            ALU.mult, ALU.add).then_inc(s.eps_added, 1)
                for i, r in enumerate(ROWS):
                    dve.wait_ge(s.rooted, i + 1)
                    st.link(nc.vector.reciprocal(st_[0:r, 2, i:i + 1], st_[0:r, 1, i:i + 1]))
                    nc.vector.scalar_tensor_tensor(out=y[0:r, i, :], in0=m.h[0:r, i, :], scalar=st_[0:r, 2, i:i + 1],
                                                   in1=g[0:r, :], op0=ALU.mult, op1=ALU.mult).then_inc(s.done, 1)


def program(nc, d):
    m = Parts()
    m.dram = namedtuple("Dram", sorted(d))(*(d[n] for n in sorted(d)))
    with ExitStack() as ctx:
        def sb(name, shape):
            return ctx.enter_context(sbuf(nc, name, shape, F32))

        m.h = sb("h", [P, NT, D])
        m.ident, m.iota = sb("ident", [P, P]), sb("iota", [P, P])
        m.g1, m.g2 = sb("g1", [P, KD]), sb("g2", [P, KD])
        with stage(nc, "loaded") as (block, s):
            @block.sync
            def _(sp):
                loads = [(m.h[:, 0:4, :], m.dram.x_prompt), (m.h[0:TS_, 4, :], m.dram.x_sample),
                         (m.ident[:], m.dram.c_ident), (m.iota[:], m.dram.c_iota)]
                for dst, src in loads:
                    sp.dma_start(dst, src).then_inc(s.loaded, 16)
                sp.wait_ge(s.loaded, 16 * len(loads))
        with nc.Fori(0, LAYERS) as l:
            m.l = l
            with ExitStack() as mixer:
                def mb(name, shape):
                    return mixer.enter_context(sbuf(nc, name, shape, F32))

                m.mixed = mb("mixed", [P, KD, T])
                m.pair_ones = mb("pair_ones", [P, P])
                m.chunk_reset = mb("chunk_reset", [P, T])
                mk = mb("masks", [P, 2, 5, P])
                m.own_req = mb("own_req", [TS_, REQ])
                m.masks_prompt = (mk[:, 0, 0:2], mk[:, 0, 2:4], mk[:, 0, 4])
                m.masks_sample = (mk[:, 1, 0:2], mk[:, 1, 2:4], mk[:, 1, 4])
                load_constants(nc, [(m.pair_ones[:], m.dram.c_pair_ones), (m.chunk_reset[:], m.dram.c_chunk_reset),
                                    (mk[:], m.dram.c_masks), (m.own_req[:], m.dram.c_own_req),
                                    (m.g1[:], m.dram.norm1_g[l]), (m.g2[:], m.dram.norm2_g[l])])
                with ExitStack() as pb:
                    m.proj_rw = pb.enter_context(sbuf(nc, "proj_rw", [P, NB_RW, T], F32))
                    with ExitStack() as pa:
                        m.proj = pa.enter_context(sbuf(nc, "proj", [P, BR, T], F32))
                        m.v_tok = pa.enter_context(sbuf(nc, "v_tok", [P, NT, HEADS * HD], F32))
                        with ExitStack() as px:
                            m.x_hi, m.x_lo = (px.enter_context(sbuf(nc, n, [P, KD, T], F32R))
                                              for n in ("x_hi", "x_lo"))
                            norm_transpose(nc, m, m.g1)
                            project(nc, m, m.dram.w_in[m.l, BR:NB_IN], NB_RW, m.proj_rw)
                            project(nc, m, m.dram.w_in[m.l, 0:BR], BR, m.proj)
                        with ExitStack() as rp:
                            m.rope_cos = rp.enter_context(sbuf(nc, "rope_cos", [P, T], F32))
                            m.rope_sin = rp.enter_context(sbuf(nc, "rope_sin", [P, T], F32))
                            m.rope_swap = rp.enter_context(sbuf(nc, "rope_swap", [P, P], F32))
                            m.pool_inv = rp.enter_context(sbuf(nc, "pool_inv", [P, 2, T], F32))
                            load_constants(nc, [(m.rope_cos[:], m.dram.c_cos), (m.rope_sin[:], m.dram.c_sin),
                                                (m.rope_swap[:], m.dram.c_swap),
                                                (m.pool_inv[:], m.dram.c_pool_inv)])
                            rotate(nc, m)
                            pool(nc, m)
                        attend_prompt(nc, m)
                        attend_sample(nc, m)
                    rwkv(nc, m)
                mix_out(nc, m)
            with ExitStack() as peer:
                m.x_hi, m.x_lo = (peer.enter_context(sbuf(nc, n, [P, KD, T], F32R)) for n in ("x_hi", "x_lo"))
                norm_transpose(nc, m, m.g2)
                with ExitStack() as pi:
                    i1T, i2T, gT = (pi.enter_context(sbuf(nc, n, [P, TPAD], F32)) for n in ("i1T", "i2T", "gT"))
                    route(nc, m, i1T, i2T, gT)
                    gates(nc, m, i1T, i2T, gT)
                experts(nc, m)
        final_norm(nc, m)


def _constants():
    c = {}
    c["c_ident"] = np.eye(P, dtype=np.float32)
    c["c_iota"] = np.tile(np.arange(P, dtype=np.float32), (P, 1))
    c["c_pair_ones"] = np.kron(np.eye(2, dtype=np.float32), np.ones((HD, HD), np.float32))
    reset = np.ones((P, T), np.float32)
    reset[:, 0:TP_:CH] = 0
    reset[:, TP_::STEPS] = 0
    c["c_chunk_reset"] = reset
    masks = np.zeros((P, 2, 5, P), np.float32)
    s_, t_ = np.arange(P)[:, None], np.arange(P)[None, :]
    for n, w in enumerate((CH, STEPS)):
        same = s_ // w == t_ // w
        masks[:, n, 0] = same & (s_ < t_)
        masks[:, n, 1] = same & (s_ <= t_)
        masks[:, n, 2] = -masks[:, n, 0]
        masks[:, n, 3] = -masks[:, n, 1]
        masks[:, n, 4] = -(same & (t_ < s_)).astype(np.float32)
    c["c_masks"] = masks
    c["c_own_req"] = (np.arange(TS_)[:, None] // STEPS == np.arange(REQ)[None]).astype(np.float32)
    pos = np.concatenate([np.arange(TP_), PAST + np.tile(np.arange(STEPS), REQ)]).astype(np.float32)
    half = HD // 8
    inv = (np.float32(500000.0) ** (-np.arange(half, dtype=np.float32) * np.float32(2.0) / np.float32(2 * half)))
    ang = (pos[:, None] * inv.astype(np.float32)[None]).astype(np.float32)
    cos, sin, swap = np.ones((P, T), np.float32), np.zeros((P, T), np.float32), np.zeros((P, P), np.float32)
    for o in (0, HD):
        for j in range(half):
            cos[o + j] = cos[o + half + j] = np.cos(ang[:, j])
            sin[o + j] = sin[o + half + j] = np.sin(ang[:, j])
            swap[o + half + j, o + j] = -1
            swap[o + j, o + half + j] = 1
    c["c_cos"], c["c_sin"], c["c_swap"] = cos, sin, swap
    pinv = np.zeros((P, 2, T), np.float32)
    for a in range(2):
        for o in range(2):
            win = 2 << (2 * a + o)
            pinv[64 * o:64 * o + 64, a, 0:TP_] = np.float32(1) / np.minimum(win, np.arange(TP_) + 1).astype(np.float32)
            pinv[64 * o:64 * o + 64, a, TP_:] = np.float32(1) / np.float32(win)
    c["c_pool_inv"] = pinv

    def count(rel):
        n = sum(((rel >= 0) & (rel <= w) & (rel % d == 0)).astype(int) for w, d in ((128, 1), (512, 4), (2048, 16)))
        return np.where(n > 0, np.log(np.maximum(n, 1)), NEG).astype(np.float32)

    c["count_prompt"] = np.ascontiguousarray(
        count(np.arange(TP_)[:, None] - np.arange(TP_)[None]).reshape(4, P, TP_).transpose(1, 0, 2))
    q = np.tile(np.arange(STEPS), HEADS)
    c["count_past"] = count(PAST + q[:, None] - np.arange(PAST)[None])
    new = count(q[:, None] - np.tile(np.arange(STEPS), REQ)[None])
    own = np.arange(TS_)[None, None] // STEPS == np.arange(REQ)[None, :, None]
    c["count_new"] = np.ascontiguousarray(np.where(own, new[:, None], np.float32(NEG)).astype(np.float32))
    return c


def _layouts(i):
    i = {k: np.asarray(v) for k, v in i.items()}
    L = LAYERS
    cc = np.ascontiguousarray
    fm = lambda a: cc(a.reshape(L, -1, P).transpose(0, 2, 1))
    a = {}
    a["x_prompt"] = cc(i["x_prompt"].reshape(4, P, D).transpose(1, 0, 2))
    a["x_sample"] = i["x_sample"].reshape(TS_, D)
    blocks = lambda w: cc(w.reshape(L, KD, P, -1, P).transpose(0, 3, 2, 1, 4))
    a["w_in"], a["peer_wq"] = blocks(i["w_in"]), blocks(i["peer_wq"])
    a["w_out"] = cc(i["w_out"].reshape(L, KD, P, D).transpose(0, 2, 1, 3))
    for n in ("norm1_g", "norm2_g"):
        a[n] = fm(i[n])
    a["pool_scale"] = fm(i["pool_scale"])
    a["final_g"] = cc(np.broadcast_to(i["final_g"], (P, D)))
    a["state_pool"] = cc(i["state_pool"].transpose(0, 3, 1, 2).reshape(L, 2, P, REQ, POOL_BUF)
                         .transpose(0, 2, 1, 3, 4).reshape(L, P, 2 * REQ, POOL_BUF))
    a["pool_w"] = i["pool_w"]
    a["cache_kT"] = cc(i["cache_k"].reshape(L, REQ, PAST, PAIRS, P).transpose(0, 1, 4, 3, 2))
    a["cache_v"] = cc(i["cache_v"].reshape(L, REQ, PAST // P, P, HEADS * HD).transpose(0, 1, 3, 2, 4))
    for n in ("k", "v"):
        a[f"cache_{n}_kept"] = cc(i[f"cache_{n}"][:, :, STEPS:].reshape(L, NG, P, -1))
    a["state_shift"] = cc(i["state_shift"].reshape(L, REQ, NB_RW, P).transpose(0, 3, 2, 1))
    a["state_wkv"] = cc(i["state_wkv"].reshape(L, REQ, PAIRS, 2, HD, HD).transpose(0, 3, 5, 2, 1, 4)
                        .reshape(L, P, PAIRS, REQ, HD))
    a["rwkv_mu"] = fm(i["rwkv_mu"])
    vecs = [i["rwkv_" + n].reshape(L, HEADS * HD) for n in ("w0", "a0", "k_k", "k_a", "r_k", "ln_w", "ln_b")]
    a["rwkv_vec"] = cc(np.stack([fm(v) for v in vecs], 2))
    a["rwkv_wa"] = np.concatenate([i["rwkv_w_up"], i["rwkv_a_up"]], 1)
    a["rwkv_g"] = i["rwkv_g_up"]
    a["peer_keys"] = cc(i["peer_subkeys"].reshape(L, PH, 2, NKEY, P).transpose(0, 1, 4, 2, 3))
    a["peer_uT"] = cc(i["peer_u"].reshape(L, NG, EG * P, KD, P).transpose(0, 1, 4, 3, 2))
    a["peer_v"] = cc(i["peer_v"].reshape(L, NG, EG, P, D).transpose(0, 1, 3, 2, 4))
    return a


_OUTS = {
    "y": (T, D), "p_pool": (LAYERS, P, 2, POOL_BUF), "s_pool": (LAYERS, P, 2 * REQ, POOL_BUF),
    "out_k": (LAYERS, P, PAIRS, T), "out_v": (LAYERS, P, PAIRS, T),
    "p_shift": (LAYERS, P, NB_RW, 1), "s_shift": (LAYERS, P, NB_RW, REQ),
    "p_wkv": (LAYERS, P, PAIRS, HD), "s_wkv": (LAYERS, P, PAIRS, REQ, HD),
    "s_k": (LAYERS, NG, P, REQ * (PAST - STEPS) * HEADS * HD // (P * NG)),
    "s_v": (LAYERS, NG, P, REQ * (PAST - STEPS) * HEADS * HD // (P * NG)),
}


def _build(nc, arrays):
    d = {n: nc.dram_tensor("in_" + n, a.shape, F32, kind="ExternalInput").ap() for n, a in arrays.items()}
    for n, shape in _OUTS.items():
        d[n] = nc.dram_tensor("out_" + n, shape, F32, kind="ExternalOutput").ap()
    d["gate_dram"] = nc.dram_tensor("gate_matrix", (NU, NG, P, EG * UNIT), F32, kind="Internal").ap()
    program(nc, d)


def _returned(o):
    L = LAYERS
    tok = lambda a: a.transpose(0, 3, 2, 1).reshape(L, T, HEADS, HD)
    k, v = tok(o["out_k"]), tok(o["out_v"])
    kept = lambda a: a.reshape(L, REQ, PAST - STEPS, HEADS, HD)
    new = lambda a: a[:, TP_:].reshape(L, REQ, STEPS, HEADS, HD)
    pool_ = lambda a, b: a.reshape(L, P, 2, b, POOL_BUF).transpose(0, 3, 4, 2, 1).reshape(L, b, POOL_BUF, 2 * P)
    shift = lambda a: a.transpose(0, 3, 2, 1).reshape(L, a.shape[3], NB_RW * P)
    wkv = lambda a, b: (a.reshape(L, 2, HD, PAIRS, b, HD).transpose(0, 4, 3, 1, 5, 2)
                        .reshape(L, b, HEADS, HD, HD))
    out = (o["y"][:TP_].reshape(1, TP_, D), o["y"][TP_:].reshape(REQ, STEPS, D),
           pool_(o["p_pool"], 1), k[:, None, :TP_], v[:, None, :TP_], shift(o["p_shift"]), wkv(o["p_wkv"], 1),
           pool_(o["s_pool"], REQ), np.concatenate([kept(o["s_k"]), new(k)], 2),
           np.concatenate([kept(o["s_v"]), new(v)], 2), shift(o["s_shift"]), wkv(o["s_wkv"], REQ))
    return tuple(np.ascontiguousarray(x) for x in out)


def kernel(**inputs):
    import concourse.bacc as _bacc
    from concourse.bass_utils import run_bass_kernel_spmd as _run

    nc = _bacc.Bacc("TRN2", target_bir_lowering=False, num_devices=1)
    arrays = {**_layouts(inputs), **_constants()}
    _build(nc, arrays)
    r = _run(nc, [{"in_" + n: a for n, a in arrays.items()}], core_ids=[0])
    return _returned({n: r.results[0]["out_" + n] for n in _OUTS})
```

```python
from contextlib import ExitStack, contextmanager
from collections import namedtuple

import numpy as np
import concourse.bass as bass
from concourse import mybir

F32 = mybir.dt.float32
F32R = mybir.dt.float32r
U32 = mybir.dt.uint32
BF16 = mybir.dt.bfloat16
ALU = mybir.AluOpType
ACT = mybir.ActivationFunctionType
X = mybir.AxisListType.X

P = 128
LAYERS = 2
D = 1024
KD = D // P
TP_, TS_ = 512, 64
T = TP_ + TS_
HALF = T // 2
NT = 5
ROWS = [P, P, P, P, TS_]
REQ, STEPS = 8, 8
PAST = 1024
HD = 64
HEADS = 6
PAIRS = HEADS // 2
RMS_EPS = 1e-6
GN_EPS = HD * 1e-5
POOL_BUF = 15
NEG = -1e30
BQ, BK, BV, BR = 2, 5, 8, 11
NB_IN = 22
NB_RW = NB_IN - BR
W0, A0, KK, KA, RK, GN_W, GN_B = range(7)
CH = 32
NCH = TP_ // CH
DECAY = float(np.exp(-0.5))
PH, TOPK = 8, 16
NKEY = 128
CANDIDATES = [(0, 1, 16), (1, 4, 8), (4, 8, 4), (8, 16, 1)]
NCAND = sum((hi - lo) * width for lo, hi, width in CANDIDATES)
NB_Q = 16
TPAD = NT * P
EG = 2
NG = NKEY // EG
UNIT = 64
NU = T // UNIT


def _count():
    n = 0
    while True:
        yield n
        n += 1


_serial = _count()


class Parts:
    pass


def sbuf(nc, name, shape, dt):
    return nc.sbuf_tensor(f"{name}_{next(_serial)}", shape, dt)


def psum(nc, name, shape, dt):
    return nc.psum_tensor(f"{name}_{next(_serial)}", shape, dt)


class Steps:

    def __init__(self, eng, sem):
        self.eng, self.sem, self.n = eng, sem, 0

    def link(self, ins):
        ins.then_inc(self.sem, 1)
        self.n += 1
        self.eng.wait_ge(self.sem, self.n)


@contextmanager
def stage(nc, *names):
    with ExitStack() as ctx:
        sems = namedtuple("Semaphores", names)(*(ctx.enter_context(nc.semaphore(f"{n}_{next(_serial)}")) for n in names))
        with nc.Block() as block:
            yield block, sems
        with nc.Block() as tidy:
            @tidy.sync
            def _(sp):
                for sem in sems:
                    sp.sem_clear(sem)


def load_constants(nc, c):
    with stage(nc, "loaded") as (block, s):
        @block.sync
        def _(sp):
            for n, (dst, src) in enumerate(c):
                sp.dma_start(dst, src).then_inc(s.loaded, 16)
            sp.wait_ge(s.loaded, 16 * len(c))


def norm_transpose(nc, m, gain, head=None):
    with ExitStack() as ctx:
        junk = ctx.enter_context(sbuf(nc, "norm_junk", [P, D], F32))
        ssq = ctx.enter_context(sbuf(nc, "norm_ssq", [P, NT], F32))
        std = ctx.enter_context(sbuf(nc, "norm_std", [P, NT], F32))
        inv = ctx.enter_context(sbuf(nc, "norm_inv", [P, NT], F32))
        xn = ctx.enter_context(sbuf(nc, "norm_xn", [P, NT, D], F32))
        xg = ctx.enter_context(sbuf(nc, "norm_xg", [P, 2, 4, P], F32))
        ps = ctx.enter_context(psum(nc, "norm_ps", [P, 4, 4, P], F32))
        with stage(nc, "squares", "eps_added", "rooted", "dve_step", "scaled", "turned", "gained", "hi",
                   "lo", "w_in", "w_hi") as (block, s):
            if head is not None:
                @block.sync
                def _(sp):
                    sp.dma_start(head.w[:], m.dram.peer_wq[m.l, 0:2].rearrange("b p k c -> p b k c")
                                 ).then_inc(s.w_in, 16)

                @block.gpsimd
                def _(pool):
                    for j in range(2):
                        pool.wait_ge(s.w_hi, j + 1)
                        nc.gpsimd.tensor_tensor(head.w_lo[0][:, j], head.w[:, j], head.w_hi[0][:, j].bitcast(F32),
                                                ALU.subtract)

            @block.scalar
            def _(act):
                for i, r in enumerate(ROWS):
                    ins = nc.scalar.activation(junk[0:r, :], m.h[0:r, i, :], ACT.Square,
                                               accum_out=ssq[0:r, i:i + 1])
                    ins.then_inc(s.squares, 1)
                    act.wait_ge(s.squares, i + 1)
                for i, r in enumerate(ROWS):
                    act.wait_ge(s.eps_added, i + 1)
                    nc.scalar.activation(std[0:r, i:i + 1], ssq[0:r, i:i + 1], ACT.Sqrt).then_inc(s.rooted, 1)
                for n in range(2 * NT):
                    i, r, k = n // 2, ROWS[n // 2], 4 * (n % 2)
                    act.wait_ge(s.gained, n + 1)
                    nc.scalar.activation(m.x_hi[:, k:k + 4, i * P:i * P + r], xg[:, n % 2, :, 0:r],
                                         ACT.Copy).then_inc(s.hi, 1)
                    if head is not None and n in (2, 5):
                        j = n // 3
                        act.wait_ge(s.w_in, 16)
                        nc.scalar.activation(head.w_hi[0][:, j], head.w[:, j], ACT.Copy).then_inc(s.w_hi, 1)

            @block.vector
            def _(dve):
                st = Steps(dve, s.dve_step)
                for i, r in enumerate(ROWS):
                    dve.wait_ge(s.squares, i + 1)
                    nc.vector.tensor_scalar(ssq[0:r, i:i + 1], ssq[0:r, i:i + 1], 1.0 / D, RMS_EPS,
                                            ALU.mult, ALU.add).then_inc(s.eps_added, 1)
                for i, r in enumerate(ROWS):
                    dve.wait_ge(s.rooted, i + 1)
                    st.link(nc.vector.reciprocal(inv[0:r, i:i + 1], std[0:r, i:i + 1]))
                    nc.vector.tensor_scalar(xn[0:r, i, :], m.h[0:r, i, :], inv[0:r, i:i + 1], None,
                                            ALU.mult).then_inc(s.scaled, 1)

                def low(n):
                    i, r, k = n // 2, ROWS[n // 2], 4 * (n % 2)
                    dve.wait_ge(s.hi, n + 1)
                    nc.vector.tensor_tensor(m.x_lo[:, k:k + 4, i * P:i * P + r], xg[:, n % 2, :, 0:r],
                                            m.x_hi[:, k:k + 4, i * P:i * P + r].bitcast(F32), ALU.subtract
                                            ).then_inc(s.lo, 1)

                for n in range(2 * NT):
                    i, r, k = n // 2, ROWS[n // 2], 4 * (n % 2)
                    dve.wait_ge(s.turned, n + 1)
                    if n >= 2:
                        dve.wait_ge(s.lo, n - 1)
                    nc.vector.tensor_tensor(xg[:, n % 2, :, 0:r], ps[:, n % 4, :, 0:r],
                                            gain[:, k:k + 4].unsqueeze(2).to_broadcast([P, 4, r]),
                                            ALU.mult).then_inc(s.gained, 1)
                    if n:
                        low(n - 1)
                low(2 * NT - 1)

            @block.tensor
            def _(pe):
                for n in range(2 * NT):
                    i, r = n // 2, ROWS[n // 2]
                    pe.wait_ge(s.scaled, i + 1)
                    if n >= 4:
                        pe.wait_ge(s.gained, n - 3)
                    for q in range(4):
                        k = 4 * (n % 2) + q
                        ins = nc.tensor.transpose(ps[:, n % 4, q, 0:r], xn[0:r, i, k * P:(k + 1) * P],
                                                  m.ident[0:r, 0:r])
                    ins.then_inc(s.turned, 1)


def three_passes(nc, out, w_hi, w_lo, x_hi, x_lo, first, last):
    nc.tensor.matmul(out, w_lo, x_hi, start=first, stop=False)
    nc.tensor.matmul(out, w_hi, x_lo, start=False, stop=False)
    return nc.tensor.matmul(out, w_hi, x_hi, start=False, stop=last)


def project(nc, m, w, blocks, out):
    odd = blocks % 2
    with ExitStack() as ctx:
        wb = ctx.enter_context(sbuf(nc, "proj_w", [P, 2, KD, P], F32))
        w_hi = ctx.enter_context(sbuf(nc, "proj_w_hi", [P, 2, KD, P], F32R))
        w_lo = ctx.enter_context(sbuf(nc, "proj_w_lo", [P, 2, KD, P], F32R))
        ps = ctx.enter_context(psum(nc, "proj_ps", [P, 4, 512], F32))
        with stage(nc, "even_in", "odd_in", "hi", "lo", "made", "copied_lo", "copied_hi") as (block, s):
            landed = (s.even_in, s.odd_in)

            @block.sync
            def _(sp):
                for j in range(2):
                    sp.dma_start(wb[:, j], w[j]).then_inc(landed[j], 16)
                def refill(i, j):
                    sp.wait_ge(s.lo, i * 2 + (j + 1))
                    sp.dma_start(wb[:, j], w[i * 2 + (2 + j)]).then_inc(landed[j], 16)

                with sp.Fori(0, blocks // 2 - 1) as i:
                    for j in range(2):
                        refill(i, j)
                if odd:
                    refill(blocks // 2 - 1, 0)

            @block.tensor
            def _(pe):
                def body(i, first, js=(0, 1)):
                    for j in js:
                        pe.wait_ge(s.lo, i * 2 + (j + 1))
                        for half in range(2):
                            t = slice(half * HALF, (half + 1) * HALF)
                            if not first:
                                pe.wait_ge((s.copied_lo, s.copied_hi)[half], i * 2 + (j - 1))
                            for k in range(KD):
                                ins = three_passes(nc, ps[:, 2 * j + half, 0:HALF], w_hi[:, j, k, :], w_lo[:, j, k, :],
                                                   m.x_hi[:, k, t], m.x_lo[:, k, t], k == 0, k == KD - 1)
                            ins.then_inc(s.made, 1)

                body(0, True)
                with pe.Fori(1, blocks // 2) as i:
                    body(i, False)
                if odd:
                    body(blocks // 2, False, (0,))

            @block.scalar
            def _(act):
                def split(i, j, first=False):
                    act.wait_ge(landed[j], i * 16 + 16)
                    if not first:
                        act.wait_ge(s.made, i * 4 + (2 * j - 2))
                    nc.scalar.activation(w_hi[:, j], wb[:, j], ACT.Copy).then_inc(s.hi, 1)

                def copy(i, j):
                    act.wait_ge(s.made, i * 4 + (2 * j + 1))
                    nc.scalar.activation(out[:, bass.ds(i * 2 + j, 1), 0:HALF],
                                         ps[:, 2 * j:2 * j + 1, 0:HALF], ACT.Copy).then_inc(s.copied_lo, 1)

                split(0, 0, True)
                split(0, 1, True)
                with act.Fori(0, blocks // 2 - 1) as i:
                    for j in range(2):
                        copy(i, j)
                        split(i + 1, j)
                copy(blocks // 2 - 1, 0)
                if odd:
                    split(blocks // 2, 0)
                copy(blocks // 2 - 1, 1)
                if odd:
                    copy(blocks // 2, 0)

            @block.vector
            def _(dve):
                def split(i, j):
                    dve.wait_ge(s.hi, i * 2 + (j + 1))
                    nc.vector.tensor_tensor(w_lo[:, j], wb[:, j], w_hi[:, j].bitcast(F32),
                                            ALU.subtract).then_inc(s.lo, 1)

                def copy(i, j):
                    dve.wait_ge(s.made, i * 4 + (2 * j + 2))
                    nc.vector.tensor_copy(out[:, bass.ds(i * 2 + j, 1), HALF:T],
                                          ps[:, 2 * j + 1:2 * j + 2, 0:HALF]).then_inc(s.copied_hi, 1)

                split(0, 0)
                split(0, 1)
                with dve.Fori(0, blocks // 2 - 1) as i:
                    for j in range(2):
                        copy(i, j)
                        split(i + 1, j)
                copy(blocks // 2 - 1, 0)
                if odd:
                    split(blocks // 2, 0)
                copy(blocks // 2 - 1, 1)
                if odd:
                    copy(blocks // 2, 0)


def rotate(nc, m):
    with ExitStack() as ctx:
        tmp = ctx.enter_context(sbuf(nc, "rope_tmp", [P, T], F32))
        ps = ctx.enter_context(psum(nc, "rope_ps", [P, 4, 512], F32))
        vps = ctx.enter_context(psum(nc, "rope_vps", [P, 2, 512], F32))
        with stage(nc, "swapped", "mixed", "dve_step", "v_turned", "v_copied") as (block, s):
            @block.tensor
            def _(pe):
                for b in range(6):
                    for half in range(2):
                        n = 2 * b + half
                        if n >= 4:
                            pe.wait_ge(s.mixed, n // 2 - 1)
                        nc.tensor.matmul(ps[:, n % 4, 0:HALF], m.rope_swap[:],
                                         m.proj[:, BQ + b, half * HALF:(half + 1) * HALF],
                                         start=True, stop=True).then_inc(s.swapped, 1)
                for i, r in enumerate(ROWS):
                    if i >= 2:
                        pe.wait_ge(s.v_copied, i - 1)
                    for c in range(PAIRS):
                        ins = nc.tensor.transpose(vps[0:r, i % 2, c * P:(c + 1) * P],
                                                  m.proj[:, BV + c, i * P:i * P + r], m.ident[:])
                    ins.then_inc(s.v_turned, 1)

            @block.vector
            def _(dve):
                st = Steps(dve, s.dve_step)
                for b in range(6):
                    dve.wait_ge(s.swapped, 2 * b + 2)
                    src = ps[:, 2 * (b % 2):2 * (b % 2) + 2, 0:HALF]
                    st.link(nc.vector.tensor_tensor(tmp[:].rearrange("p (a t) -> p a t", a=2), src,
                                                    m.rope_sin[:].rearrange("p (a t) -> p a t", a=2), ALU.mult))
                    st.link(nc.vector.tensor_tensor(m.proj[:, BQ + b, :], m.proj[:, BQ + b, :], m.rope_cos[:],
                                                    ALU.mult))
                    nc.vector.tensor_tensor(m.proj[:, BQ + b, :], m.proj[:, BQ + b, :], tmp[:],
                                            ALU.add).then_inc(s.mixed, 1)
                    dve.wait_ge(s.mixed, b + 1)

            @block.scalar
            def _(act):
                for i, r in enumerate(ROWS):
                    act.wait_ge(s.v_turned, i + 1)
                    nc.scalar.activation(m.v_tok[0:r, i, :], vps[0:r, i % 2, 0:PAIRS * P], ACT.Copy).then_inc(s.v_copied, 1)


class Pooling:
    WP = POOL_BUF + TP_
    WS = POOL_BUF + STEPS

    def __init__(self, nc, m, ctx):
        def sb(name, shape):
            return ctx.enter_context(sbuf(nc, name, shape, F32))

        self.nc, self.m = nc, m
        self.xp, self.xs = sb("pool_xp", [P, 2, 1, self.WP]), sb("pool_xs", [P, 2, REQ, self.WS])
        self.sums_p, self.sums_s = sb("pool_sp", [P, 2, 1, self.WP]), sb("pool_ss", [P, 2, REQ, self.WS])
        self.other_p, self.other_s = sb("pool_tp", [P, 1, self.WP]), sb("pool_ts", [P, REQ, self.WS])
        self.diff = sb("pool_diff", [P, 2, T])
        self.inv = sb("pool_inv", [P, 2, T])
        self.w, self.scale = sb("pool_w", [P, 2, P]), sb("pool_scale", [P, 2])

    def load(self, sp, s):
        m = self.m
        sp.dma_start(self.xs[:, :, :, 0:POOL_BUF].rearrange("p a b r -> p (a b) r"),
                     m.dram.state_pool[m.l]).then_inc(s.pool_in, 16)
        sp.dma_start(self.scale[:], m.dram.pool_scale[m.l]).then_inc(s.pool_in, 16)
        sp.dma_start(self.inv[:], m.dram.c_pool_inv).then_inc(s.pool_in, 16)
        sp.wait_ge(s.pool_zeroed, 1)
        for a in range(2):
            for o in range(2):
                sp.dma_start(self.w[64 * o:64 * o + 64, a, 64 * o:64 * o + 64],
                             m.dram.pool_w[m.l, 2 * a + o]).then_inc(s.pool_in, 16)
        sp.dma_start(m.dram.p_pool[m.l], m.proj[:, 0:2, TP_ - POOL_BUF:TP_]).then_inc(s.pool_stored, 16)

    def store(self, sp, s):
        m = self.m
        sp.wait_ge(s.pool_filled, 1)
        sp.dma_start(m.dram.s_pool[m.l], self.xs[:, :, :, STEPS:self.WS].rearrange("p a b r -> p (a b) r")
                     ).then_inc(s.pool_stored, 16)
        sp.wait_ge(s.pool_stored, 32)

    def means(self, pool, s):
        nc, m, xp, xs, diff = self.nc, self.m, self.xp, self.xs, self.diff
        st = Steps(pool, s.pool_step)
        nc.gpsimd.memset(self.w[:], 0.0).then_inc(s.pool_zeroed, 1)
        st.link(nc.gpsimd.memset(xp[:, :, :, 0:POOL_BUF], 0.0))
        pool.wait_ge(s.pool_in, 112)
        nc.gpsimd.tensor_copy(xp[:, :, 0, POOL_BUF:self.WP], m.proj[:, 0:2, 0:TP_])
        for a in range(2):
            ins = nc.gpsimd.tensor_copy(xs[:, a, :, POOL_BUF:self.WS],
                                        m.proj[:, a, TP_:T].rearrange("p (b t) -> p b t", b=REQ))
        ins.then_inc(s.pool_filled, 1)
        pool.wait_ge(s.pool_filled, 1)
        for x, sums, other, wd in ((xp, self.sums_p, self.other_p, self.WP), (xs, self.sums_s, self.other_s, self.WS)):
            for a in range(2):
                for o in range(2):
                    q = slice(64 * o, 64 * o + 64)
                    win = 2 << (2 * a + o)
                    st.link(nc.gpsimd.tensor_tensor(sums[q, a, :, 1:wd], x[q, a, :, 1:wd],
                                                    x[q, a, :, 0:wd - 1], ALU.add))
                    done, src, dst = 2, sums[:, a], other[:]
                    while done < win:
                        lo = 2 * done - 1
                        st.link(nc.gpsimd.tensor_tensor(dst[q, :, lo:wd], src[q, :, lo:wd],
                                                        src[q, :, lo - done:wd - done], ALU.add))
                        src, dst = dst, src
                        done *= 2
                    of_x = ((lambda y: y[q, a, 0:TP_].unsqueeze(1)) if x is xp else
                            (lambda y: y[q, a, TP_:T].rearrange("p (b t) -> p b t", b=REQ)))
                    st.link(nc.gpsimd.tensor_tensor(of_x(diff), src[q, :, POOL_BUF:wd], of_x(self.inv), ALU.mult))
        nc.gpsimd.tensor_tensor(diff[:], diff[:], m.proj[:, 0:2, :], ALU.subtract).then_inc(s.pool_differed, 1)

    def map(self, pe, s, out):
        pe.wait_ge(s.pool_differed, 1)
        for n in range(4):
            a, half = n // 2, n % 2
            self.nc.tensor.matmul(out(n), self.w[:, a, :], self.diff[:, a, half * HALF:(half + 1) * HALF],
                                  start=True, stop=True).then_inc(s.pool_mapped, 1)

    def collect(self, act, s, out):
        act.wait_ge(s.pool_in, 112)
        for n in range(4):
            a, half = n // 2, n % 2
            act.wait_ge(s.pool_mapped, n + 1)
            self.nc.scalar.activation(self.m.mixed[:, a, half * HALF:(half + 1) * HALF], out(n), ACT.Copy,
                                      scale=self.scale[:, a:a + 1])


def attend_prompt(nc, m):
    units = [(qt, h) for qt in range(4) for h in range(HEADS)]
    with ExitStack() as ctx:
        sm = ctx.enter_context(sbuf(nc, "att_s", [P, 2, TP_], F32))
        pr = ctx.enter_context(sbuf(nc, "att_p", [P, 2, TP_], F32))
        pt = ctx.enter_context(sbuf(nc, "att_pt", [P, 2, 4, P], F32))
        st_ = ctx.enter_context(sbuf(nc, "att_stat", [P, 2, 4], F32))
        lc = ctx.enter_context(sbuf(nc, "att_lc", [P, 4, TP_], F32))
        s_ps = ctx.enter_context(psum(nc, "att_sps", [P, 3, TP_], F32))
        t_ps = ctx.enter_context(psum(nc, "att_tps", [P, 2, 4, P], F32))
        o_ps = ctx.enter_context(psum(nc, "att_ops", [P, 2, 512], F32))
        with stage(nc, "counts_in", "scored", "maxed", "expd", "normed", "turned", "turned_in", "valued",
                   "out_in", "dve_step", "stored") as (block, s):
            @block.sync
            def _(sp):
                sp.dma_start(lc[:], m.dram.count_prompt).then_inc(s.counts_in, 16)
                sp.dma_start(m.dram.out_k[m.l], m.proj[:, BK:BK + PAIRS, :]).then_inc(s.stored, 16)
                sp.dma_start(m.dram.out_v[m.l], m.proj[:, BV:BV + PAIRS, :]).then_inc(s.stored, 16)
                sp.wait_ge(s.stored, 32)

            @block.tensor
            def _(pe):
                def scores(u):
                    qt, h = units[u]
                    c, o = h // 2, 64 * (h % 2)
                    n = (qt + 1) * P
                    if u >= 3:
                        pe.wait_ge(s.maxed, u - 2)
                    nc.tensor.matmul(s_ps[:, u % 3, 0:n], m.proj[o:o + 64, BQ + c, qt * P:(qt + 1) * P],
                                     m.proj[o:o + 64, BK + c, 0:n], start=True, stop=True).then_inc(s.scored, 1)

                for u in range(3):
                    scores(u)
                for u, (qt, h) in enumerate(units):
                    c, o = h // 2, 64 * (h % 2)
                    pe.wait_ge(s.normed, u + 1)
                    if u >= 2:
                        pe.wait_ge(s.turned_in, u - 1)
                    for b in range(qt + 1):
                        ins = nc.tensor.transpose(t_ps[:, u % 2, b, :], pr[:, u % 2, b * P:(b + 1) * P], m.ident[:])
                    ins.then_inc(s.turned, 1)
                    if u + 3 < len(units):
                        scores(u + 3)
                    pe.wait_ge(s.turned_in, u + 1)
                    if u >= 2:
                        pe.wait_ge(s.out_in, u - 1)
                    for b in range(qt + 1):
                        ins = nc.tensor.matmul(o_ps[o:o + 64, u % 2, 0:P], m.v_tok[:, b, h * HD:(h + 1) * HD],
                                               pt[:, u % 2, b, :], start=(b == 0), stop=(b == qt))
                    ins.then_inc(s.valued, 1)

            @block.scalar
            def _(act):
                def exps(u):
                    n = (units[u][0] + 1) * P
                    act.wait_ge(s.maxed, u + 1)
                    if u >= 2:
                        act.wait_ge(s.turned, u - 1)
                    nc.scalar.activation(pr[:, u % 2, 0:n], sm[:, u % 2, 0:n], ACT.Exp, bias=st_[:, u % 2, 0:1],
                                         accum_out=st_[:, u % 2, 1:2]).then_inc(s.expd, 1)

                exps(0)
                for u, (qt, h) in enumerate(units):
                    if u + 1 < len(units):
                        exps(u + 1)
                    act.wait_ge(s.turned, u + 1)
                    if u >= 2:
                        act.wait_ge(s.valued, u - 1)
                    nc.scalar.activation(pt[:, u % 2, 0:qt + 1, :], t_ps[:, u % 2, 0:qt + 1, :],
                                         ACT.Copy).then_inc(s.turned_in, 1)

            @block.vector
            def _(dve):
                st = Steps(dve, s.dve_step)
                dve.wait_ge(s.counts_in, 16)

                def mask_max(u):
                    qt = units[u][0]
                    n = (qt + 1) * P
                    dve.wait_ge(s.scored, u + 1)
                    if u >= 2:
                        dve.wait_ge(s.expd, u - 1)
                    st.link(nc.vector.scalar_tensor_tensor(out=sm[:, u % 2, 0:n], in0=s_ps[:, u % 3, 0:n],
                                                           scalar=HD ** -0.5, in1=lc[:, qt, 0:n],
                                                           op0=ALU.mult, op1=ALU.add))
                    nc.vector.tensor_reduce(st_[:, u % 2, 0:1], sm[:, u % 2, 0:n], X, ALU.max,
                                            negate=True).then_inc(s.maxed, 1)

                def collect(u):
                    qt, h = units[u]
                    c, o = h // 2, 64 * (h % 2)
                    dve.wait_ge(s.valued, u + 1)
                    nc.vector.tensor_copy(m.mixed[o:o + 64, 2 + c, qt * P:(qt + 1) * P],
                                          o_ps[o:o + 64, u % 2, 0:P]).then_inc(s.out_in, 1)

                mask_max(0)
                mask_max(1)
                for u, (qt, h) in enumerate(units):
                    n = (qt + 1) * P
                    dve.wait_ge(s.expd, u + 1)
                    st.link(nc.vector.reciprocal(st_[:, u % 2, 2:3], st_[:, u % 2, 1:2]))
                    nc.vector.tensor_scalar(pr[:, u % 2, 0:n], pr[:, u % 2, 0:n], st_[:, u % 2, 2:3], None,
                                            ALU.mult).then_inc(s.normed, 1)
                    if u + 2 < len(units):
                        mask_max(u + 2)
                    if u >= 1:
                        collect(u - 1)
                collect(len(units) - 1)


def attend_sample(nc, m):
    R = HEADS * STEPS
    NKEYS = PAST + TS_
    NKB = PAST // P
    H3 = HEADS * HD
    with ExitStack() as ctx:
        kc = ctx.enter_context(sbuf(nc, "dec_k", [P, 2, PAIRS, PAST], F32))
        vc = ctx.enter_context(sbuf(nc, "dec_v", [P, 2, NKB, H3], F32))
        lcp = ctx.enter_context(sbuf(nc, "dec_lcp", [R, PAST], F32))
        lcn = ctx.enter_context(sbuf(nc, "dec_lcn", [R, REQ, TS_], F32))
        qbd = ctx.enter_context(sbuf(nc, "dec_q", [P, REQ, PAIRS, R], F32))
        sm = ctx.enter_context(sbuf(nc, "dec_s", [R, 2, NKEYS], F32))
        pr = ctx.enter_context(sbuf(nc, "dec_p", [R, 2, NKEYS], F32))
        pt = ctx.enter_context(sbuf(nc, "dec_pt", [P, NKB + 1, R], F32))
        st_ = ctx.enter_context(sbuf(nc, "dec_stat", [R, 2, 4], F32))
        o = ctx.enter_context(sbuf(nc, "dec_o", [R, H3], F32))
        s_ps = ctx.enter_context(psum(nc, "dec_sps", [P, 2, 3, 512], F32))
        t_bank = ctx.enter_context(psum(nc, "dec_tps", [P, 512], F32))
        t_ps = t_bank[:, 0:(NKB + 1) * R].rearrange("p (n r) -> p n r", r=R)
        o_ps = ctx.enter_context(psum(nc, "dec_ops", [P, 512], F32))

        pooling = Pooling(nc, m, ctx)

        def pooled(n):
            return s_ps[:, n // 2, n % 2, 0:HALF]

        def back(b):
            return s_ps[:, (b + 1) % 2, 2, TS_:TS_ + PAIRS * R].rearrange("p (c r) -> p c r", c=PAIRS)

        with stage(nc, "counts_in", "k_in0", "k_in1", "v_in0", "v_in1", "q_in", "scored", "maxed", "expd", "turned",
                   "turned_in", "valued", "scaled", "back", "back_in", "dve_step", "pool_in", "pool_zeroed",
                   "pool_filled", "pool_differed", "pool_mapped", "pool_stored", "pool_step") as (block, s):
            k_in, v_in = (s.k_in0, s.k_in1), (s.v_in0, s.v_in1)

            @block.sync
            def _(sp):
                def keys(b):
                    if b >= 2:
                        sp.wait_ge(s.scored, b - 1)
                    sp.dma_start(kc[:, b % 2], m.dram.cache_kT[m.l, b]).then_inc(k_in[b % 2], 16)

                def values(b):
                    if b >= 2:
                        sp.wait_ge(s.valued, b - 1)
                    sp.dma_start(vc[:, b % 2], m.dram.cache_v[m.l, b]).then_inc(v_in[b % 2], 16)

                keys(0)
                sp.dma_start(lcp[:], m.dram.count_past).then_inc(s.counts_in, 16)
                sp.dma_start(lcn[:], m.dram.count_new).then_inc(s.counts_in, 16)
                keys(1)
                for b in range(REQ):
                    if b == 1:
                        keys(2)
                    if b >= 2 and b + 1 < REQ:
                        keys(b + 1)
                    values(b)
                    if b == 0:
                        pooling.load(sp, s)
                pooling.store(sp, s)

            @block.tensor
            def _(pe):
                def scores(b):
                    pe.wait_ge(k_in[b % 2], 16 * (b // 2 + 1))
                    if b >= 2:
                        pe.wait_ge(s.maxed, b - 1)
                    if b >= 3:
                        pe.wait_ge(s.back_in, b - 2)
                    for c in range(PAIRS):
                        for n in range(2):
                            nc.tensor.matmul(s_ps[0:R, b % 2, n, :], qbd[:, b, c, :],
                                             kc[:, b % 2, c, n * 512:(n + 1) * 512],
                                             start=(c == 0), stop=(c == PAIRS - 1))
                        ins = nc.tensor.matmul(s_ps[0:R, b % 2, 2, 0:TS_], qbd[:, b, c, :],
                                               m.proj[:, BK + c, TP_:T], start=(c == 0), stop=(c == PAIRS - 1))
                    ins.then_inc(s.scored, 1)

                def turn_back(b):
                    pe.wait_ge(s.scaled, b + 1)
                    for c in range(PAIRS):
                        ins = nc.tensor.transpose(back(b)[:, c, :], o[:, c * P:(c + 1) * P], m.ident[0:R, 0:R])
                    ins.then_inc(s.back, 1)

                pe.wait_ge(s.q_in, 1)
                scores(0)
                for b in range(REQ):
                    pe.wait_ge(s.expd, b + 1)
                    for n in range(NKB):
                        nc.tensor.transpose(t_ps[:, n, :], pr[:, b % 2, n * P:(n + 1) * P], m.ident[0:R, 0:R])
                    nc.tensor.transpose(t_ps[0:TS_, NKB, :], pr[:, b % 2, PAST:NKEYS], m.ident[0:R, 0:R]
                                        ).then_inc(s.turned, 1)
                    if b + 1 < REQ:
                        scores(b + 1)
                    if b:
                        turn_back(b - 1)
                    pe.wait_ge(s.turned_in, b + 1)
                    pe.wait_ge(v_in[b % 2], 16 * (b // 2 + 1))
                    for n in range(NKB):
                        nc.tensor.matmul(o_ps[0:R, 0:H3], pt[:, n, :], vc[:, b % 2, n, :], start=(n == 0), stop=False)
                    nc.tensor.matmul(o_ps[0:R, 0:H3], pt[0:TS_, NKB, :], m.v_tok[0:TS_, 4, :],
                                     start=False, stop=True).then_inc(s.valued, 1)
                turn_back(REQ - 1)
                pooling.map(pe, s, pooled)

            @block.scalar
            def _(act):
                def exps(b):
                    act.wait_ge(s.maxed, b + 1)
                    if b >= 2:
                        act.wait_ge(s.turned, b - 1)
                        act.wait_ge(s.scaled, b - 1)
                    nc.scalar.activation(pr[:, b % 2, :], sm[:, b % 2, :], ACT.Exp, bias=st_[:, b % 2, 0:1],
                                         accum_out=st_[:, b % 2, 1:2]).then_inc(s.expd, 1)

                exps(0)
                for b in range(REQ):
                    act.wait_ge(s.turned, b + 1)
                    if b:
                        act.wait_ge(s.valued, b)
                    nc.scalar.activation(pt[:, 0:NKB, :], t_ps[:, 0:NKB, :], ACT.Copy)
                    nc.scalar.activation(pt[0:TS_, NKB, :], t_ps[0:TS_, NKB, :], ACT.Copy).then_inc(s.turned_in, 1)
                    if b + 1 < REQ:
                        exps(b + 1)
                pooling.collect(act, s, pooled)

            @block.gpsimd
            def _(pool):
                pooling.means(pool, s)

            @block.vector
            def _(dve):
                st = Steps(dve, s.dve_step)
                st.link(nc.vector.memset(qbd[:], 0.0))
                for h in range(HEADS):
                    c, q = h // 2, 64 * (h % 2)
                    ins = nc.vector.tensor_copy(
                        qbd[q:q + 64, :, c, h * STEPS:(h + 1) * STEPS],
                        m.proj[q:q + 64, BQ + c, TP_:T].rearrange("p (b t) -> p b t", b=REQ))
                ins.then_inc(s.q_in, 1)
                dve.wait_ge(s.counts_in, 32)

                def mask_max(b):
                    dve.wait_ge(s.scored, b + 1)
                    if b >= 2:
                        dve.wait_ge(s.expd, b - 1)
                    nc.vector.scalar_tensor_tensor(
                        out=sm[:, b % 2, 0:PAST], in0=s_ps[0:R, b % 2, 0:2, :].rearrange("p a n -> p (a n)"),
                        scalar=HD ** -0.5, in1=lcp[:], op0=ALU.mult, op1=ALU.add)
                    st.link(nc.vector.scalar_tensor_tensor(out=sm[:, b % 2, PAST:NKEYS],
                                                           in0=s_ps[0:R, b % 2, 2, 0:TS_],
                                                           scalar=HD ** -0.5, in1=lcn[:, b, :],
                                                           op0=ALU.mult, op1=ALU.add))
                    nc.vector.tensor_reduce(st_[:, b % 2, 0:1], sm[:, b % 2, :], X, ALU.max,
                                            negate=True).then_inc(s.maxed, 1)

                def scale(b):
                    dve.wait_ge(s.valued, b + 1)
                    st.link(nc.vector.reciprocal(st_[:, b % 2, 2:3], st_[:, b % 2, 1:2]))
                    nc.vector.tensor_scalar(o[:], o_ps[0:R, 0:H3], st_[:, b % 2, 2:3], None,
                                            ALU.mult).then_inc(s.scaled, 1)

                def collect(b):
                    dve.wait_ge(s.back, b + 1)
                    for h in range(HEADS):
                        c, q = h // 2, slice(64 * (h % 2), 64 * (h % 2) + 64)
                        ins = nc.vector.tensor_copy(m.mixed[q, 2 + c, TP_ + b * STEPS:TP_ + (b + 1) * STEPS],
                                                    back(b)[q, c, h * STEPS:(h + 1) * STEPS])
                    ins.then_inc(s.back_in, 1)

                mask_max(0)
                for b in range(REQ):
                    if b + 1 < REQ:
                        mask_max(b + 1)
                    if b:
                        collect(b - 1)
                    scale(b)
                collect(REQ - 1)


def rwkv_prepare(nc, m, r):
    rw = m.proj_rw[:]
    halves = [(c, half, slice(half * HALF, (half + 1) * HALF)) for c in range(PAIRS) for half in range(2)]
    with ExitStack() as ctx:
        diff = ctx.enter_context(sbuf(nc, "rw_diff", [P, NB_RW, T], F32))
        wd = ctx.enter_context(sbuf(nc, "rw_wd", [P, T], F32))
        sq = ctx.enter_context(sbuf(nc, "rw_sq", [P, PAIRS, T], F32))
        tmp = r.bonus
        shift = ctx.enter_context(sbuf(nc, "rw_shift", [P, NB_RW, REQ], F32))
        last_p = ctx.enter_context(sbuf(nc, "rw_last_p", [P, NB_RW, 1], F32))
        last_s = ctx.enter_context(sbuf(nc, "rw_last_s", [P, NB_RW, REQ], F32))
        mu = ctx.enter_context(sbuf(nc, "rw_mu", [P, NB_RW], F32))
        vec = r.vec
        wa_up = ctx.enter_context(sbuf(nc, "rw_wa", [P, PAIRS * P], F32))
        g_up = ctx.enter_context(sbuf(nc, "rw_g", [P, PAIRS * P], F32))
        ps = ctx.enter_context(psum(nc, "rw_ps", [P, 6, 512], F32))

        with stage(nc, "loaded", "shifted", "stored", "dve_step", "act_step", "gates_in", "w_up", "w_read",
                   "a_up", "a_read", "g_done", "g_read", "squared", "summed", "rooted", "prod", "bonus_sum",
                   "bonus_read", "decays", "scanned", "lasts", "lengths", "unit", "states_in") as (block, s):
            @block.sync
            def _(sp):
                for dst, src in ((shift[:], m.dram.state_shift[m.l]), (mu[:], m.dram.rwkv_mu[m.l]), (vec[:], m.dram.rwkv_vec[m.l]),
                                 (wa_up[:], m.dram.rwkv_wa[m.l]), (g_up[:], m.dram.rwkv_g[m.l])):
                    sp.dma_start(dst, src).then_inc(s.loaded, 16)
                sp.dma_start(r.states[:], m.dram.state_wkv[m.l]).then_inc(s.states_in, 16)
                sp.wait_ge(s.lasts, 2)
                sp.dma_start(m.dram.p_shift[m.l], last_p[:]).then_inc(s.stored, 16)
                sp.dma_start(m.dram.s_shift[m.l], last_s[:]).then_inc(s.stored, 16)
                sp.wait_ge(s.states_in, 16)
                sp.wait_ge(s.stored, 32)

            @block.tensor
            def _(pe):
                pe.wait_ge(s.gates_in, 1)
                for n, (c, half, t) in enumerate(halves):
                    ins = nc.tensor.matmul(ps[:, n, 0:HALF], wa_up[0:64, c * P:(c + 1) * P], wd[0:64, t],
                                           start=True, stop=True)
                ins.then_inc(s.w_up, 1)
                pe.wait_ge(s.w_read, 6)
                for n, (c, half, t) in enumerate(halves):
                    ins = nc.tensor.matmul(ps[:, n, 0:HALF], wa_up[64:P, c * P:(c + 1) * P], diff[64:P, 9, t],
                                           start=True, stop=True)
                ins.then_inc(s.a_up, 1)
                pe.wait_ge(s.a_read, 6)
                pe.wait_ge(s.gates_in, 2)
                for n, (c, half, t) in enumerate(halves):
                    ins = nc.tensor.matmul(ps[:, n, 0:HALF], g_up[:, c * P:(c + 1) * P], r.g[:, 0, t],
                                           start=True, stop=True)
                ins.then_inc(s.g_done, 1)
                pe.wait_ge(s.g_read, 6)
                pe.wait_ge(s.squared, 1)
                for n, (c, half, t) in enumerate(halves):
                    ins = nc.tensor.matmul(ps[:, n, 0:HALF], m.pair_ones[:], sq[:, c, t], start=True, stop=True)
                ins.then_inc(s.summed, 1)
                pe.wait_ge(s.rooted, 6)
                pe.wait_ge(s.prod, 1)
                for n, (c, half, t) in enumerate(halves):
                    ins = nc.tensor.matmul(ps[:, n, 0:HALF], m.pair_ones[:], tmp[:, c, t], start=True, stop=True)
                ins.then_inc(s.bonus_sum, 1)

            @block.scalar
            def _(act):
                nc.scalar.activation(last_p[:], rw[:, :, TP_ - 1:TP_], ACT.Copy).then_inc(s.lasts, 1)
                nc.scalar.activation(last_s[:], rw[:, :, TP_ + STEPS - 1:T:STEPS], ACT.Copy).then_inc(s.lasts, 1)
                act.wait_ge(s.shifted, 1)
                nc.scalar.activation(wd[0:64, :], diff[0:64, 9, :], ACT.Tanh).then_inc(s.gates_in, 1)
                nc.scalar.activation(r.g[:, 0, :], diff[:, 10, :], ACT.Sigmoid).then_inc(s.gates_in, 1)
                act.wait_ge(s.w_up, 1)
                for n, (c, half, t) in enumerate(halves):
                    nc.scalar.activation(r.ld[:, c, t], ps[:, n, 0:HALF], ACT.Sigmoid,
                                         bias=vec[:, W0, c:c + 1]).then_inc(s.w_read, 1)
                act.wait_ge(s.a_up, 1)
                for n, (c, half, t) in enumerate(halves):
                    nc.scalar.activation(r.b[:, c, t], ps[:, n, 0:HALF], ACT.Sigmoid,
                                         bias=vec[:, A0, c:c + 1]).then_inc(s.a_read, 1)
                act.wait_ge(s.g_done, 1)
                for n, (c, half, t) in enumerate(halves):
                    nc.scalar.activation(r.g[:, c, t], ps[:, n, 0:HALF], ACT.Copy).then_inc(s.g_read, 1)
                act.wait_ge(s.summed, 1)
                for n, (c, half, t) in enumerate(halves):
                    nc.scalar.activation(sq[:, c, t], ps[:, n, 0:HALF], ACT.Sqrt).then_inc(s.rooted, 1)
                act.wait_ge(s.scanned, 1)
                nc.scalar.activation(r.inv[:], r.cum[:], ACT.Exp, scale=-1.0).then_inc(s.decays, 1)
                nc.scalar.activation(r.end[:], r.end[:], ACT.Exp).then_inc(s.decays, 1)
                nc.scalar.activation(r.prev[:], r.prev[:], ACT.Exp).then_inc(s.decays, 1)
                act.wait_ge(s.decays, 1)
                nc.scalar.activation(r.cum[:], r.cum[:], ACT.Exp).then_inc(s.decays, 1)

            @block.gpsimd
            def _(pool):
                nc.gpsimd.memset(r.state[:], 0.0)
                for c in range(PAIRS):
                    pool.wait_ge(s.lengths, c + 1)
                    nc.gpsimd.tensor_tensor(r.kk[:, c, :], r.kk[:, c, :], sq[:, c, :], ALU.mult).then_inc(s.unit, 1)

            @block.vector
            def _(dve):
                st = Steps(dve, s.dve_step)

                def split(x, lo, hi):
                    return x[:, lo:hi, TP_:T].rearrange("p c (b t) -> p c b t", b=REQ)

                nc.vector.memset(r.o[TS_:P, NT - 1, :], 0.0)
                dve.wait_ge(s.loaded, 80)

                def shift_mix(lo, hi, out):
                    nc.vector.tensor_tensor(diff[:, lo:hi, 1:TP_], rw[:, lo:hi, 0:TP_ - 1], rw[:, lo:hi, 1:TP_],
                                            ALU.subtract)
                    nc.vector.tensor_scalar(diff[:, lo:hi, 0:1], rw[:, lo:hi, 0:1], -1.0, None, ALU.mult)
                    nc.vector.tensor_tensor(split(diff, lo, hi)[:, :, :, 1:STEPS],
                                            split(rw, lo, hi)[:, :, :, 0:STEPS - 1],
                                            split(rw, lo, hi)[:, :, :, 1:STEPS], ALU.subtract)
                    st.link(nc.vector.tensor_tensor(split(diff, lo, hi)[:, :, :, 0], shift[:, lo:hi],
                                                    split(rw, lo, hi)[:, :, :, 0], ALU.subtract))
                    for n in range(lo, hi):
                        ins = nc.vector.scalar_tensor_tensor(out=out(n), in0=diff[:, n, :], scalar=mu[:, n:n + 1],
                                                             in1=rw[:, n, :], op0=ALU.mult, op1=ALU.add)
                    return ins

                shift_mix(9, 11, lambda n: diff[:, n, :]).then_inc(s.shifted, 1)
                st.link(shift_mix(3, 6, lambda n: diff[:, n, :]))
                k_ = diff[:, 3:6, :]
                for c in range(PAIRS):
                    ins = nc.vector.tensor_scalar(r.kk[:, c, :], k_[:, c, :], vec[:, KK, c:c + 1], None, ALU.mult)
                st.link(ins)
                nc.vector.tensor_tensor(sq[:], r.kk[:], r.kk[:], ALU.mult).then_inc(s.squared, 1)
                shift_mix(0, 3, lambda n: r.r[:, n, :])
                st.link(shift_mix(6, 9, lambda n: r.v[:, n - 6, :]))
                dve.wait_ge(s.w_read, 6)
                st.link(nc.vector.tensor_scalar(r.ld[:], r.ld[:], -DECAY, None, ALU.mult))
                for c in range(PAIRS):
                    ins = nc.vector.tensor_tensor_scan(r.cum[:, c, :], m.chunk_reset[:], r.ld[:, c, :], 0.0,
                                                       ALU.mult, ALU.add)
                    st.link(ins)
                nc.vector.tensor_tensor(r.prev[:], r.cum[:], r.ld[:], ALU.subtract)
                for lo, hi, n, w in ((0, TP_, NCH, CH), (TP_, T, REQ, STEPS)):
                    for c in range(PAIRS):
                        cum = r.cum[:, c, lo:hi].rearrange("p (n w) -> p n w", n=n)
                        ins = nc.vector.tensor_tensor(r.end[:, c, lo:hi].rearrange("p (n w) -> p n w", n=n),
                                                      cum[:, :, w - 1:w].to_broadcast([P, n, w]), cum, ALU.subtract)
                ins.then_inc(s.scanned, 1)
                dve.wait_ge(s.a_read, 6)
                st.link(nc.vector.scalar_tensor_tensor(out=tmp[:], in0=r.b[:], scalar=-1.0, in1=k_,
                                                       op0=ALU.add, op1=ALU.mult))
                for c in range(PAIRS):
                    ins = nc.vector.scalar_tensor_tensor(out=r.k[:, c, :], in0=tmp[:, c, :], scalar=vec[:, KA, c:c + 1],
                                                         in1=k_[:, c, :], op0=ALU.mult, op1=ALU.add)
                st.link(ins)
                for c in range(PAIRS):
                    ins = nc.vector.scalar_tensor_tensor(out=tmp[:, c, :], in0=r.r[:, c, :], scalar=vec[:, RK, c:c + 1],
                                                         in1=r.k[:, c, :], op0=ALU.mult, op1=ALU.mult)
                ins.then_inc(s.prod, 1)
                dve.wait_ge(s.rooted, 6)
                st.link(nc.vector.tensor_scalar(sq[:], sq[:], 1e-12, None, ALU.max))
                for c in range(PAIRS):
                    nc.vector.reciprocal(sq[:, c, :], sq[:, c, :]).then_inc(s.lengths, 1)
                for c in range(PAIRS):
                    dve.wait_ge(s.unit, c + 1)
                    nc.vector.tensor_tensor(r.b[:, c, :], r.b[:, c, :], r.kk[:, c, :], ALU.mult)
                dve.wait_ge(s.bonus_sum, 1)
                for n, (c, half, t) in enumerate(halves):
                    nc.vector.tensor_tensor(r.bonus[:, c, t], ps[:, n, 0:HALF], r.v[:, c, t], ALU.mult)
                dve.wait_ge(s.decays, 4)


def rwkv_tile(nc, m, r, tile, w, masks, chunks):
    sample = chunks == 0
    t = bass.ds(tile * P, w)
    H3 = HEADS * HD
    step = STEPS if sample else CH
    nch = w // step
    levels = step.bit_length() - 2
    ACT_UV = 3
    with ExitStack() as ctx:
        def sb(name, shape):
            return ctx.enter_context(sbuf(nc, name, shape, F32))

        kr = sb("rt_kr", [P, PAIRS, 2, w])
        ki, bi = sb("rt_ki", [P, PAIRS, w]), sb("rt_bi", [P, PAIRS, w])
        ke, be, vs = sb("rt_ke", [P, PAIRS, w]), sb("rt_be", [P, PAIRS, w]), sb("rt_vs", [P, PAIRS, w])
        dc = sb("rt_dc", [P, PAIRS, REQ])
        tok = sb("rt_tok", [w, 4, H3])
        n_m = sb("rt_n", [w, HEADS, 2, w])
        qb = sb("rt_qb", [w, HEADS, w])
        bq = sb("rt_bq", [w, HEADS, 2, w])
        tt = sb("rt_tt", [w, HEADS, w])
        bv, uv = sb("rt_bv", [w, HEADS, HD]), sb("rt_uv", [w, HEADS, HD])
        wt = sb("rt_wt", [P, PAIRS, w])
        u = sb("rt_u", [w, HEADS, HD])
        o = r.o[0:w, bass.ds(tile, 1), :].rearrange("p a (h i) -> p (a h) i", h=HEADS)
        if sample:
            ux, vx, ox = (sb("rt_" + n, [w, 2, REQ, HD]) for n in ("ux", "vx", "ox"))
        ps = ctx.enter_context(psum(nc, "rt_ps", [P, 8, 512], F32))
        pos = lambda h: (h // 2, 64 * (h % 2))
        strict_incl, neg_strict_incl, neg_lower = masks
        names = ["staged", "v_staged", "turned", "turned_in", "gram", "gram_in", "powers", "powers_in", "folded",
                 "added", "bv_made", "bv_in", "uv_made", "uv_act", "uv_dve", "u_made", "u_in", "vx_in", "o_made",
                 "o_in", "st_made", "st_in", "intra", "dve_step"]

        def move_uv(copy, h):
            c, q = pos(h)
            copy(uv[:, h, :], ps[0:w, h, 64:128])
            return copy(wt[q:q + 64, c, :], ps[q:q + 64, h, 256:256 + w])

        with stage(nc, *names) as (block, s):
            @block.vector
            def _(dve):
                st = Steps(dve, s.dve_step)
                nc.vector.tensor_tensor(kr[:, :, 0, :], r.kk[:, :, t], r.prev[:, :, t], ALU.mult)
                nc.vector.tensor_tensor(kr[:, :, 1, :], r.r[:, :, t], r.cum[:, :, t], ALU.mult)
                nc.vector.tensor_tensor(bi[:], r.b[:, :, t], r.inv[:, :, t], ALU.mult)
                nc.vector.tensor_tensor(ki[:], r.k[:, :, t], r.inv[:, :, t], ALU.mult).then_inc(s.staged, 1)
                for c in range(PAIRS):
                    nc.vector.tensor_copy(dc[:, c, 0:nch].unsqueeze(2),
                                          r.cum[:, c, t].rearrange("p (n w) -> p n w", w=step)[:, :, step - 1:step])
                nc.vector.tensor_tensor(ke[:], r.k[:, :, t], r.end[:, :, t], ALU.mult)
                nc.vector.scalar_tensor_tensor(out=be[:], in0=r.b[:, :, t], scalar=-1.0, in1=r.end[:, :, t],
                                               op0=ALU.mult, op1=ALU.mult).then_inc(s.staged, 1)
                for h in range(HEADS):
                    dve.wait_ge(s.gram, h + 1)
                    st.link(nc.vector.tensor_tensor(n_m[:, h, 0, :], ps[0:w, h, 0:w], neg_strict_incl[0:w, 0, 0:w],
                                                    ALU.mult))
                    nc.vector.tensor_tensor(n_m[:, h, 1, :], ps[0:w, 6 + h % 2, 0:w], neg_lower[0:w, 0:w], ALU.mult)
                    nc.vector.tensor_tensor(qb[:, h, :], ps[0:w, h, w:2 * w], neg_strict_incl[0:w, 1, 0:w], ALU.mult)
                    nc.vector.tensor_tensor(bq[:, h, :, :], ps[0:w, h, 2 * w:4 * w].rearrange("p (a w) -> p a w", a=2),
                                            strict_incl[0:w, :, 0:w], ALU.mult)
                    nc.vector.tensor_tensor(tt[:, h, :], n_m[:, h, 0, :], m.ident[0:w, 0:w],
                                            ALU.add).then_inc(s.gram_in, 1)
                for k in range(levels):
                    for h in range(HEADS):
                        dve.wait_ge(s.folded, HEADS * k + h + 1)
                        nc.vector.tensor_tensor(tt[:, h, :], tt[:, h, :], ps[0:w, h, 2 * w:3 * w],
                                                ALU.add).then_inc(s.added, 1)
                for h in range(ACT_UV, HEADS):
                    dve.wait_ge(s.uv_made, h + 1)
                    move_uv(nc.vector.tensor_copy, h).then_inc(s.uv_dve, 1)
                dve.wait_ge(s.uv_act, ACT_UV)
                if not sample:
                    for n in range(chunks):
                        q = slice(n * CH, (n + 1) * CH)
                        dve.wait_ge(s.u_made, n + 1)
                        heads = lambda x: x[q, :, :].rearrange("p (c a) i -> p c a i", a=2)
                        nc.vector.tensor_tensor(heads(u), heads(uv),
                                                ps[q, 0:2, 0:PAIRS * HD].rearrange("p a (c i) -> p c a i", c=PAIRS),
                                                ALU.add).then_inc(s.u_in, 1)
                        dve.wait_ge(s.o_made, n + 1)
                        st.link(nc.vector.tensor_tensor(r.state[:], r.state[:],
                                                        dc[:, :, n:n + 1].to_broadcast([P, PAIRS, HD]), ALU.mult))
                        dve.wait_ge(s.st_made, n + 1)
                        nc.vector.tensor_tensor(r.state[:], r.state[:],
                                                ps[:, 2, 0:PAIRS * HD].rearrange("p (c i) -> p c i", c=PAIRS),
                                                ALU.add).then_inc(s.st_in, 1)
                        dve.wait_ge(s.st_in, n + 1)
                    dve.wait_ge(s.o_in, chunks)
                else:
                    own = m.own_req[:, :].unsqueeze(2).to_broadcast([w, REQ, HD])

                    def request_u(h):
                        p = h % 2
                        dve.wait_ge(s.u_made, h + 1)
                        if h >= 2:
                            dve.wait_ge(s.st_made, h - 1)
                        st.link(nc.vector.tensor_tensor(
                            ux[:, p], ps[0:w, 4 * p, :].rearrange("p (b i) -> p b i", b=REQ),
                            uv[:, h, :].unsqueeze(1).to_broadcast([w, REQ, HD]), ALU.add))
                        st.link(nc.vector.tensor_tensor(ux[:, p], ux[:, p], own, ALU.mult))
                        nc.vector.tensor_tensor(vx[:, p], tok[:, 3, h * HD:(h + 1) * HD].unsqueeze(1)
                                                .to_broadcast([w, REQ, HD]), own, ALU.mult).then_inc(s.u_in, 1)
                        nc.vector.tensor_reduce(u[:, h, :], ux[:, p].rearrange("p b i -> p i b"), X, ALU.add)
                        st.link(nc.vector.tensor_tensor(
                            ox[:, p], ps[0:w, 4 * p + 1, :].rearrange("p (b i) -> p b i", b=REQ), own, ALU.mult))
                        nc.vector.tensor_reduce(o[:, h, :], ox[:, p].rearrange("p b i -> p i b"), X,
                                                ALU.add).then_inc(s.o_in, 1)

                    def request_state(h):
                        c, q = pos(h)
                        state = r.states[q:q + 64, c, :, :]
                        st.link(nc.vector.tensor_tensor(state, state, dc[q:q + 64, c, :].unsqueeze(2)
                                                        .to_broadcast([64, REQ, HD]), ALU.mult))
                        dve.wait_ge(s.st_made, h + 1)
                        nc.vector.tensor_tensor(state, state,
                                                ps[q:q + 64, 4 * (h % 2) + 2, :].rearrange("p (b i) -> p b i", b=REQ),
                                                ALU.add).then_inc(s.st_in, 1)

                    for h in range(HEADS):
                        request_u(h)
                        if h:
                            request_state(h - 1)
                    request_state(HEADS - 1)
                    dve.wait_ge(s.o_in, HEADS)
                dve.wait_ge(s.intra, 1)
                nc.vector.tensor_tensor(o, o, ps[0:w, 3, 0:H3].rearrange("p (h i) -> p h i", h=HEADS), ALU.add)

            @block.scalar
            def _(act):
                def copy(out, src):
                    return nc.scalar.activation(out, src, ACT.Copy)

                copy(vs[:], r.v[:, :, t]).then_inc(s.v_staged, 1)
                for i in range(4):
                    act.wait_ge(s.turned, i + 1)
                    copy(tok[:, i, :], ps[0:w, 2 + i, 0:H3]).then_inc(s.turned_in, 1)
                for h in range(HEADS):
                    act.wait_ge(s.bv_made, h + 1)
                    copy(bv[:, h, :], ps[0:w, h, 3 * w:3 * w + HD]).then_inc(s.bv_in, 1)
                for k in range(levels):
                    a = slice(0, 2) if k < levels - 1 else slice(1, 2)
                    for h in range(HEADS):
                        act.wait_ge(s.powers, HEADS * k + h + 1)
                        copy(n_m[:, h, a, :], ps[0:w, h, 0:2 * w].rearrange("p (a w) -> p a w", a=2)[:, a, :]
                             ).then_inc(s.powers_in, 1)
                for h in range(ACT_UV):
                    act.wait_ge(s.uv_made, h + 1)
                    move_uv(copy, h).then_inc(s.uv_act, 1)
                for n in range(chunks):
                    q = slice(n * CH, (n + 1) * CH)
                    act.wait_ge(s.o_made, n + 1)
                    for a in range(2):
                        ins = copy(o[q, :, :].rearrange("p (c a) i -> p a c i", a=2)[:, a],
                                   ps[q, 4 + a, 0:PAIRS * HD].rearrange("p (c i) -> p c i", c=PAIRS))
                    ins.then_inc(s.o_in, 1)

            @block.tensor
            def _(pe):
                def gram(h):
                    c, q = pos(h)
                    q = slice(q, q + 64)
                    both = kr[q, c, :, :].rearrange("p a w -> p (a w)")
                    nc.tensor.matmul(ps[0:w, h, 0:2 * w], bi[q, c, :], both, start=True, stop=True)
                    nc.tensor.matmul(ps[0:w, h, 2 * w:4 * w], ki[q, c, :], both, start=True, stop=True)
                    nc.tensor.matmul(ps[0:w, 6 + h % 2, 0:w], kr[q, c, 0, :], bi[q, c, :],
                                     start=True, stop=True).then_inc(s.gram, 1)

                pe.wait_ge(s.staged, 1)
                gram(0)
                gram(1)
                pe.wait_ge(s.staged, 2)
                pe.wait_ge(s.v_staged, 1)
                for i, src in enumerate((kr[:, :, 0, :], ke[:], be[:], vs[:])):
                    for c in range(PAIRS):
                        ins = nc.tensor.transpose(ps[0:w, 2 + i, c * P:(c + 1) * P], src[:, c, :], m.ident[:])
                    ins.then_inc(s.turned, 1)
                for h in range(HEADS):
                    pe.wait_ge(s.gram_in, h + 1)
                    if h + 2 < HEADS:
                        pe.wait_ge(s.turned_in, h + 1)
                        gram(h + 2)
                    else:
                        pe.wait_ge(s.turned_in, 4)
                        for j in (range(HEADS - 1) if h == HEADS - 2 else (HEADS - 1,)):
                            nc.tensor.matmul(ps[0:w, j, 3 * w:3 * w + HD], bq[:, j, 0, :],
                                             tok[:, 3, j * HD:(j + 1) * HD],
                                             start=True, stop=True).then_inc(s.bv_made, 1)
                for k in range(levels):
                    for h in range(HEADS):
                        if k == 0:
                            pe.wait_ge(s.bv_in, h + 1)
                        else:
                            pe.wait_ge(s.added, HEADS * (k - 1) + h + 1)
                        if k < levels - 1:
                            nc.tensor.matmul(ps[0:w, h, 0:w], n_m[:, h, 1, :], n_m[:, h, 0, :], start=True, stop=True)
                        nc.tensor.matmul(ps[0:w, h, w:2 * w], n_m[:, h, 0, :], n_m[:, h, 1, :],
                                         start=True, stop=True).then_inc(s.powers, 1)
                    for h in range(HEADS):
                        pe.wait_ge(s.powers_in, HEADS * k + h + 1)
                        nc.tensor.matmul(ps[0:w, h, 2 * w:3 * w], n_m[:, h, 1, :], tt[:, h, :],
                                         start=True, stop=True).then_inc(s.folded, 1)
                for h in range(HEADS):
                    c, q = pos(h)
                    pe.wait_ge(s.added, HEADS * (levels - 1) + h + 1)
                    nc.tensor.matmul(ps[0:w, h, 64:128], tt[:, h, :], bv[:, h, :], start=True, stop=True)
                    nc.tensor.matmul(ps[q:q + 64, h, 256:256 + w], tok[:, 0, h * HD:(h + 1) * HD], tt[:, h, :],
                                     start=True, stop=True).then_inc(s.uv_made, 1)
                pe.wait_ge(s.uv_act, ACT_UV)
                pe.wait_ge(s.uv_dve, HEADS - ACT_UV)
                if not sample:
                    for n in range(chunks):
                        tc = slice(n * CH, (n + 1) * CH)

                        def by_state(bank, of):
                            for h in range(HEADS):
                                c, q = pos(h)
                                q = slice(q, q + 64)
                                ins = nc.tensor.matmul(ps[tc, bank + h % 2, c * HD:(c + 1) * HD], of(q, c),
                                                       r.state[q, c, :], start=True, stop=True)
                            return ins

                        if n:
                            pe.wait_ge(s.st_in, n)
                        by_state(0, lambda q, c: wt[q, c, tc]).then_inc(s.u_made, 1)
                        by_state(4, lambda q, c: kr[q, c, 1, tc]).then_inc(s.o_made, 1)
                        pe.wait_ge(s.u_in, n + 1)
                        for h in range(HEADS):
                            c, q = pos(h)
                            out = ps[q:q + 64, 2, c * HD:(c + 1) * HD]
                            nc.tensor.matmul(out, tok[tc, 1, h * HD:(h + 1) * HD], tok[tc, 3, h * HD:(h + 1) * HD],
                                             start=True, stop=False)
                            ins = nc.tensor.matmul(out, tok[tc, 2, h * HD:(h + 1) * HD], u[tc, h, :],
                                                   start=False, stop=True)
                        ins.then_inc(s.st_made, 1)
                else:
                    def by_states(h):
                        c, q = pos(h)
                        q, p = slice(q, q + 64), 4 * (h % 2)
                        if h >= 2:
                            pe.wait_ge(s.o_in, h - 1)
                        state = r.states[q, c, :, :].rearrange("p b i -> p (b i)")
                        nc.tensor.matmul(ps[0:w, p, :], wt[q, c, :], state, start=True, stop=True)
                        nc.tensor.matmul(ps[0:w, p + 1, :], kr[q, c, 1, :], state, start=True,
                                         stop=True).then_inc(s.u_made, 1)

                    by_states(0)
                    for h in range(HEADS):
                        c, q = pos(h)
                        q, p = slice(q, q + 64), h % 2
                        if h + 1 < HEADS:
                            by_states(h + 1)
                        pe.wait_ge(s.u_in, h + 1)
                        if h >= 2:
                            pe.wait_ge(s.st_in, h - 1)
                        nc.tensor.matmul(ps[q, 4 * p + 2, :], tok[:, 1, h * HD:(h + 1) * HD],
                                         vx[:, p].rearrange("p b i -> p (b i)"), start=True, stop=False)
                        nc.tensor.matmul(ps[q, 4 * p + 2, :], tok[:, 2, h * HD:(h + 1) * HD],
                                         ux[:, p].rearrange("p b i -> p (b i)"), start=False,
                                         stop=True).then_inc(s.st_made, 1)
                    pe.wait_ge(s.o_in, HEADS)
                for h in range(HEADS):
                    out = ps[0:w, 3, h * HD:(h + 1) * HD]
                    nc.tensor.matmul(out, qb[:, h, :], u[:, h, :], start=True, stop=False)
                    ins = nc.tensor.matmul(out, bq[:, h, 1, :], tok[:, 3, h * HD:(h + 1) * HD],
                                           start=False, stop=True)
                ins.then_inc(s.intra, 1)


def rwkv_out(nc, m, r):
    NHT = NT * HEADS
    with ExitStack() as ctx:
        osq = ctx.enter_context(sbuf(nc, "ro_sq", [P, NHT, HD], F32))
        stat = ctx.enter_context(sbuf(nc, "ro_stat", [P, 4, NHT], F32))
        ps = ctx.enter_context(psum(nc, "ro_ps", [P, PAIRS, 2, 512], F32))
        o = r.o[:].rearrange("p n (h i) -> p (n h) i", h=HEADS)
        wide = lambda n: stat[:, n, :].unsqueeze(2).to_broadcast([P, NHT, HD])
        with stage(nc, "stored", "centred", "squared", "varied", "rooted", "normed", "back", "scaled",
                   "dve_step") as (block, s):
            @block.sync
            def _(sp):
                sp.dma_start(m.dram.p_wkv[m.l], r.state[:]).then_inc(s.stored, 16)
                sp.dma_start(m.dram.s_wkv[m.l], r.states[:]).then_inc(s.stored, 16)
                sp.wait_ge(s.stored, 32)

            @block.vector
            def _(dve):
                st = Steps(dve, s.dve_step)
                st.link(nc.vector.tensor_reduce(stat[:, 0, :], o, X, ALU.add))
                st.link(nc.vector.tensor_scalar(stat[:, 0, :], stat[:, 0, :], -1.0 / HD, None, ALU.mult))
                nc.vector.tensor_tensor(o, o, wide(0), ALU.add).then_inc(s.centred, 1)
                dve.wait_ge(s.squared, 1)
                st.link(nc.vector.tensor_reduce(stat[:, 1, :], osq[:], X, ALU.add))
                nc.vector.tensor_scalar(stat[:, 1, :], stat[:, 1, :], 1.0 / HD, GN_EPS, ALU.mult,
                                        ALU.add).then_inc(s.varied, 1)
                dve.wait_ge(s.rooted, 1)
                st.link(nc.vector.reciprocal(stat[:, 3, :], stat[:, 2, :]))
                nc.vector.tensor_tensor(o, o, wide(3), ALU.mult).then_inc(s.normed, 1)
                for c in range(PAIRS):
                    out = m.mixed[:, 5 + c, :]
                    dve.wait_ge(s.scaled, c + 1)
                    st.link(nc.vector.tensor_tensor(out, out, r.bonus[:, c, :], ALU.add))
                    nc.vector.tensor_tensor(out, out, r.g[:, c, :], ALU.mult)

            @block.scalar
            def _(act):
                act.wait_ge(s.centred, 1)
                nc.scalar.activation(osq[:], o, ACT.Square).then_inc(s.squared, 1)
                act.wait_ge(s.varied, 1)
                nc.scalar.activation(stat[:, 2, :], stat[:, 1, :], ACT.Sqrt).then_inc(s.rooted, 1)
                for c in range(PAIRS):
                    act.wait_ge(s.back, c + 1)
                    for part, t in ((0, slice(0, TP_)), (1, slice(TP_, T))):
                        ins = nc.scalar.activation(m.mixed[:, 5 + c, t], ps[:, c, part, 0:t.stop - t.start],
                                                   ACT.Identity, bias=r.vec[:, GN_B, c:c + 1], scale=r.vec[:, GN_W, c:c + 1])
                    ins.then_inc(s.scaled, 1)

            @block.tensor
            def _(pe):
                pe.wait_ge(s.normed, 1)
                for c in range(PAIRS):
                    for i, rows in enumerate(ROWS):
                        ins = nc.tensor.transpose(ps[:, c, i // 4, (i % 4) * P:(i % 4) * P + rows],
                                                  r.o[0:rows, i, c * P:(c + 1) * P], m.ident[0:rows, 0:rows])
                    ins.then_inc(s.back, 1)


def rwkv(nc, m):
    with ExitStack() as ctx:
        def sb(name, shape):
            return ctx.enter_context(sbuf(nc, name, shape, F32))

        r = Parts()
        r.r, r.k, r.v, r.kk, r.b, r.g, r.bonus = (sb("rwkv_" + n, [P, PAIRS, T])
                                                  for n in ("r", "k", "v", "kk", "b", "g", "bonus"))
        r.ld, r.cum, r.prev, r.inv, r.end = (sb("rwkv_" + n, [P, PAIRS, T])
                                             for n in ("ld", "cum", "prev", "inv", "end"))
        r.state = sb("rwkv_state", [P, PAIRS, HD])
        r.states = sb("rwkv_states", [P, PAIRS, REQ, HD])
        r.o = sb("rwkv_o", [P, NT, HEADS * HD])
        r.vec = sb("rwkv_vec", [P, 7, PAIRS])
        rwkv_prepare(nc, m, r)
        with nc.Fori(0, TP_ // P) as i:
            rwkv_tile(nc, m, r, i, P, m.masks_prompt, P // CH)
        rwkv_tile(nc, m, r, TP_ // P, TS_, m.masks_sample, 0)
        rwkv_out(nc, m, r)


def mix_out(nc, m):
    with ExitStack() as ctx:
        w = ctx.enter_context(sbuf(nc, "out_w", [P, KD, D], F32))
        w_hi = ctx.enter_context(sbuf(nc, "out_w_hi", [P, KD, D], F32R))
        w_lo = ctx.enter_context(sbuf(nc, "out_w_lo", [P, KD, D], F32R))
        x_hi = ctx.enter_context(sbuf(nc, "out_x_hi", [P, KD, T], F32R))
        x_lo = ctx.enter_context(sbuf(nc, "out_x_lo", [P, KD, T], F32R))
        ps = ctx.enter_context(psum(nc, "out_ps", [P, 8, 512], F32))
        with stage(nc, "loaded0", "loaded1", "hi", "lo", "made", "added") as (block, s):
            loaded = (s.loaded0, s.loaded1)

            @block.sync
            def _(sp):
                for n in range(2):
                    q = slice(4 * n, 4 * n + 4)
                    sp.dma_start(w[:, q], m.dram.w_out[m.l, :, q]).then_inc(loaded[n], 16)

            @block.scalar
            def _(act):
                for k in range(KD):
                    nc.scalar.activation(x_hi[:, k], m.mixed[:, k], ACT.Copy)
                    act.wait_ge(loaded[k // 4], 16)
                    nc.scalar.activation(w_hi[:, k], w[:, k], ACT.Copy).then_inc(s.hi, 1)

            @block.tensor
            def _(pe):
                def products(n, k):
                    i, half, rows = n // 2, n % 2, ROWS[n // 2]
                    t, c = slice(i * P, i * P + rows), slice(half * 512, (half + 1) * 512)
                    return three_passes(nc, ps[0:rows, n % 8, :], x_hi[:, k, t], x_lo[:, k, t],
                                        w_hi[:, k, c], w_lo[:, k, c], k == 0, k == KD - 1)

                for k in range(KD):
                    pe.wait_ge(s.lo, k + 1)
                    for n in range(8):
                        ins = products(n, k)
                        if k == KD - 1:
                            ins.then_inc(s.made, 1)
                for n in range(8, 2 * NT):
                    pe.wait_ge(s.added, n - 7)
                    for k in range(KD):
                        ins = products(n, k)
                    ins.then_inc(s.made, 1)

            @block.vector
            def _(dve):
                for k in range(KD):
                    dve.wait_ge(s.hi, k + 1)
                    nc.vector.tensor_tensor(x_lo[:, k], m.mixed[:, k], x_hi[:, k].bitcast(F32), ALU.subtract)
                    nc.vector.tensor_tensor(w_lo[:, k], w[:, k], w_hi[:, k].bitcast(F32),
                                            ALU.subtract).then_inc(s.lo, 1)
                for n in range(2 * NT):
                    i, half, rows = n // 2, n % 2, ROWS[n // 2]
                    dve.wait_ge(s.made, n + 1)
                    hh = m.h[0:rows, i, half * 512:(half + 1) * 512]
                    nc.vector.tensor_tensor(hh, hh, ps[0:rows, n % 8, :], ALU.add).then_inc(s.added, 1)


def top_keys(nc, L, r, h, par):
    def top16(n, values, spare, best, where):
        for u in range(n):
            ins = nc.vector.max(best(u)[:, 0:8], values(u))
        L(ins)
        for u in range(n):
            nc.vector.max_index(where(u)[:, 0:8], best(u)[:, 0:8], values(u))
            ins = nc.vector.match_replace(spare(u), best(u)[:, 0:8], values(u), -3.0e38)
        L(ins)
        for u in range(n):
            ins = nc.vector.max(best(u)[:, 8:16], spare(u))
        L(ins)
        for u in range(n):
            ins = nc.vector.max_index(where(u)[:, 8:16], best(u)[:, 8:16], spare(u))
        L(ins)

    top16(2 * NT, lambda u: r.sc[par][:, u, :], lambda u: r.spare[:, u, :],
          lambda u: r.top[:, u // 2, u % 2, :], lambda u: r.idx[:, u // 2, u % 2, :])
    nc.vector.tensor_copy(r.idxf[par][:], r.idx[:])
    at = 0
    for lo, hi, width in CANDIDATES:
        n = (hi - lo) * width
        ins = nc.vector.tensor_tensor(
            r.cand[:, :, at:at + n].rearrange("p i (a b) -> p i a b", b=width),
            r.top[:, :, 0, lo:hi].unsqueeze(3).to_broadcast([P, NT, hi - lo, width]),
            r.top[:, :, 1, 0:width].unsqueeze(2).to_broadcast([P, NT, hi - lo, width]), ALU.add)
        at += n
    L(ins)
    top16(NT, lambda u: r.cand[:, u, :], lambda u: r.cand2[:, u, :],
          lambda u: r.best[:, u, :], lambda u: r.place[par][:, u, :])
    nc.vector.tensor_copy(r.out[:, 2, :, bass.ds(h, 1), :], r.best[:].unsqueeze(2))


def find_slots(nc, L, r, par):
    place = r.place[par][:].rearrange("p i k -> p (i k)")
    pf, a, start, start2 = (r.dec[:, n, :] for n in range(4))
    nc.vector.tensor_scalar(r.shifted[:, 0], place, 3, None, ALU.logical_shift_right)
    nc.vector.tensor_scalar(r.shifted[:, 1], place, 2, None, ALU.logical_shift_right)
    L(nc.vector.tensor_copy(pf, place))
    L(nc.vector.tensor_copy(r.shiftedf[:], r.shifted[:]))
    L(nc.vector.tensor_scalar(a, r.shiftedf[:, 0], 1.0, 0.0, ALU.subtract, ALU.max))
    L(nc.vector.scalar_tensor_tensor(out=a, in0=r.shiftedf[:, 1], scalar=-6.0, in1=a, op0=ALU.add, op1=ALU.max))
    L(nc.vector.scalar_tensor_tensor(out=a, in0=pf, scalar=-48.0, in1=a, op0=ALU.add, op1=ALU.max))
    nc.vector.tensor_copy(r.slot[:, 0], a)
    nc.vector.tensor_scalar(start, a, 8.0, 8.0, ALU.mult, ALU.add)
    L(nc.vector.tensor_scalar(start2, a, 4.0, 24.0, ALU.mult, ALU.add))
    nc.vector.scalar_tensor_tensor(out=start, in0=a, scalar=16.0, in1=start, op0=ALU.mult, op1=ALU.min)
    L(nc.vector.scalar_tensor_tensor(out=start2, in0=a, scalar=48.0, in1=start2, op0=ALU.add, op1=ALU.min))
    L(nc.vector.tensor_tensor(start, start, start2, ALU.min))
    L(nc.vector.tensor_tensor(r.slot[:, 1], pf, start, ALU.subtract))
    for n in range(2):
        ins = nc.vector.tensor_tensor(r.eq[:, n], r.slot[:, n].unsqueeze(1).to_broadcast([P, TOPK, NT * TOPK]),
                                      r.slots[:], ALU.is_equal)
    return ins


def route(nc, m, r, i1T, i2T, gT):
    with ExitStack() as ctx:
        def sb(name, shape, dt=F32):
            return ctx.enter_context(sbuf(nc, name, shape, dt))

        r.keys = sb("rt_keys", [P, 2, NKEY])
        r.q = sb("rt_q", [P, 2, TPAD])
        r.sc = [sb("rt_sc", [P, 2 * NT, NKEY]) for _ in range(2)]
        r.spare = sb("rt_spare", [P, 2 * NT, NKEY])
        r.top = sb("rt_top", [P, NT, 2, TOPK])
        r.idx = sb("rt_idx", [P, NT, 2, TOPK], U32)
        r.idxf = [sb("rt_idxf", [P, NT, 2, TOPK], BF16) for _ in range(2)]
        r.cand, r.cand2 = sb("rt_cand", [P, NT, NCAND]), sb("rt_cand2", [P, NT, NCAND])
        r.best = sb("rt_best", [P, NT, TOPK])
        r.place = [sb("rt_place", [P, NT, TOPK], U32) for _ in range(2)]
        r.shifted, r.shiftedf = sb("rt_shift", [P, 2, NT * TOPK], U32), sb("rt_shiftf", [P, 2, NT * TOPK])
        r.dec = sb("rt_dec", [P, 4, NT * TOPK])
        r.slot = sb("rt_slot", [P, 2, NT * TOPK], BF16)
        r.slots = sb("rt_slots", [P, TOPK, NT * TOPK], BF16)
        r.eq, r.picked = (sb("rt_" + n, [P, 2, TOPK, NT * TOPK], BF16) for n in ("eq", "picked"))
        r.out = sb("rt_out", [P, 3, NT, PH, TOPK])
        gs = sb("rt_gs", [P, 2, NT * PH])
        r.q_ps = ctx.enter_context(psum(nc, "rt_qps", [P, 4, 512], F32))
        r.s_ps = ctx.enter_context(psum(nc, "rt_sps", [P, 12, NKEY], F32))
        tps = ctx.enter_context(psum(nc, "rt_tps", [P, 3, P], F32))
        names = ["w_in", "keys_in", "w_hi", "made", "q_in", "scored", "hot", "picked", "padded", "dve_step", "pool_step"]

        def turn(find, par, make=None, split=None, look=None):
            with stage(nc, *names) as (block, s):
                @block.sync
                def _(sp):
                    if make is not None:
                        sp.dma_start(r.keys[:], m.dram.peer_keys[m.l, make]).then_inc(s.keys_in, 16)
                    if split is not None:
                        sp.dma_start(r.w[:], m.dram.peer_wq[m.l, bass.ds(split * 2, 2)]
                                     .rearrange("b p k c -> p b k c")).then_inc(s.w_in, 16)

                @block.tensor
                def _(pe):
                    if make is None:
                        return
                    w_hi, w_lo = r.w_hi[1 - par], r.w_lo[1 - par]
                    for j in range(2):
                        for half in range(2):
                            t = slice(half * HALF, (half + 1) * HALF)
                            for k in range(KD):
                                ins = three_passes(nc, r.q_ps[:, 2 * j + half, 0:HALF], w_hi[:, j, k, :],
                                                   w_lo[:, j, k, :], m.x_hi[:, k, t], m.x_lo[:, k, t],
                                                   k == 0, k == KD - 1)
                            ins.then_inc(s.made, 1)
                    pe.wait_ge(s.keys_in, 16)
                    pe.wait_ge(s.q_in, 4)
                    if find is None:
                        pe.wait_ge(s.padded, 1)
                    for n in range(2 * NT):
                        i, a = n // 2, n % 2
                        ins = nc.tensor.matmul(r.s_ps[:, n, :], r.q[:, a, i * P:(i + 1) * P], r.keys[:, a, :],
                                               start=True, stop=True)
                        if n % 4 == 3 or n == 2 * NT - 1:
                            ins.then_inc(s.scored, 1)

                @block.scalar
                def _(act):
                    if split is not None:
                        act.wait_ge(s.w_in, 16)
                        for j in range(2):
                            nc.scalar.activation(r.w_hi[par][:, j], r.w[:, j], ACT.Copy).then_inc(s.w_hi, 1)
                    if make is not None:
                        for n in range(4):
                            act.wait_ge(s.made, n + 1)
                            nc.scalar.activation(r.q[:, n // 2, (n % 2) * HALF:(n % 2 + 1) * HALF],
                                                 r.q_ps[:, n, 0:HALF], ACT.Copy).then_inc(s.q_in, 1)
                        for n in range(3):
                            c = slice(4 * n, min(4 * n + 4, 2 * NT))
                            act.wait_ge(s.scored, n + 1)
                            nc.scalar.activation(r.sc[1 - par][:, c, :], r.s_ps[:, c, :], ACT.Copy)

                @block.gpsimd
                def _(pool):
                    G = Steps(pool, s.pool_step).link
                    if look is not None:
                        pool.wait_ge(s.hot, 1)
                        for a in range(2):
                            ins = nc.gpsimd.tensor_tensor(
                                r.picked[:, a].rearrange("p n (i k) -> p n i k", k=TOPK),
                                r.eq[:, a].rearrange("p n (i k) -> p n i k", k=TOPK),
                                r.idxf[1 - par][:, :, a, :].rearrange("p i n -> p n i").unsqueeze(3)
                                .to_broadcast([P, TOPK, NT, TOPK]), ALU.mult)
                        G(ins)
                    if split is not None:
                        for j in range(2):
                            pool.wait_ge(s.w_hi, j + 1)
                            nc.gpsimd.tensor_tensor(r.w_lo[par][:, j], r.w[:, j], r.w_hi[par][:, j].bitcast(F32),
                                                    ALU.subtract)
                    if look is not None:
                        for n in (TOPK // 2, TOPK // 4):
                            ins = nc.gpsimd.tensor_tensor(r.picked[:, :, 0:n], r.picked[:, :, 0:n],
                                                          r.picked[:, :, n:2 * n], ALU.add)
                            if n > TOPK // 4:
                                G(ins)
                        ins.then_inc(s.picked, 1)

                @block.vector
                def _(dve):
                    L = Steps(dve, s.dve_step).link
                    if look is not None:
                        find_slots(nc, L, r, 1 - par).then_inc(s.hot, 1)
                    if find is not None:
                        top_keys(nc, L, r, find, par)
                    elif look is None:
                        nc.vector.memset(r.q[:, :, T:TPAD], 0.0)
                        nc.vector.tensor_copy(r.slots[:], m.iota[:, 0:TOPK].unsqueeze(2)
                                              .to_broadcast([P, TOPK, NT * TOPK])).then_inc(s.padded, 1)
                    if look is not None:
                        dve.wait_ge(s.picked, 1)
                        for a in range(2):
                            nc.vector.tensor_reduce(r.out[:, a, :, bass.ds(look, 1), :],
                                                    r.picked[:, a, 0:TOPK // 4]
                                                    .rearrange("p n (i k) -> p i k n", k=TOPK),
                                                    X, ALU.add)

        turn(None, 1, make=0, split=1)
        turn(0, 0, make=1, split=2)
        with nc.Fori(0, (PH - 3) // 2) as i:
            turn(i * 2 + 1, 1, make=i * 2 + 2, split=i * 2 + 3, look=i * 2)
            turn(i * 2 + 2, 0, make=i * 2 + 3, split=i * 2 + 4, look=i * 2 + 1)
        turn(PH - 3, 1, make=PH - 2, split=PH - 1, look=PH - 4)
        turn(PH - 2, 0, make=PH - 1, look=PH - 3)
        turn(PH - 1, 1, look=PH - 2)
        turn(None, 0, look=PH - 1)
        with stage(nc, "dve_step", "centred", "expd", "outs", "turned", "turned_in") as (block, s):
            score = r.out[:, 2].rearrange("p i h k -> p (i h) k")

            def bank(i):
                return tps[:, :, :] if i % 2 == 0 else r.q_ps[:, 0, 0:3 * P].rearrange("p (n c) -> p n c", n=3)

            @block.scalar
            def _(act):
                act.wait_ge(s.centred, 1)
                nc.scalar.activation(score, score, ACT.Exp).then_inc(s.expd, 1)
                for i in range(NT):
                    act.wait_ge(s.turned, i + 1)
                    for n, dst in enumerate((i1T, i2T, gT)):
                        ins = nc.scalar.activation(dst[:, i * P:(i + 1) * P], bank(i)[:, n, :], ACT.Copy)
                    ins.then_inc(s.turned_in, 1)

            @block.vector
            def _(dve):
                st = Steps(dve, s.dve_step)
                L = st.link
                L(nc.vector.tensor_copy(gs[:, 0, :].unsqueeze(2), score[:, :, 0:1]))
                nc.vector.tensor_tensor(score, score, gs[:, 0, :].unsqueeze(2).to_broadcast([P, NT * PH, TOPK]),
                                        ALU.subtract).then_inc(s.centred, 1)
                dve.wait_ge(s.expd, 1)
                L(nc.vector.tensor_reduce(gs[:, 0, :], score, X, ALU.add))
                L(nc.vector.reciprocal(gs[:, 1, :], gs[:, 0, :]))
                nc.vector.tensor_tensor(score, score, gs[:, 1, :].unsqueeze(2).to_broadcast([P, NT * PH, TOPK]),
                                        ALU.mult).then_inc(s.outs, 1)

            @block.tensor
            def _(pe):
                pe.wait_ge(s.outs, 1)
                for i in range(NT):
                    if i >= 2:
                        pe.wait_ge(s.turned_in, i - 1)
                    for n in range(3):
                        ins = nc.tensor.transpose(bank(i)[:, n, :], r.out[:, n, i].rearrange("p h k -> p (h k)"),
                                                  m.ident[:])
                    ins.then_inc(s.turned, 1)


def gates(nc, m, i1T, i2T, gT):
    TB, BUFS = 4, 3
    ACT_TB = 1
    NB = UNIT // TB
    with ExitStack() as ctx:
        a1 = ctx.enter_context(sbuf(nc, "g_a1", [P, 4, TB, P], F32))
        a2 = ctx.enter_context(sbuf(nc, "g_a2", [P, 4, TB, P], F32))
        dist = ctx.enter_context(sbuf(nc, "g_dist", [P, 2, P], F32))
        ngT = ctx.enter_context(sbuf(nc, "g_minus", [P, TPAD], F32))
        gst = ctx.enter_context(sbuf(nc, "g_stage", [P, BUFS, NKEY, UNIT], F32))
        ps = ctx.enter_context(psum(nc, "g_ps", [P, 4, TB, P], F32))
        names = ["hot", "act_hot", "act_step", "slots_free", "made", "banks_free", "moved", "unit_free0", "unit_free1", "unit_free2", "u_in",
                 "u_hi"]
        with stage(nc, *names) as (block, s):
            unit_free = (s.unit_free0, s.unit_free1, s.unit_free2)

            @block.vector
            def _(dve):
                with dve.Fori(0, T // (4 * TB)) as n:
                    for b in range(4):
                        dve.wait_ge(s.slots_free, n * 4 + (b + 1))
                        nc.vector.tensor_tensor(a2[:, b], m.iota[:].unsqueeze(1).to_broadcast([P, TB, P]),
                                                i2T[:, bass.ds(n * (4 * TB) + b * TB, TB)].unsqueeze(2)
                                                .to_broadcast([P, TB, P]), ALU.is_equal)
                        for j in range(ACT_TB, TB):
                            t = bass.ds(n * (4 * TB) + (b * TB + j), 1)
                            ins = nc.vector.tensor_scalar(a1[:, b, j, :], m.iota[:], i1T[:, t], gT[:, t],
                                                          ALU.is_equal, ALU.mult)
                        ins.then_inc(s.hot, 1)
                dve.wait_ge(s.u_hi, 1)
                nc.vector.tensor_tensor(m.u_lo0[:], m.u_raw0[:], m.u_hi0[:].bitcast(F32), ALU.subtract)

            @block.tensor
            def _(pe):
                pe.sem_inc(s.slots_free, 3)
                with pe.Fori(0, T // (4 * TB)) as n:
                    for b in range(4):
                        pe.wait_ge(s.hot, n * 4 + (b + 1))
                        pe.wait_ge(s.act_hot, n * 4 + (b + 1))
                        pe.wait_ge(s.banks_free, n * 4 + (b + 1))
                        for j in range(TB):
                            ins = nc.tensor.matmul(ps[:, b, j, :], a2[:, b, j, :], a1[:, b, j, :],
                                                   start=True, stop=True)
                        ins.then_inc(s.made, 1)
                        pe.wait_ge(s.made, n * 4 + b)
                        pe.sem_inc(s.slots_free, 1)

            @block.scalar
            def _(act):
                def hot(batch, slot, first=False):
                    act.wait_ge(s.slots_free, batch + 1)
                    if not first:
                        act.wait_ge(s.act_hot, batch)
                    for j in range(ACT_TB):
                        nc.scalar.activation(dist[:, j, :], m.iota[:], ACT.Abs,
                                             bias=i1T[:, bass.ds(batch * TB + j, 1)], scale=-1.0
                                             ).then_inc(s.act_step, 1)
                    for j in range(ACT_TB):
                        t = bass.ds(batch * TB + j, 1)
                        act.wait_ge(s.act_step, batch * ACT_TB + (j + 2))
                        ins = nc.scalar.activation(a1[:, slot, j, :], dist[:, j, :], ACT.Relu, bias=gT[:, t],
                                                   scale=ngT[:, t])
                    ins.then_inc(s.act_hot, 1)

                act.sem_inc(s.banks_free, 4)
                for k in range(BUFS):
                    act.sem_inc(unit_free[k], 16)
                nc.scalar.activation(ngT[:], gT[:], ACT.Copy, scale=-1.0).then_inc(s.act_step, 1)
                act.wait_ge(s.act_step, 1)
                hot(0, 0, True)
                with act.Fori(0, NU // BUFS) as n:
                    for k in range(BUFS):
                        act.wait_ge(unit_free[k], n * 16 + 16)
                        with act.Fori(0, NB // 4) as q:
                            for b in range(4):
                                hot(n * (BUFS * NB) + q * 4 + (k * NB + b + 1), (b + 1) % 4)
                                act.wait_ge(s.made, n * (BUFS * NB) + q * 4 + (k * NB + b + 1))
                                nc.scalar.activation(
                                    gst[:, k, :, bass.ds(q * (4 * TB) + b * TB, TB)].rearrange("p i t -> p t i"),
                                    ps[:, b], ACT.Copy).then_inc(s.banks_free, 1)
                        act.wait_ge(s.banks_free, n * (BUFS * NB) + ((k + 1) * NB + 4))
                        act.sem_inc(s.moved, 1)
                act.wait_ge(s.u_in, 16)
                nc.scalar.activation(m.u_hi0[:], m.u_raw0[:], ACT.Copy).then_inc(s.u_hi, 1)

            @block.sync
            def _(sp):
                sp.dma_start(m.u_raw0[:], m.dram.peer_uT[m.l, 0]).then_inc(s.u_in, 16)
                with sp.Fori(0, NU // BUFS) as n:
                    for k in range(BUFS):
                        sp.wait_ge(s.moved, n * BUFS + (k + 1))
                        sp.dma_start(m.dram.gate_dram[n * BUFS + k].rearrange("g p c -> p g c"),
                                     gst[:, k].rearrange("p (g e) t -> p g (e t)", e=EG)
                                     ).then_inc(unit_free[k], 16)
                for k in range(BUFS):
                    sp.wait_ge(unit_free[k], 16 * (NU // BUFS) + 16)


def experts(nc, m):
    with ExitStack() as ctx:
        def sb(name, shape, dt=F32):
            return ctx.enter_context(sbuf(nc, name, shape, dt))

        acc = sb("ex_acc", [P, KD, T])
        u_raw = [m.u_raw0, sb("ex_u", [P, KD, EG * P])]
        u_hi, u_lo = ([first, sb("ex_u" + n, [P, KD, EG * P], F32R)] for n, first in (("h", m.u_hi0), ("l", m.u_lo0)))
        v_raw, v_hi, v_lo = (sb("ex_v" + n, [P, 2, EG, D], dt) for n, dt in (("", F32), ("h", F32R), ("l", F32R)))
        gb = sb("ex_g", [P, 2, NU, EG, UNIT])
        a_raw = sb("ex_a", [P, EG, T])
        a_hi, a_lo = (sb("ex_a" + n, [P, 2, EG, T], F32R) for n in "hl")
        hp = ctx.enter_context(psum(nc, "ex_hp", [P, EG, 2, 512], F32))
        op = ctx.enter_context(psum(nc, "ex_op", [P, 2, 2, 512], F32))
        names = ["u_in0", "u_in1", "v_in0", "v_in1", "g_in0", "g_in1", "kept", "uh", "ul", "vh", "vl", "h_made",
                 "gelud", "gated", "ah", "al", "out_made", "added", "zeroed"]
        with stage(nc, *names) as (block, s):
            u_in, v_in, g_in = (s.u_in0, s.u_in1), (s.v_in0, s.v_in1), (s.g_in0, s.g_in1)

            @block.sync
            def _(sp):
                def load(g, j, first=False):
                    if not first:
                        sp.wait_ge(s.ul, g - 1)
                    if not (first and j == 0):
                        sp.dma_start(u_raw[j][:], m.dram.peer_uT[m.l, g]).then_inc(u_in[j], 16)
                    if not first:
                        sp.wait_ge(s.gated, g * EG - EG)
                    sp.dma_start(gb[:, j].rearrange("p u e t -> p u (e t)"),
                                 m.dram.gate_dram[:, g].rearrange("u p c -> p u c")).then_inc(g_in[j], 16)
                    if not first:
                        sp.wait_ge(s.vl, g - 1)
                    sp.dma_start(v_raw[:, j], m.dram.peer_v[m.l, g]).then_inc(v_in[j], 16)
                    sp.dma_start(m.dram.s_k[m.l, g], m.dram.cache_k_kept[m.l, g]).then_inc(s.kept, 16)
                    sp.dma_start(m.dram.s_v[m.l, g], m.dram.cache_v_kept[m.l, g]).then_inc(s.kept, 16)

                load(0, 0, True)
                load(1, 1, True)
                with sp.Fori(1, NG // 2) as i:
                    for j in range(2):
                        load(i * 2 + j, j)
                sp.wait_ge(s.kept, 32 * NG)

            @block.tensor
            def _(pe):
                def first_product(g, j, first=False):
                    if not first:
                        pe.wait_ge(s.ul, g + 1)
                    for e in range(EG):
                        if not first:
                            pe.wait_ge(s.gelud, g * EG + (e - 1))
                        for half in range(2):
                            t = slice(half * HALF, (half + 1) * HALF)
                            c = slice(e * P, (e + 1) * P)
                            for k in range(KD):
                                ins = three_passes(nc, hp[:, e, half, 0:HALF], u_hi[j][:, k, c], u_lo[j][:, k, c],
                                                   m.x_hi[:, k, t], m.x_lo[:, k, t], k == 0, k == KD - 1)
                        ins.then_inc(s.h_made, 1)

                def second_product(g, j, first=False):
                    pe.wait_ge(s.al, g * EG + EG)
                    pe.wait_ge(s.vl, g + 1)
                    for n in range(KD):
                        if not (first and n < 2):
                            pe.wait_ge(s.added, g * KD + (n - 1))
                        for half in range(2):
                            t = slice(half * HALF, (half + 1) * HALF)
                            c = slice(n * P, (n + 1) * P)
                            for e in range(EG):
                                ins = three_passes(nc, op[:, n % 2, half, 0:HALF], v_hi[:, j, e, c], v_lo[:, j, e, c],
                                                   a_hi[:, j, e, t], a_lo[:, j, e, t], e == 0, e == EG - 1)
                        ins.then_inc(s.out_made, 1)

                first_product(0, 0, True)
                first_product(1, 1)
                second_product(0, 0, True)
                with pe.Fori(1, NG // 2) as i:
                    first_product(i * 2, 0)
                    second_product(i * 2 - 1, 1)
                    first_product(i * 2 + 1, 1)
                    second_product(i * 2, 0)
                second_product(NG - 1, 1)

            @block.scalar
            def _(act):
                def split_u(g, j, turn, first=False):
                    act.wait_ge(u_in[j], turn * 16 + 16)
                    if not first:
                        act.wait_ge(s.h_made, g * EG - EG)
                    nc.scalar.activation(u_hi[j][:], u_raw[j][:], ACT.Copy).then_inc(s.uh, 1)

                def step(g, j, turn, first=False, last=False):
                    if not last:
                        split_u(g + 1, 1 - j, turn + j, first and j == 0)
                    act.wait_ge(v_in[j], turn * 16 + 16)
                    if not first:
                        act.wait_ge(s.out_made, g * KD - KD)
                    nc.scalar.activation(v_hi[:, j], v_raw[:, j], ACT.Copy).then_inc(s.vh, 1)
                    for e in range(EG):
                        act.wait_ge(s.h_made, g * EG + (e + 1))
                        if not (first and j == 0):
                            act.wait_ge(s.al, g * EG + (e - 1))
                        nc.scalar.activation(a_raw[:, e, :].rearrange("p (a t) -> p a t", a=2),
                                             hp[:, e, :, 0:HALF], ACT.Gelu).then_inc(s.gelud, 1)
                        act.wait_ge(s.gated, g * EG + (e + 1))
                        nc.scalar.activation(a_hi[:, j, e, :], a_raw[:, e, :], ACT.Copy).then_inc(s.ah, 1)

                act.sem_inc(s.u_in0, 16)
                act.sem_inc(s.uh, 1)
                step(0, 0, 0, first=True)
                step(1, 1, 0, first=True)
                with act.Fori(1, NG // 2 - 1) as i:
                    step(i * 2, 0, i)
                    step(i * 2 + 1, 1, i)
                step(NG - 2, 0, NG // 2 - 1)
                step(NG - 1, 1, NG // 2 - 1, last=True)

            @block.vector
            def _(dve):
                def split_u(g, j):
                    dve.wait_ge(s.uh, g + 1)
                    nc.vector.tensor_tensor(u_lo[j][:], u_raw[j][:], u_hi[j][:].bitcast(F32),
                                            ALU.subtract).then_inc(s.ul, 1)

                def split_v(g, j):
                    dve.wait_ge(s.vh, g + 1)
                    nc.vector.tensor_tensor(v_lo[:, j], v_raw[:, j], v_hi[:, j].bitcast(F32),
                                            ALU.subtract).then_inc(s.vl, 1)

                def add(g, ns):
                    for n in ns:
                        dve.wait_ge(s.out_made, g * KD + (n + 1))
                        a = acc[:, n, :].rearrange("p (a t) -> p a t", a=2)
                        nc.vector.tensor_tensor(a, a, op[:, n % 2, :, 0:HALF], ALU.add).then_inc(s.added, 1)

                def step(g, j, turn, first=False, last=False):
                    if not last:
                        split_u(g + 1, 1 - j)
                    dve.wait_ge(g_in[j], turn * 16 + 16)
                    for e in range(EG):
                        dve.wait_ge(s.gelud, g * EG + (e + 1))
                        a = a_raw[:, e, :].rearrange("p (u t) -> p u t", u=NU)
                        nc.vector.tensor_tensor(a, a, gb[:, j, :, e, :], ALU.mult).then_inc(s.gated, 1)
                        if e == 0:
                            split_v(g, j)
                        elif not first:
                            add(g - 1, (0,))
                        dve.wait_ge(s.ah, g * EG + (e + 1))
                        nc.vector.tensor_tensor(a_lo[:, j, e, :], a_raw[:, e, :], a_hi[:, j, e, :].bitcast(F32),
                                                ALU.subtract).then_inc(s.al, 1)
                    if not first:
                        add(g - 1, range(1, KD))

                nc.vector.memset(acc[:], 0.0).then_inc(s.zeroed, 1)
                dve.wait_ge(s.zeroed, 1)
                dve.sem_inc(s.ul, 1)
                step(0, 0, 0, first=True)
                step(1, 1, 0)
                with dve.Fori(1, NG // 2 - 1) as i:
                    step(i * 2, 0, i)
                    step(i * 2 + 1, 1, i)
                step(NG - 2, 0, NG // 2 - 1)
                step(NG - 1, 1, NG // 2 - 1, last=True)
                add(NG - 1, range(KD))
        ps = op[:, :, :, :].rearrange("p a b c -> p (a b) c")
        with stage(nc, "turned", "added") as (block, s):
            @block.tensor
            def _(pe):
                for n in range(2 * NT):
                    i, rows = n // 2, ROWS[n // 2]
                    if n >= 4:
                        pe.wait_ge(s.added, n - 3)
                    for q in range(4):
                        ins = nc.tensor.transpose(ps[0:rows, n % 4, q * P:(q + 1) * P],
                                                  acc[:, 4 * (n % 2) + q, i * P:i * P + rows], m.ident[:])
                    ins.then_inc(s.turned, 1)

            @block.vector
            def _(dve):
                for n in range(2 * NT):
                    i, rows = n // 2, ROWS[n // 2]
                    dve.wait_ge(s.turned, n + 1)
                    hh = m.h[0:rows, i, (n % 2) * 512:(n % 2 + 1) * 512]
                    nc.vector.tensor_tensor(hh, hh, ps[0:rows, n % 4, :], ALU.add).then_inc(s.added, 1)


def final_norm(nc, m):
    with ExitStack() as ctx:
        junk = ctx.enter_context(sbuf(nc, "fin_junk", [P, D], F32))
        st_ = ctx.enter_context(sbuf(nc, "fin_stat", [P, 3, NT], F32))
        y = ctx.enter_context(sbuf(nc, "fin_y", [P, NT, D], F32))
        g = ctx.enter_context(sbuf(nc, "fin_g", [P, D], F32))
        with stage(nc, "loaded", "squares", "eps_added", "rooted", "dve_step", "done", "stored") as (block, s):
            @block.sync
            def _(sp):
                sp.dma_start(g[:], m.dram.final_g).then_inc(s.loaded, 16)
                for i, r in enumerate(ROWS):
                    sp.wait_ge(s.done, i + 1)
                    sp.dma_start(m.dram.y[i * P:i * P + r, :], y[0:r, i, :]).then_inc(s.stored, 16)
                sp.wait_ge(s.stored, 16 * NT)

            @block.scalar
            def _(act):
                for i, r in enumerate(ROWS):
                    nc.scalar.activation(junk[0:r, :], m.h[0:r, i, :], ACT.Square,
                                         accum_out=st_[0:r, 0, i:i + 1]).then_inc(s.squares, 1)
                    act.wait_ge(s.squares, i + 1)
                for i, r in enumerate(ROWS):
                    act.wait_ge(s.eps_added, i + 1)
                    nc.scalar.activation(st_[0:r, 1, i:i + 1], st_[0:r, 0, i:i + 1], ACT.Sqrt).then_inc(s.rooted, 1)

            @block.vector
            def _(dve):
                st = Steps(dve, s.dve_step)
                dve.wait_ge(s.loaded, 16)
                for i, r in enumerate(ROWS):
                    dve.wait_ge(s.squares, i + 1)
                    nc.vector.tensor_scalar(st_[0:r, 0, i:i + 1], st_[0:r, 0, i:i + 1], 1.0 / D, RMS_EPS,
                                            ALU.mult, ALU.add).then_inc(s.eps_added, 1)
                for i, r in enumerate(ROWS):
                    dve.wait_ge(s.rooted, i + 1)
                    st.link(nc.vector.reciprocal(st_[0:r, 2, i:i + 1], st_[0:r, 1, i:i + 1]))
                    nc.vector.scalar_tensor_tensor(out=y[0:r, i, :], in0=m.h[0:r, i, :], scalar=st_[0:r, 2, i:i + 1],
                                                   in1=g[0:r, :], op0=ALU.mult, op1=ALU.mult).then_inc(s.done, 1)


def program(nc, d):
    m = Parts()
    m.dram = namedtuple("Dram", sorted(d))(*(d[n] for n in sorted(d)))
    with ExitStack() as ctx:
        def sb(name, shape):
            return ctx.enter_context(sbuf(nc, name, shape, F32))

        m.h = sb("h", [P, NT, D])
        m.ident, m.iota = sb("ident", [P, P]), sb("iota", [P, P])
        m.g1, m.g2 = sb("g1", [P, KD]), sb("g2", [P, KD])
        with stage(nc, "loaded") as (block, s):
            @block.sync
            def _(sp):
                loads = [(m.h[:, 0:4, :], m.dram.x_prompt), (m.h[0:TS_, 4, :], m.dram.x_sample),
                         (m.ident[:], m.dram.c_ident), (m.iota[:], m.dram.c_iota)]
                for dst, src in loads:
                    sp.dma_start(dst, src).then_inc(s.loaded, 16)
                sp.wait_ge(s.loaded, 16 * len(loads))
        with nc.Fori(0, LAYERS) as l:
            m.l = l
            with ExitStack() as mixer:
                def mb(name, shape):
                    return mixer.enter_context(sbuf(nc, name, shape, F32))

                m.mixed = mb("mixed", [P, KD, T])
                m.pair_ones = mb("pair_ones", [P, P])
                m.chunk_reset = mb("chunk_reset", [P, T])
                mk = mb("masks", [P, 2, 5, P])
                m.own_req = mb("own_req", [TS_, REQ])
                m.masks_prompt = (mk[:, 0, 0:2], mk[:, 0, 2:4], mk[:, 0, 4])
                m.masks_sample = (mk[:, 1, 0:2], mk[:, 1, 2:4], mk[:, 1, 4])
                with ExitStack() as pb:
                    m.proj_rw = pb.enter_context(sbuf(nc, "proj_rw", [P, NB_RW, T], F32))
                    with ExitStack() as pa:
                        m.proj = pa.enter_context(sbuf(nc, "proj", [P, BR, T], F32))
                        m.v_tok = pa.enter_context(sbuf(nc, "v_tok", [P, NT, HEADS * HD], F32))
                        with ExitStack() as rp:
                            m.rope_cos = rp.enter_context(sbuf(nc, "rope_cos", [P, T], F32))
                            m.rope_sin = rp.enter_context(sbuf(nc, "rope_sin", [P, T], F32))
                            m.rope_swap = rp.enter_context(sbuf(nc, "rope_swap", [P, P], F32))
                            load_constants(nc, [(m.pair_ones[:], m.dram.c_pair_ones), (m.chunk_reset[:], m.dram.c_chunk_reset),
                                                (mk[:], m.dram.c_masks), (m.own_req[:], m.dram.c_own_req),
                                                (m.rope_cos[:], m.dram.c_cos), (m.rope_sin[:], m.dram.c_sin),
                                                (m.rope_swap[:], m.dram.c_swap), (m.g1[:], m.dram.norm1_g[l]), (m.g2[:], m.dram.norm2_g[l])])
                            with ExitStack() as px:
                                m.x_hi, m.x_lo = (px.enter_context(sbuf(nc, n, [P, KD, T], F32R))
                                                  for n in ("x_hi", "x_lo"))
                                norm_transpose(nc, m, m.g1)
                                project(nc, m, m.dram.w_in[m.l, BR:NB_IN], NB_RW, m.proj_rw)
                                project(nc, m, m.dram.w_in[m.l, 0:BR], BR, m.proj)
                            rotate(nc, m)
                        attend_prompt(nc, m)
                        attend_sample(nc, m)
                    rwkv(nc, m)
                mix_out(nc, m)
            with ExitStack() as peer:
                m.x_hi, m.x_lo = (peer.enter_context(sbuf(nc, n, [P, KD, T], F32R)) for n in ("x_hi", "x_lo"))
                def peer_sb(name, shape, dt, ctx=peer):
                    return ctx.enter_context(sbuf(nc, name, shape, dt))

                m.u_raw0 = peer_sb("ex_u", [P, KD, EG * P], F32)
                m.u_hi0, m.u_lo0 = (peer_sb("ex_u" + n, [P, KD, EG * P], F32R) for n in "hl")
                with ExitStack() as pi:
                    i1T, i2T, gT = (peer_sb(n, [P, TPAD], F32, pi) for n in ("i1T", "i2T", "gT"))
                    with ExitStack() as pr:
                        r = Parts()
                        r.w = peer_sb("rt_w", [P, 2, KD, P], F32, pr)
                        r.w_hi, r.w_lo = ([peer_sb("rt_w" + n, [P, 2, KD, P], F32R, pr) for _ in range(2)] for n in "hl")
                        norm_transpose(nc, m, m.g2, r)
                        route(nc, m, r, i1T, i2T, gT)
                    gates(nc, m, i1T, i2T, gT)
                experts(nc, m)
        final_norm(nc, m)


def _constants():
    c = {}
    c["c_ident"] = np.eye(P, dtype=np.float32)
    c["c_iota"] = np.tile(np.arange(P, dtype=np.float32), (P, 1))
    c["c_pair_ones"] = np.kron(np.eye(2, dtype=np.float32), np.ones((HD, HD), np.float32))
    reset = np.ones((P, T), np.float32)
    reset[:, 0:TP_:CH] = 0
    reset[:, TP_::STEPS] = 0
    c["c_chunk_reset"] = reset
    masks = np.zeros((P, 2, 5, P), np.float32)
    s_, t_ = np.arange(P)[:, None], np.arange(P)[None, :]
    for n, w in enumerate((CH, STEPS)):
        same = s_ // w == t_ // w
        masks[:, n, 0] = same & (s_ < t_)
        masks[:, n, 1] = same & (s_ <= t_)
        masks[:, n, 2] = -masks[:, n, 0]
        masks[:, n, 3] = -masks[:, n, 1]
        masks[:, n, 4] = -(same & (t_ < s_)).astype(np.float32)
    c["c_masks"] = masks
    c["c_own_req"] = (np.arange(TS_)[:, None] // STEPS == np.arange(REQ)[None]).astype(np.float32)
    pos = np.concatenate([np.arange(TP_), PAST + np.tile(np.arange(STEPS), REQ)]).astype(np.float32)
    half = HD // 8
    inv = (np.float32(500000.0) ** (-np.arange(half, dtype=np.float32) * np.float32(2.0) / np.float32(2 * half)))
    ang = (pos[:, None] * inv.astype(np.float32)[None]).astype(np.float32)
    cos, sin, swap = np.ones((P, T), np.float32), np.zeros((P, T), np.float32), np.zeros((P, P), np.float32)
    for o in (0, HD):
        for j in range(half):
            cos[o + j] = cos[o + half + j] = np.cos(ang[:, j])
            sin[o + j] = sin[o + half + j] = np.sin(ang[:, j])
            swap[o + half + j, o + j] = -1
            swap[o + j, o + half + j] = 1
    c["c_cos"], c["c_sin"], c["c_swap"] = cos, sin, swap
    pinv = np.zeros((P, 2, T), np.float32)
    for a in range(2):
        for o in range(2):
            win = 2 << (2 * a + o)
            pinv[64 * o:64 * o + 64, a, 0:TP_] = np.float32(1) / np.minimum(win, np.arange(TP_) + 1).astype(np.float32)
            pinv[64 * o:64 * o + 64, a, TP_:] = np.float32(1) / np.float32(win)
    c["c_pool_inv"] = pinv

    def count(rel):
        n = sum(((rel >= 0) & (rel <= w) & (rel % d == 0)).astype(int) for w, d in ((128, 1), (512, 4), (2048, 16)))
        return np.where(n > 0, np.log(np.maximum(n, 1)), NEG).astype(np.float32)

    c["count_prompt"] = np.ascontiguousarray(
        count(np.arange(TP_)[:, None] - np.arange(TP_)[None]).reshape(4, P, TP_).transpose(1, 0, 2))
    q = np.tile(np.arange(STEPS), HEADS)
    c["count_past"] = count(PAST + q[:, None] - np.arange(PAST)[None])
    new = count(q[:, None] - np.tile(np.arange(STEPS), REQ)[None])
    own = np.arange(TS_)[None, None] // STEPS == np.arange(REQ)[None, :, None]
    c["count_new"] = np.ascontiguousarray(np.where(own, new[:, None], np.float32(NEG)).astype(np.float32))
    return c


def _layouts(i):
    i = {k: np.asarray(v) for k, v in i.items()}
    L = LAYERS
    cc = np.ascontiguousarray
    fm = lambda a: cc(a.reshape(L, -1, P).transpose(0, 2, 1))
    a = {}
    a["x_prompt"] = cc(i["x_prompt"].reshape(4, P, D).transpose(1, 0, 2))
    a["x_sample"] = i["x_sample"].reshape(TS_, D)
    blocks = lambda w: cc(w.reshape(L, KD, P, -1, P).transpose(0, 3, 2, 1, 4))
    a["w_in"], a["peer_wq"] = blocks(i["w_in"]), blocks(i["peer_wq"])
    a["w_out"] = cc(i["w_out"].reshape(L, KD, P, D).transpose(0, 2, 1, 3))
    for n in ("norm1_g", "norm2_g"):
        a[n] = fm(i[n])
    a["pool_scale"] = fm(i["pool_scale"])
    a["final_g"] = cc(np.broadcast_to(i["final_g"], (P, D)))
    a["state_pool"] = cc(i["state_pool"].transpose(0, 3, 1, 2).reshape(L, 2, P, REQ, POOL_BUF)
                         .transpose(0, 2, 1, 3, 4).reshape(L, P, 2 * REQ, POOL_BUF))
    a["pool_w"] = i["pool_w"]
    a["cache_kT"] = cc(i["cache_k"].reshape(L, REQ, PAST, PAIRS, P).transpose(0, 1, 4, 3, 2))
    a["cache_v"] = cc(i["cache_v"].reshape(L, REQ, PAST // P, P, HEADS * HD).transpose(0, 1, 3, 2, 4))
    for n in ("k", "v"):
        a[f"cache_{n}_kept"] = cc(i[f"cache_{n}"][:, :, STEPS:].reshape(L, NG, P, -1))
    a["state_shift"] = cc(i["state_shift"].reshape(L, REQ, NB_RW, P).transpose(0, 3, 2, 1))
    a["state_wkv"] = cc(i["state_wkv"].reshape(L, REQ, PAIRS, 2, HD, HD).transpose(0, 3, 5, 2, 1, 4)
                        .reshape(L, P, PAIRS, REQ, HD))
    a["rwkv_mu"] = fm(i["rwkv_mu"])
    vecs = [i["rwkv_" + n].reshape(L, HEADS * HD) for n in ("w0", "a0", "k_k", "k_a", "r_k", "ln_w", "ln_b")]
    a["rwkv_vec"] = cc(np.stack([fm(v) for v in vecs], 2))
    a["rwkv_wa"] = np.concatenate([i["rwkv_w_up"], i["rwkv_a_up"]], 1)
    a["rwkv_g"] = i["rwkv_g_up"]
    a["peer_keys"] = cc(i["peer_subkeys"].reshape(L, PH, 2, NKEY, P).transpose(0, 1, 4, 2, 3))
    a["peer_uT"] = cc(i["peer_u"].reshape(L, NG, EG * P, KD, P).transpose(0, 1, 4, 3, 2))
    a["peer_v"] = cc(i["peer_v"].reshape(L, NG, EG, P, D).transpose(0, 1, 3, 2, 4))
    return a


_OUTS = {
    "y": (T, D), "p_pool": (LAYERS, P, 2, POOL_BUF), "s_pool": (LAYERS, P, 2 * REQ, POOL_BUF),
    "out_k": (LAYERS, P, PAIRS, T), "out_v": (LAYERS, P, PAIRS, T),
    "p_shift": (LAYERS, P, NB_RW, 1), "s_shift": (LAYERS, P, NB_RW, REQ),
    "p_wkv": (LAYERS, P, PAIRS, HD), "s_wkv": (LAYERS, P, PAIRS, REQ, HD),
    "s_k": (LAYERS, NG, P, REQ * (PAST - STEPS) * HEADS * HD // (P * NG)),
    "s_v": (LAYERS, NG, P, REQ * (PAST - STEPS) * HEADS * HD // (P * NG)),
}


def _build(nc, arrays):
    d = {n: nc.dram_tensor("in_" + n, a.shape, F32, kind="ExternalInput").ap() for n, a in arrays.items()}
    for n, shape in _OUTS.items():
        d[n] = nc.dram_tensor("out_" + n, shape, F32, kind="ExternalOutput").ap()
    d["gate_dram"] = nc.dram_tensor("gate_matrix", (NU, NG, P, EG * UNIT), F32, kind="Internal").ap()
    program(nc, d)


def _returned(o):
    L = LAYERS
    tok = lambda a: a.transpose(0, 3, 2, 1).reshape(L, T, HEADS, HD)
    k, v = tok(o["out_k"]), tok(o["out_v"])
    kept = lambda a: a.reshape(L, REQ, PAST - STEPS, HEADS, HD)
    new = lambda a: a[:, TP_:].reshape(L, REQ, STEPS, HEADS, HD)
    pool_ = lambda a, b: a.reshape(L, P, 2, b, POOL_BUF).transpose(0, 3, 4, 2, 1).reshape(L, b, POOL_BUF, 2 * P)
    shift = lambda a: a.transpose(0, 3, 2, 1).reshape(L, a.shape[3], NB_RW * P)
    wkv = lambda a, b: (a.reshape(L, 2, HD, PAIRS, b, HD).transpose(0, 4, 3, 1, 5, 2)
                        .reshape(L, b, HEADS, HD, HD))
    out = (o["y"][:TP_].reshape(1, TP_, D), o["y"][TP_:].reshape(REQ, STEPS, D),
           pool_(o["p_pool"], 1), k[:, None, :TP_], v[:, None, :TP_], shift(o["p_shift"]), wkv(o["p_wkv"], 1),
           pool_(o["s_pool"], REQ), np.concatenate([kept(o["s_k"]), new(k)], 2),
           np.concatenate([kept(o["s_v"]), new(v)], 2), shift(o["s_shift"]), wkv(o["s_wkv"], REQ))
    return tuple(np.ascontiguousarray(x) for x in out)


def kernel(**inputs):
    import concourse.bacc as _bacc
    from concourse.bass_utils import run_bass_kernel_spmd as _run

    nc = _bacc.Bacc("TRN2", target_bir_lowering=False, num_devices=1)
    arrays = {**_layouts(inputs), **_constants()}
    _build(nc, arrays)
    r = _run(nc, [{"in_" + n: a for n, a in arrays.items()}], core_ids=[0])
    return _returned({n: r.results[0]["out_" + n] for n in _OUTS})
```
